# Optimizing a Trainium2 kernel written in Bass

```python
import math
import jax, jax.numpy as jnp
from jax import lax
import numpy as np

D_MODEL = 1024
BATCH = 1
SEQ = 512
DEPTH = 2

FOX_HEADS = 8
FOX_HEAD_DIM = 64
DIFF_HEADS = 4
DIFF_HEAD_DIM = 64
DIFF_V_DIM = 2 * DIFF_HEAD_DIM
FOX_WIDTH = FOX_HEADS * FOX_HEAD_DIM
DIFF_WIDTH = DIFF_HEADS * DIFF_V_DIM
MIX_WIDTH = FOX_WIDTH + DIFF_WIDTH
D_FF = 2816
Q_BLOCK = 128
ROPE_THETA = 10000.0
NORM_EPS = 1e-5
FFN_RES_WEIGHT = 0.5
IN_SPLITS = [FOX_WIDTH, FOX_WIDTH, FOX_WIDTH, FOX_HEADS,
             2 * DIFF_HEADS * DIFF_HEAD_DIM, 2 * DIFF_HEADS * DIFF_HEAD_DIM, DIFF_WIDTH]
IN_COLS = int(sum(IN_SPLITS))
IN_OFFSETS = [int(v) for v in np.cumsum(IN_SPLITS)[:-1]]


def _rmsnorm(x, gain):
    x32 = x.astype(jnp.float32)
    y = x32 * lax.rsqrt(jnp.mean(x32 * x32, axis=-1, keepdims=True) + NORM_EPS)
    return (y * gain.astype(jnp.float32)).astype(x.dtype)

def _swiglu(h, w_gate_up, w_down):
    g, u = jnp.split(h @ w_gate_up, 2, axis=-1)
    return (jax.nn.silu(g) * u) @ w_down

def _rope_tables(seq, dim):
    inv_freq = 1.0 / (ROPE_THETA ** (jnp.arange(0, dim, 2, dtype=jnp.float32) / dim))
    pos = jnp.arange(seq, dtype=jnp.float32)
    freqs = pos[:, None] * inv_freq[None, :]
    emb = jnp.concatenate([freqs, freqs], axis=-1)
    return jnp.cos(emb), jnp.sin(emb)

def _apply_rope(t, cos, sin):
    t32 = t.astype(jnp.float32)
    t1, t2 = jnp.split(t32, 2, axis=-1)
    rot = jnp.concatenate([-t2, t1], axis=-1)
    return (t32 * cos + rot * sin).astype(t.dtype)

def _causal_block_attention(q_f, k_f, v_f, cum_f, q_d, k_d, v_d, lam):
    B, Hf, S, Df = q_f.shape
    Hd, Dh = q_d.shape[1], q_d.shape[-1]
    Dv = v_d.shape[-1]
    nb = S // Q_BLOCK
    qf_blk = jnp.moveaxis(q_f.reshape(B, Hf, nb, Q_BLOCK, Df), 2, 0)
    cf_blk = jnp.moveaxis(cum_f.reshape(B, Hf, nb, Q_BLOCK), 2, 0)
    qd_blk = jnp.moveaxis(q_d.reshape(B, Hd, 2, nb, Q_BLOCK, Dh), 3, 0)
    k_pos = jnp.arange(S)
    scale_f = Df ** -0.5
    scale_d = Dh ** -0.5

    def one_block(args):
        qf, cf, qd, blk = args
        q_pos = blk * Q_BLOCK + jnp.arange(Q_BLOCK)
        causal = k_pos[None, :] <= q_pos[:, None]
        s_f = jnp.einsum('bhqd,bhkd->bhqk', qf, k_f).astype(jnp.float32) * scale_f
        s_f = s_f + cf[..., :, None] - cum_f[..., None, :]
        s_f = jnp.where(causal, s_f, -jnp.inf)
        p_f = jax.nn.softmax(s_f, axis=-1)
        o_f = jnp.einsum('bhqk,bhkd->bhqd', p_f.astype(v_f.dtype), v_f)
        s_d = jnp.einsum('bhcqd,bhckd->bhcqk', qd, k_d).astype(jnp.float32) * scale_d
        s_d = jnp.where(causal, s_d, -jnp.inf)
        p_d = jax.nn.softmax(s_d, axis=-1)
        a_d = p_d[:, :, 0] - lam * p_d[:, :, 1]
        o_d = jnp.einsum('bhqk,bhkd->bhqd', a_d.astype(v_d.dtype), v_d)
        return o_f, o_d

    o_f, o_d = lax.map(one_block, (qf_blk, cf_blk, qd_blk, jnp.arange(nb)))
    o_f = jnp.moveaxis(o_f, 0, 2).reshape(B, Hf, S, Df)
    o_d = jnp.moveaxis(o_d, 0, 2).reshape(B, Hd, S, Dv)
    return o_f, o_d

def _hybrid_mixer(h, w_in, forget_bias, lq1, lk1, lq2, lk2, subln, w_out, lambda_init):
    B, S, _ = h.shape
    proj = h @ w_in
    fq, fk, fv, ff, dq, dk, dv = jnp.split(proj, IN_OFFSETS, axis=-1)
    to_heads_f = lambda t: t.reshape(B, S, FOX_HEADS, FOX_HEAD_DIM).transpose(0, 2, 1, 3)
    q_f, k_f, v_f = to_heads_f(fq), to_heads_f(fk), to_heads_f(fv)
    log_f = jax.nn.log_sigmoid((ff + forget_bias).astype(jnp.float32))
    cum_f = jnp.cumsum(log_f.transpose(0, 2, 1), axis=-1)
    to_heads_d = lambda t: t.reshape(B, S, DIFF_HEADS, 2, DIFF_HEAD_DIM).transpose(0, 2, 3, 1, 4)
    cos, sin = _rope_tables(S, DIFF_HEAD_DIM)
    q_d = _apply_rope(to_heads_d(dq), cos, sin)
    k_d = _apply_rope(to_heads_d(dk), cos, sin)
    v_d = dv.reshape(B, S, DIFF_HEADS, DIFF_V_DIM).transpose(0, 2, 1, 3)
    lam = (jnp.exp(jnp.sum(lq1.astype(jnp.float32) * lk1.astype(jnp.float32)))
           - jnp.exp(jnp.sum(lq2.astype(jnp.float32) * lk2.astype(jnp.float32)))
           + lambda_init)
    o_f, o_d = _causal_block_attention(q_f, k_f, v_f, cum_f, q_d, k_d, v_d, lam)
    o_d = _rmsnorm(o_d, subln) * (1.0 - lambda_init)
    o_f = o_f.transpose(0, 2, 1, 3).reshape(B, S, FOX_WIDTH)
    o_d = o_d.transpose(0, 2, 1, 3).reshape(B, S, DIFF_WIDTH)
    return jnp.concatenate([o_f, o_d], axis=-1) @ w_out

def first_inputs(seed: int = 0) -> dict:
    key = jax.random.key(seed)
    ks = jax.random.split(key, 20)
    nrm = lambda k, shape, fan_in: jax.random.normal(k, shape, jnp.float32) * fan_in ** -0.5
    gain = lambda k, shape: 1.0 + 0.02 * jax.random.normal(k, shape, jnp.float32)
    return {
        "x": jax.random.normal(ks[0], (BATCH, SEQ, D_MODEL), jnp.float32),
        "ffn1_norm": gain(ks[1], (DEPTH, D_MODEL)),
        "ffn1_w_gate_up": nrm(ks[2], (DEPTH, D_MODEL, 2 * D_FF), D_MODEL),
        "ffn1_w_down": nrm(ks[3], (DEPTH, D_FF, D_MODEL), D_FF),
        "mix_norm": gain(ks[4], (DEPTH, D_MODEL)),
        "w_in": nrm(ks[5], (DEPTH, D_MODEL, IN_COLS), D_MODEL),
        "forget_bias": jax.random.uniform(ks[6], (DEPTH, FOX_HEADS), jnp.float32, 1.0, 4.0),
        "lambda_q1": 0.1 * jax.random.normal(ks[7], (DEPTH, DIFF_HEAD_DIM), jnp.float32),
        "lambda_k1": 0.1 * jax.random.normal(ks[8], (DEPTH, DIFF_HEAD_DIM), jnp.float32),
        "lambda_q2": 0.1 * jax.random.normal(ks[9], (DEPTH, DIFF_HEAD_DIM), jnp.float32),
        "lambda_k2": 0.1 * jax.random.normal(ks[10], (DEPTH, DIFF_HEAD_DIM), jnp.float32),
        "diff_subln": gain(ks[11], (DEPTH, DIFF_V_DIM)),
        "w_out": nrm(ks[12], (DEPTH, MIX_WIDTH, D_MODEL), MIX_WIDTH),
        "ffn2_norm": gain(ks[13], (DEPTH, D_MODEL)),
        "ffn2_w_gate_up": nrm(ks[14], (DEPTH, D_MODEL, 2 * D_FF), D_MODEL),
        "ffn2_w_down": nrm(ks[15], (DEPTH, D_FF, D_MODEL), D_FF),
        "final_norm": gain(ks[16], (D_MODEL,)),
    }

def first_block(x, ffn1_norm, ffn1_w_gate_up, ffn1_w_down, mix_norm, w_in, forget_bias,
              lambda_q1, lambda_k1, lambda_q2, lambda_k2, diff_subln, w_out,
              ffn2_norm, ffn2_w_gate_up, ffn2_w_down, final_norm):
    for layer in range(DEPTH):
        lambda_init = 0.8 - 0.6 * math.exp(-0.3 * layer)
        x = x + FFN_RES_WEIGHT * _swiglu(_rmsnorm(x, ffn1_norm[layer]),
                                         ffn1_w_gate_up[layer], ffn1_w_down[layer])
        x = x + _hybrid_mixer(_rmsnorm(x, mix_norm[layer]), w_in[layer], forget_bias[layer],
                              lambda_q1[layer], lambda_k1[layer], lambda_q2[layer],
                              lambda_k2[layer], diff_subln[layer], w_out[layer], lambda_init)
        x = x + FFN_RES_WEIGHT * _swiglu(_rmsnorm(x, ffn2_norm[layer]),
                                         ffn2_w_gate_up[layer], ffn2_w_down[layer])
    return _rmsnorm(x, final_norm)


CHUNK = 64
RMS_EPS = 1e-6
M_HEADS = 4
M_HEAD_DIM = D_MODEL // 4
M_WIDTH = M_HEADS * M_HEAD_DIM
CONV_K = 4
P_GROUPS = 4
P_WINDOWS = (2, 4, 8, 16)
P_GROUP_DIM = D_MODEL // 4
P_WIDTH = P_GROUPS * P_GROUP_DIM
A_IN = 3 * M_WIDTH + 2 * M_HEADS + 2 * P_WIDTH
A_OUT_IN = M_WIDTH + P_WIDTH
C_HEADS = 8
QK_NOPE = 128
QK_ROPE = 64
QK_HEAD = QK_NOPE + QK_ROPE
V_HEAD = 128
Q_LORA = 384
KV_LORA = 256
C_WIDTH = C_HEADS * V_HEAD
C_IN = Q_LORA + KV_LORA + QK_ROPE + C_WIDTH
N_A = (DEPTH + 1) // 2
N_C = DEPTH // 2


def rms_norm(x, g):
    xf = x.astype(jnp.float32)
    y = xf * lax.rsqrt(jnp.mean(xf * xf, axis=-1, keepdims=True) + RMS_EPS)
    return (y * g.astype(jnp.float32)).astype(x.dtype)

def causal_conv(x, w, b):
    y = lax.conv_general_dilated(x, w[:, None, :].astype(x.dtype), window_strides=(1,),
                                 padding=[(CONV_K - 1, 0)],
                                 dimension_numbers=('NWC', 'WIO', 'NWC'),
                                 feature_group_count=x.shape[-1])
    return y + b

def mlstm_chunkwise(q, k, v, i_pre, log_f):
    B, H, S, Dk = q.shape
    Dv = v.shape[-1]
    nc = S // CHUNK

    def to_chunks(a):
        return jnp.moveaxis(a.reshape(B, H, nc, CHUNK, *a.shape[3:]), 2, 0)

    xs = (to_chunks(q), to_chunks(k), to_chunks(v), to_chunks(i_pre), to_chunks(log_f))
    tri = jnp.tril(jnp.ones((CHUNK, CHUNK), dtype=bool))

    def step(carry, inp):
        C, n, m = carry
        qb, kb, vb, ib, fb = inp
        bcum = jnp.cumsum(fb, axis=-1)
        dmat = jnp.where(tri, bcum[..., :, None] - bcum[..., None, :] + ib[..., None, :], -jnp.inf)
        inter = bcum + m[..., None]
        m_t = jnp.maximum(inter, jnp.max(dmat, axis=-1))
        w_inter = jnp.exp(inter - m_t)
        s = jnp.einsum('bhtd,bhsd->bhts', qb, kb) * jnp.exp(dmat - m_t[..., None])
        num = jnp.einsum('bhts,bhsv->bhtv', s, vb) + w_inter[..., None] * jnp.einsum('bhtd,bhdv->bhtv', qb, C)
        den = jnp.sum(s, axis=-1) + w_inter * jnp.einsum('bhtd,bhd->bht', qb, n)
        h = num / jnp.maximum(jnp.abs(den), jnp.exp(-m_t))[..., None]
        b_last = bcum[..., -1]
        g = b_last[..., None] - bcum + ib
        m_new = jnp.maximum(b_last + m, jnp.max(g, axis=-1))
        ws = jnp.exp(g - m_new[..., None])
        wc = jnp.exp(b_last + m - m_new)
        kw = kb * ws[..., None]
        C_new = wc[..., None, None] * C + jnp.einsum('bhsd,bhsv->bhdv', kw, vb)
        n_new = wc[..., None] * n + jnp.sum(kw, axis=2)
        return (C_new, n_new, m_new), h

    init = (jnp.zeros((B, H, Dk, Dv), jnp.float32), jnp.zeros((B, H, Dk), jnp.float32),
            jnp.zeros((B, H), jnp.float32))
    _, hs = lax.scan(step, init, xs)
    return jnp.moveaxis(hs, 0, 2).reshape(B, H, S, Dv)

def multiscale_pool(xp):
    B, S, _ = xp.shape
    xf = xp.astype(jnp.float32)
    cs = jnp.pad(jnp.cumsum(xf, axis=1), ((0, 0), (1, 0), (0, 0)))
    t = jnp.arange(S)
    means = []
    for g, w in enumerate(P_WINDOWS):
        csg = cs[..., g * P_GROUP_DIM:(g + 1) * P_GROUP_DIM]
        lo = jnp.maximum(t + 1 - w, 0)
        cnt = jnp.minimum(t + 1, w).astype(jnp.float32)
        means.append((csg[:, 1:] - jnp.take(csg, lo, axis=1)) / cnt[None, :, None])
    return (jnp.concatenate(means, axis=-1) - xf).astype(xp.dtype)

def mlstm_pool_layer(x, norm_g, w_in, b_if, conv_w, conv_b, w_q, w_k, w_v, head_norm_g, skip,
                     pool_w, pool_scale, w_out):
    B, S, _ = x.shape
    u = rms_norm(x, norm_g) @ w_in
    s1 = M_WIDTH
    s2 = 2 * M_WIDTH
    s3 = s2 + 2 * M_HEADS
    s4 = s3 + M_WIDTH
    s5 = s4 + P_WIDTH
    xm, om, gates, zm, xp, zp = jnp.split(u, [s1, s2, s3, s4, s5], axis=-1)
    xc = jax.nn.silu(causal_conv(xm, conv_w, conv_b))
    xc_h = xc.reshape(B, S, M_HEADS, M_HEAD_DIM)
    xm_h = xm.reshape(B, S, M_HEADS, M_HEAD_DIM)
    q = jnp.einsum('bshc,hcd->bhsd', xc_h, w_q).astype(jnp.float32)
    k = jnp.einsum('bshc,hcd->bhsd', xc_h, w_k).astype(jnp.float32) * (M_HEAD_DIM ** -0.5)
    v = jnp.einsum('bshc,hcd->bhsd', xm_h, w_v).astype(jnp.float32)
    gates = (gates + b_if).astype(jnp.float32)
    i_pre = jnp.moveaxis(gates[..., :M_HEADS], -1, 1)
    log_f = jnp.moveaxis(jax.nn.log_sigmoid(gates[..., M_HEADS:]), -1, 1)
    hm = mlstm_chunkwise(q, k, v, i_pre, log_f)
    hm = jnp.moveaxis(hm, 1, 2).reshape(B, S, M_WIDTH).astype(x.dtype) * jax.nn.sigmoid(om)
    hm = rms_norm(hm.reshape(B, S, M_HEADS, M_HEAD_DIM),
                  head_norm_g.reshape(M_HEADS, M_HEAD_DIM)).reshape(B, S, M_WIDTH)
    ya = (hm + skip * xc) * jax.nn.silu(zm)
    mix = multiscale_pool(xp).reshape(B, S, P_GROUPS, P_GROUP_DIM)
    yb = jnp.einsum('bsgc,gcd->bsgd', mix, pool_w).reshape(B, S, P_WIDTH) * pool_scale * jax.nn.silu(zp)
    return x + jnp.concatenate([ya, yb], axis=-1) @ w_out

def rope(x, cos, sin):
    x1, x2 = jnp.split(x.astype(jnp.float32), 2, axis=-1)
    return jnp.concatenate([x1 * cos - x2 * sin, x2 * cos + x1 * sin], axis=-1).astype(x.dtype)

def block_causal_attention(q, k, v):
    B, S, H, _ = q.shape
    scale = QK_HEAD ** -0.5
    chunk_id = jnp.arange(S) // CHUNK
    outs = []
    for qb in range(S // Q_BLOCK):
        q0, q1 = qb * Q_BLOCK, (qb + 1) * Q_BLOCK
        s = jnp.einsum('bqhd,bkhd->bhqk', q[:, q0:q1], k[:, :q1],
                       preferred_element_type=jnp.float32) * scale
        mask = chunk_id[q0:q1, None] >= chunk_id[None, :q1]
        p = jax.nn.softmax(jnp.where(mask, s, -jnp.inf), axis=-1).astype(v.dtype)
        outs.append(jnp.einsum('bhqk,bkhd->bqhd', p, v[:, :q1]))
    return jnp.concatenate(outs, axis=1)

def mla_layer(x, positions, norm_g, w_in, q_norm_g, kv_norm_g, w_uq, w_ukv, qn_g, kn_g, w_out):
    B, S, _ = x.shape
    u = rms_norm(x, norm_g) @ w_in
    cq, ckv, kpe, z = jnp.split(u, [Q_LORA, Q_LORA + KV_LORA, Q_LORA + KV_LORA + QK_ROPE], axis=-1)
    q = (rms_norm(cq, q_norm_g) @ w_uq).reshape(B, S, C_HEADS, QK_HEAD)
    kv = (rms_norm(ckv, kv_norm_g) @ w_ukv).reshape(B, S, C_HEADS, QK_NOPE + V_HEAD)
    k_nope, v = jnp.split(kv, [QK_NOPE], axis=-1)
    k = jnp.concatenate([k_nope, jnp.broadcast_to(kpe[:, :, None, :], (B, S, C_HEADS, QK_ROPE))], axis=-1)
    q = rms_norm(q, qn_g)
    k = rms_norm(k, kn_g)
    inv_freq = ROPE_THETA ** (-jnp.arange(0, QK_ROPE, 2, dtype=jnp.float32) / QK_ROPE)
    ang = positions.astype(jnp.float32)[..., None] * inv_freq
    cos = jnp.cos(ang)[:, :, None, :]
    sin = jnp.sin(ang)[:, :, None, :]
    q = jnp.concatenate([q[..., :QK_NOPE], rope(q[..., QK_NOPE:], cos, sin)], axis=-1)
    k = jnp.concatenate([k[..., :QK_NOPE], rope(k[..., QK_NOPE:], cos, sin)], axis=-1)
    o = block_causal_attention(q, k, v).reshape(B, S, C_WIDTH) * jax.nn.silu(z)
    return x + o @ w_out

def second_inputs(seed: int = 0) -> dict:
    key = jax.random.key(seed)
    ks = list(jax.random.split(key, 32))
    f32 = jnp.float32

    def normal(shape, scale):
        return jax.random.normal(ks.pop(), shape, f32) * scale

    def gain(shape):
        return 1.0 + normal(shape, 0.02)

    x = normal((BATCH, SEQ, D_MODEL), 1.0)
    offsets = jax.random.randint(ks.pop(), (BATCH, 1), 0, 64) * CHUNK
    positions = (offsets + jnp.arange(SEQ)[None, :]).astype(jnp.int32)
    a_b_if = jnp.concatenate([normal((N_A, M_HEADS), 0.1),
                              jnp.linspace(3.0, 6.0, M_HEADS)[None, :] + normal((N_A, M_HEADS), 0.1)], axis=-1)
    return {
        'x': x,
        'positions': positions,
        'a_norm_g': gain((N_A, D_MODEL)),
        'a_w_in': normal((N_A, D_MODEL, A_IN), D_MODEL ** -0.5),
        'a_b_if': a_b_if,
        'a_conv_w': normal((N_A, CONV_K, M_WIDTH), CONV_K ** -0.5),
        'a_conv_b': normal((N_A, M_WIDTH), 0.02),
        'a_w_q': normal((N_A, M_HEADS, M_HEAD_DIM, M_HEAD_DIM), M_HEAD_DIM ** -0.5),
        'a_w_k': normal((N_A, M_HEADS, M_HEAD_DIM, M_HEAD_DIM), M_HEAD_DIM ** -0.5),
        'a_w_v': normal((N_A, M_HEADS, M_HEAD_DIM, M_HEAD_DIM), M_HEAD_DIM ** -0.5),
        'a_head_norm_g': gain((N_A, M_WIDTH)),
        'a_skip': gain((N_A, M_WIDTH)),
        'a_pool_w': normal((N_A, P_GROUPS, P_GROUP_DIM, P_GROUP_DIM), P_GROUP_DIM ** -0.5),
        'a_pool_scale': 1.0 + normal((N_A, P_WIDTH), 0.1),
        'a_w_out': normal((N_A, A_OUT_IN, D_MODEL), A_OUT_IN ** -0.5),
        'c_norm_g': gain((N_C, D_MODEL)),
        'c_w_in': normal((N_C, D_MODEL, C_IN), D_MODEL ** -0.5),
        'c_q_norm_g': gain((N_C, Q_LORA)),
        'c_kv_norm_g': gain((N_C, KV_LORA)),
        'c_w_uq': normal((N_C, Q_LORA, C_HEADS * QK_HEAD), Q_LORA ** -0.5),
        'c_w_ukv': normal((N_C, KV_LORA, C_HEADS * (QK_NOPE + V_HEAD)), KV_LORA ** -0.5),
        'c_qn_g': gain((N_C, QK_HEAD)),
        'c_kn_g': gain((N_C, QK_HEAD)),
        'c_w_out': normal((N_C, C_WIDTH, D_MODEL), C_WIDTH ** -0.5),
    }

def second_block(x, positions, a_norm_g, a_w_in, a_b_if, a_conv_w, a_conv_b, a_w_q, a_w_k, a_w_v,
              a_head_norm_g, a_skip, a_pool_w, a_pool_scale, a_w_out, c_norm_g, c_w_in,
              c_q_norm_g, c_kv_norm_g, c_w_uq, c_w_ukv, c_qn_g, c_kn_g, c_w_out):
    for layer in range(DEPTH):
        j = layer // 2
        if layer % 2 == 0:
            x = mlstm_pool_layer(x, a_norm_g[j], a_w_in[j], a_b_if[j], a_conv_w[j], a_conv_b[j],
                                 a_w_q[j], a_w_k[j], a_w_v[j], a_head_norm_g[j], a_skip[j],
                                 a_pool_w[j], a_pool_scale[j], a_w_out[j])
        else:
            x = mla_layer(x, positions, c_norm_g[j], c_w_in[j], c_q_norm_g[j], c_kv_norm_g[j],
                          c_w_uq[j], c_w_ukv[j], c_qn_g[j], c_kn_g[j], c_w_out[j])
    return x


def setup_inputs(seed=0):
    out = dict(first_inputs(seed))
    for name, value in second_inputs(seed + 1).items():
        if name != "x":
            out[name + "_2"] = value
    return out


def reference(
    x, ffn1_norm, ffn1_w_gate_up, ffn1_w_down, mix_norm, w_in, forget_bias, lambda_q1,
    lambda_k1, lambda_q2, lambda_k2, diff_subln, w_out, ffn2_norm, ffn2_w_gate_up, ffn2_w_down,
    final_norm, positions_2, a_norm_g_2, a_w_in_2, a_b_if_2, a_conv_w_2, a_conv_b_2, a_w_q_2,
    a_w_k_2, a_w_v_2, a_head_norm_g_2, a_skip_2, a_pool_w_2, a_pool_scale_2, a_w_out_2,
    c_norm_g_2, c_w_in_2, c_q_norm_g_2, c_kv_norm_g_2, c_w_uq_2, c_w_ukv_2, c_qn_g_2, c_kn_g_2,
    c_w_out_2,
):
    x = first_block(
        x, ffn1_norm, ffn1_w_gate_up, ffn1_w_down, mix_norm, w_in, forget_bias, lambda_q1,
        lambda_k1, lambda_q2, lambda_k2, diff_subln, w_out, ffn2_norm, ffn2_w_gate_up,
        ffn2_w_down, final_norm,
    )
    return second_block(
        x, positions_2, a_norm_g_2, a_w_in_2, a_b_if_2, a_conv_w_2, a_conv_b_2, a_w_q_2,
        a_w_k_2, a_w_v_2, a_head_norm_g_2, a_skip_2, a_pool_w_2, a_pool_scale_2, a_w_out_2,
        c_norm_g_2, c_w_in_2, c_q_norm_g_2, c_kv_norm_g_2, c_w_uq_2, c_w_ukv_2, c_qn_g_2,
        c_kn_g_2, c_w_out_2,
    )


_drawn_inputs = setup_inputs


def setup_inputs(seed=0):
    import zlib

    import numpy as np

    out = dict(_drawn_inputs(seed))
    spreads = {}
    factors = {'ffn1_norm': 3.072,
     'lambda_q2': 3.473,
     'diff_subln': 2.718,
     'ffn2_norm': 4.394,
     'a_norm_g_2': 2.756,
     'a_conv_b_2': 2.892,
     'a_head_norm_g_2': 7.653,
     'a_skip_2': 8.0,
     'c_norm_g_2': 8.0,
     'c_q_norm_g_2': 8.0,
     'c_kv_norm_g_2': 8.0,
     'c_qn_g_2': 8.0,
     'c_kn_g_2': 8.0}
    for name, (base, spread) in spreads.items():
        noise = np.random.default_rng([zlib.crc32(name.encode()), seed]).standard_normal(out[name].shape)
        drawn = base * np.exp(spread * noise) if base else spread * noise
        out[name] = __import__('jax').numpy.asarray(drawn.astype(out[name].dtype))
    for name, factor in factors.items():
        out[name] = (out[name] * factor).astype(out[name].dtype)
    return out
```

```python
import math
from contextlib import ExitStack

import concourse.bass as bass
from concourse import mybir

P = 128
D = 1024
S = 512
KT = D // P
TB = S // P
DEPTH = 2
D_FF = 2816
FT = D_FF // P
FOX_HEADS = 8
DIFF_HEADS = 4
HEAD = 64
M_HEADS = 4
M_DIM = D // M_HEADS
CONV_K = 4
P_WINDOWS = (2, 4, 8, 16)
C_HEADS = 8
QK_NOPE, QK_ROPE = 128, 64
QK_HEAD = QK_NOPE + QK_ROPE
Q_LORA, KV_LORA = 384, 256
QT, KVT = Q_LORA // P, KV_LORA // P
ROPE_THETA = 10000.0
NORM_EPS, RMS_EPS = 1e-5, 1e-6
SLOTS = 4
UNIT = 8 * P
BIG = 1.0e30

F32 = mybir.dt.float32
F32R = mybir.dt.float32r
I32 = mybir.dt.int32
ALU = mybir.AluOpType
ACT = mybir.ActivationFunctionType
AX_X = mybir.AxisListType.X

UP_UNITS, DOWN_UNITS = 2 * FT, FT
FFN_UNITS = UP_UNITS + DOWN_UNITS
MIX_IN = 25
MIX_UNITS = MIX_IN + KT
LAYER_UNITS = 2 * FFN_UNITS + MIX_UNITS
A_START = DEPTH * LAYER_UNITS
A_UNITS = 1 + 4 * M_HEADS + 2 * KT + 5 * 4 + 2 * KT
C_START = A_START + A_UNITS
C_IN = QT + KVT + 1
C_UQ, C_UKV = 6, 4
C_UNITS = C_IN + C_UQ + C_UKV + 2 * KT
UNITS = C_START + C_UNITS
NORMS = 3 * DEPTH + 3
FINAL = 3 * DEPTH

COLS = {}


def _columns():
    at = 0
    for name, n in (
        [(f"{k}{l}", 8) for l in range(DEPTH) for k in ("ffn1_norm", "mix_norm", "ffn2_norm")]
        + [(f"{k}{l}", 1) for l in range(DEPTH) for k in ("subln", "forget_bias", "lq1_", "lk1_", "lq2_", "lk2_")]
        + [("final_norm", 8), ("a_norm", 8), ("conv_w", 32), ("conv_b", 8), ("head_norm", 8), ("skip", 8),
           ("pool_scale", 8), ("b_if", 1), ("c_norm", 8), ("q_norm", QT), ("kv_norm", KVT),
           ("qn_nope", 1), ("qn_rope", 1), ("kn_nope", 1), ("kn_rope", 1), ("inv_freq", 1), ("rope_sign", 1)]
    ):
        COLS[name] = at
        at += n
    return at


NCOLS = _columns()
NTAB = P * 5 + P * FOX_HEADS + 4 * 16 + 2
TAB = {"identity": 0, "ones": P, "causal": 2 * P, "causal_t": 3 * P, "chunked": 4 * P, "select": 5 * P,
       "pool_head": 5 * P + P * FOX_HEADS, "halves": NTAB - 2}


def lambda_init(layer):
    return 0.8 - 0.6 * math.exp(-0.3 * layer)


def count(start, it, step):
    return start if it is None else it * step + start


def build(nc, x_in, stream, cols_in, tab_in, rope_in, pos_in, out):
    with ExitStack() as ctx:
        def sem(name):
            return ctx.enter_context(nc.semaphore(name))

        here = [0]
        arena_bytes = 207 * 1024
        arena = ctx.enter_context(nc.sbuf_tensor("arena", [P, arena_bytes // 4], F32))
        origin = -(-(nc.sbuf_base - arena_bytes) // 32) * 32

        def place(name, shape, dt=F32, at=None):
            size = 4 * math.prod(shape[1:])
            at = -(-here[0] // 32) * 32 if at is None else at
            here[0] = at + size
            assert here[0] <= arena_bytes, (name, here[0])
            return nc.alloc_sbuf_tensor_at(name, shape, dt, offset=origin + at)

        x = place("x", [P, KT, S])
        w_raw = place("w_raw", [P, SLOTS, UNIT])
        w_hi = place("w_hi", [P, SLOTS, UNIT], F32R)
        w_lo = place("w_lo", [P, SLOTS, UNIT], F32R)
        rstd = place("rstd", [P, S])
        sqsum = place("sqsum", [P, S])
        tmp = place("tmp", [P, 4, S])
        cols = place("cols", [P, NCOLS])
        tab = place("tab", [P, NTAB])
        lam = place("lam", [P, 8])
        small = place("small", [P, 4])
        softstat = place("softstat", [P, 64, 3])
        m_cols = place("m_cols", [P, 4 * TB])
        m_mask = place("m_mask", [P, 2, P])
        q_scale = place("q_scale", [P, C_HEADS * TB])
        H_AT = -(-here[0] // 32) * 32
        h_hi = place("h_hi", [P, KT, S], F32R)
        h_lo = place("h_lo", [P, KT, S], F32R)
        R_AT = here[0]
        hid_hi = place("hid_hi", [P, FT, S], F32R, at=R_AT)
        hid_lo = place("hid_lo", [P, FT, S], F32R)
        x_tok = place("x_tok", [P, TB, D], at=R_AT)
        dq = place("dq", [P, 4, S], at=R_AT)
        dk = place("dk", [P, 4, S])
        fq = place("fq", [P, 4, S])
        fk = place("fk", [P, 4, S])
        fv = place("fv", [P, TB, S])
        dv = place("dv", [P, TB, S])
        o_hi = place("o_hi", [P, KT, S], F32R)
        o_lo = place("o_lo", [P, KT, S], F32R)
        probs = place("probs", [P, 4, S])
        cos_sin = place("cos_sin", [P, 2, S], at=here[0] - 4 * 4 * S)
        probs_t = place("probs_t", [P, 2, TB, S], at=H_AT)
        norm_sq = tmp[:, 2:4, :]
        gate_rows = tmp[0:8, 2:4, :]
        negcum = sqsum[0:8, :]

        bank = [ctx.enter_context(nc.psum_tensor(f"bank{b}", [P, S], F32)) for b in range(8)]

        identity = tab[:, 0:P]
        ones = tab[:, P:2 * P]

        def table(name, n=P):
            return tab[:, TAB[name]:TAB[name] + n]

        def col(name, i=0, rows=slice(0, P)):
            return cols[rows, COLS[name] + i:COLS[name] + i + 1]

        consts_in = sem("consts_in")
        x_in_sem = sem("x_in_sem")
        landed = [sem(f"landed{b}") for b in range(SLOTS)]
        hi_ready = sem("hi_ready")
        lo_ready = sem("lo_ready")
        unit_used = sem("unit_used")
        x_ready = sem("x_ready")
        sq_ready = sem("sq_ready")
        sq_added = sem("sq_added")
        h_half = sem("h_half")
        h_ready = sem("h_ready")
        ss_ready = sem("ss_ready")
        sd_ready = sem("sd_ready")
        small_ready = sem("small_ready")
        lam_prod, lam_sum, lam_exp = sem("lam_prod"), sem("lam_sum"), sem("lam_exp")
        x_turned = sem("x_turned")
        up_evac = sem("up_evac")
        gate_silu = sem("gate_silu")
        prod_ready, hid_half, hid_ready = sem("prod_ready"), sem("hid_half"), sem("hid_ready")
        down_done = sem("down_done")
        in_evac = sem("in_evac")
        rope_in_sem = sem("rope_in_sem")
        turned = sem("turned")
        v_turned, v_ready = sem("v_turned"), sem("v_ready")
        g_step = sem("g_step")
        cum_ready, qk_ready = sem("cum_ready"), sem("qk_ready")
        scored, maxed, exped = sem("scored"), sem("maxed"), sem("exped")
        weighed, flipped, flip_out = sem("weighed"), sem("flipped"), sem("flip_out")
        mixed = sem("mixed")
        d_out, d_sq, d_ss, d_root, d_norm = (sem(n) for n in ("d_out", "d_sq", "d_ss", "d_root", "d_norm"))
        o_half, o_ready = sem("o_half"), sem("o_ready")

        block = ctx.enter_context(nc.Block())
        half_gain = {0: "ffn1_norm0", 1: "mix_norm0", 2: "ffn2_norm0", 3: "ffn1_norm1", 4: "mix_norm1",
                     5: "ffn2_norm1", 7: "a_norm", 8: "c_norm"}

        MIX_ORDER = [(k, i) for k in ("dq", "dk", "fq", "fk") for i in range(4)] + [("gates", 0)] + \
                    [(k, i) for k in ("fv", "dv") for i in range(4)]
        STEPS = [("d", h, b) for h in range(DIFF_HEADS) for b in range(TB)] + \
                [("f", h, b) for h in range(FOX_HEADS) for b in range(TB)]
        EXPS = []
        FIRST_EXP = []
        for k, (kind, _, _) in enumerate(STEPS):
            FIRST_EXP.append(len(EXPS))
            EXPS += [(k, c) for c in range(2 if kind == "d" else 1)]
        NSTEP, NEXP = len(STEPS), len(EXPS)
        NHEAD = DIFF_HEADS + FOX_HEADS
        head_of = [h if kind == "d" else DIFF_HEADS + h for kind, h, _ in STEPS]
        FLIP_LAG, MIX_LAG, OUT_LAG = 2, 3, 4
        D_NORM_STEP = TB * DIFF_HEADS + OUT_LAG

        def h_count(r):
            return KT * (r - (r > FINAL))

        def act_cut(n, it=None):
            if n >= UNITS:
                return
            s = n % SLOTS
            nc.scalar.wait_ge(landed[s], count(16 * (n // SLOTS + 1), it, 16))
            if n >= SLOTS:
                nc.scalar.wait_ge(unit_used, count(n - SLOTS + 1, it, SLOTS))
            nc.scalar.activation(w_hi[:, s, :], w_raw[:, s, :], ACT.Copy).then_inc(hi_ready, 1)

        def act_h_tile(r, m):
            nc.scalar.wait_ge(x_ready, KT * r + m + 1)
            if m >= 2:
                nc.scalar.wait_ge(sq_added, KT * r + m - 1)
            nc.scalar.activation(tmp[:, m % 2, :], x[:, m, :], ACT.Square).then_inc(sq_ready, 1)
            if r != FINAL:
                nc.scalar.activation(h_hi[:, m, :], x[:, m, :], ACT.Copy,
                                     scale=col(half_gain[r], m)).then_inc(h_half, 1)

        def act_root(r):
            nc.scalar.wait_ge(ss_ready, r + 1)
            eps = small[:, 0:1] if r <= FINAL else small[:, 1:2]
            nc.scalar.activation(tmp[:, 2, :], bank[7][:, :], ACT.Sqrt, scale=1.0 / D, bias=eps).then_inc(sd_ready, 1)

        def dve_cut(n, it=None):
            if n >= UNITS:
                return
            s = n % SLOTS
            nc.vector.wait_ge(hi_ready, count(n + 1, it, SLOTS))
            nc.vector.tensor_tensor(w_lo[:, s, :], w_raw[:, s, :], w_hi[:, s, :].bitcast(F32),
                                    ALU.subtract).then_inc(lo_ready, 1)

        def dve_h_tile(r, m):
            if r == FINAL:
                return
            nc.vector.wait_ge(h_half, h_count(r) + m + 1)
            nc.vector.scalar_tensor_tensor(out=h_lo[:, m, :], in0=x[:, m, :], scalar=col(half_gain[r], m),
                                           in1=h_hi[:, m, :].bitcast(F32), op0=ALU.mult,
                                           op1=ALU.subtract).then_inc(h_ready, 1)

        def dve_norm(r):
            nc.vector.wait_ge(sd_ready, r + 1)
            nc.vector.reciprocal(rstd[:, :], tmp[:, 2, :])
            nc.vector.drain()

        def pe_three(dst, whi, wlo, xhi, xlo, start, stop):
            nc.tensor.matmul(dst, whi, xhi, start=start, stop=False)
            nc.tensor.matmul(dst, whi, xlo, start=False, stop=False)
            return nc.tensor.matmul(dst, wlo, xhi, start=False, stop=stop)

        def pe_unit(n, it, dst, hi, lo, arrive=None):
            s = n % SLOTS
            nc.tensor.wait_ge(lo_ready, count(n + 1, it, SLOTS))
            for kt in range(8):
                if arrive:
                    arrive(kt)
                ins = pe_three(dst, w_hi[:, s, P * kt:P * kt + P], w_lo[:, s, P * kt:P * kt + P],
                            hi[:, kt, :], lo[:, kt, :], kt == 0, kt == 7)
            ins.then_inc(unit_used, 1)

        def pe_h_arrive(r):
            return lambda kt: nc.tensor.wait_ge(h_ready, h_count(r) + kt + 1)

        def pe_sum_squares(r):
            nc.tensor.wait_ge(sq_added, KT * r + KT)
            nc.tensor.matmul(bank[7][:, :], ones, sqsum[:, :], start=True, stop=True).then_inc(ss_ready, 1)

        @block.sync
        def _(sp):
            sp.dma_start(cols[:, :], cols_in).then_inc(consts_in, 16)
            sp.dma_start(tab[:, :], tab_in).then_inc(consts_in, 16)
            sp.dma_start(x_tok[:, :, :], x_in.rearrange("(b p) d -> p b d", p=P)).then_inc(x_in_sem, 16)
            for n in range(SLOTS):
                sp.dma_start(w_raw[:, n, :], stream[n, :, :]).then_inc(landed[n], 16)
            with sp.Fori(1, UNITS // SLOTS) as it:
                for s in range(SLOTS):
                    sp.wait_ge(lo_ready, it * SLOTS + (s - SLOTS + 1))
                    sp.dma_start(w_raw[:, s, :], stream[bass.ds(it * SLOTS + s, 1), :, :]
                                 .rearrange("o p n -> p (o n)")).then_inc(landed[s], 16)
            for n in range(UNITS // SLOTS * SLOTS, UNITS):
                sp.wait_ge(lo_ready, n - SLOTS + 1)
                sp.dma_start(w_raw[:, n % SLOTS, :], stream[n, :, :]).then_inc(landed[n % SLOTS], 16)

        @block.gpsimd
        def _(pool):
            for r in range(NORMS):
                for m in range(KT):
                    pool.wait_ge(sq_ready, 8 * r + m + 1)
                    if m == 0:
                        if r:
                            pool.wait_ge(ss_ready, r)
                        if r in (2, 5):
                            pool.wait_ge(mixed, (r // 3 + 1) * NHEAD)
                        nc.gpsimd.tensor_copy(sqsum[:, :], tmp[:, 0, :]).then_inc(sq_added, 1)
                    else:
                        pool.wait_ge(sq_added, 8 * r + m)
                        nc.gpsimd.tensor_tensor(sqsum[:, :], sqsum[:, :], tmp[:, m % 2, :],
                                                ALU.add).then_inc(sq_added, 1)

        @block.scalar
        def _(act):
            def ffn(f, r, n0):
                def up(c, it):
                    act_cut(n0 + c + 3, it)
                    j = 22 * f + c // 2 + 1
                    if c % 2 == 0:
                        act.wait_ge(up_evac, count(4 + UP_UNITS * f + c + 1, it, 4))
                        nc.scalar.activation(tmp[:, 1, :], tmp[:, 0, :], ACT.Silu).then_inc(gate_silu, 1)
                    else:
                        act.wait_ge(prod_ready, count(j, it, 2))
                        dst = hid_hi[:, c // 2, :] if it is None else \
                            hid_hi[:, bass.ds(it * 2 + c // 2, 1), :].rearrange("p o n -> p (o n)")
                        nc.scalar.activation(dst, tmp[:, 3, :], ACT.Copy).then_inc(hid_half, 1)

                for c in range(4):
                    up(c, None)
                with act.Fori(1, FT // 2) as it:
                    for c in range(4):
                        up(c, it)
                n0 += UP_UNITS
                with act.Fori(0, 4) as it:
                    for c in range(4):
                        act_cut(n0 + c + 3, it)
                for j in range(16, 20):
                    act_cut(n0 + j + 3)
                for m in range(KT):
                    act_h_tile(r, m)
                act_cut(n0 + 23)
                act_cut(n0 + 24)
                act_root(r)

            def mixer(layer, r, n0):
                act.dma_start(cos_sin[:, :, :], rope_in).then_inc(rope_in_sem, 16)
                for i, (kind, t) in enumerate(MIX_ORDER + [("", 0)]):
                    if i < MIX_IN:
                        act_cut(n0 + i + 3)
                    if 1 <= i <= 8:
                        b = i - 1
                        act.wait_ge(in_evac, MIX_IN * layer + b + 1)
                        for q in range(4):
                            ins = nc.scalar.activation(tmp[32 * q:32 * q + 32, 2 + b % 2, :],
                                                       tmp[32 * (q ^ 1):32 * (q ^ 1) + 32, b % 2, :], ACT.Copy)
                        ins.then_inc(turned, 1)
                    if kind == "gates":
                        act.wait_ge(g_step, 2 * layer + 1)
                        nc.scalar.activation(gate_rows[:, 1, :], gate_rows[:, 0, :], ACT.Abs)
                        act.drain()
                        nc.scalar.activation(gate_rows[:, 1, :], gate_rows[:, 1, :], ACT.Exp, scale=-1.0)
                        act.drain()
                        nc.scalar.activation(gate_rows[:, 1, :], gate_rows[:, 1, :], ACT.Ln,
                                             bias=1.0).then_inc(g_step, 1)
                    j = i - 18
                    if 0 <= j < 8:
                        act.wait_ge(v_turned, 8 * layer + j + 1)
                        v = (fv if j < 4 else dv)[:, :, P * (j % 4):P * (j % 4) + P]
                        nc.scalar.activation(v, bank[4 + j % 2][:, :].rearrange("p (b n) -> p b n", b=TB),
                                             ACT.Copy).then_inc(v_ready, 1)
                for k in range(NSTEP + OUT_LAG):
                    if k < NSTEP:
                        width = P * (STEPS[k][2] + 1)
                        for e in range(FIRST_EXP[k], FIRST_EXP[k] + (2 if STEPS[k][0] == "d" else 1)):
                            act.wait_ge(maxed, NEXP * layer + e + 1)
                            if e >= 4:
                                act.wait_ge(flipped, NSTEP * layer + EXPS[e - 4][0] + 1)
                            nc.scalar.activation(probs[:, e % 4, 0:width], bank[e % 4][:, 0:width], ACT.Exp,
                                                 bias=softstat[:, e, 0:1],
                                                 accum_out=softstat[:, e, 1:2]).then_inc(exped, 1)
                    if 0 <= k - FLIP_LAG < NSTEP:
                        j = k - FLIP_LAG
                        b, hh = STEPS[j][2], head_of[j]
                        act.wait_ge(flipped, NSTEP * layer + j + 1)
                        if b == 0 and hh >= 2:
                            act.wait_ge(mixed, NHEAD * layer + hh - 1)
                        nc.scalar.activation(probs_t[:, hh % 2, 0:b + 1, P * b:P * b + P],
                                             bank[4 + j % 2][:, 0:P * (b + 1)].rearrange("p (b n) -> p b n", n=P),
                                             ACT.Copy).then_inc(flip_out, 1)
                    h = k - D_NORM_STEP
                    if 0 <= h < DIFF_HEADS:
                        act.wait_ge(d_out, DIFF_HEADS * layer + h + 1)
                        if h >= 2:
                            act.wait_ge(d_ss, DIFF_HEADS * layer + h - 1)
                        nc.scalar.activation(norm_sq[:, h % 2, :], dq[:, h, :], ACT.Square).then_inc(d_sq, 1)
                    if 0 <= h - 1 < DIFF_HEADS:
                        act.wait_ge(d_ss, DIFF_HEADS * layer + h)
                        nc.scalar.activation(dk[:, h - 1, :], bank[7][:, :], ACT.Sqrt, scale=1.0 / P,
                                             bias=small[:, 0:1]).then_inc(d_root, 1)
                    if 0 <= h - 2 < DIFF_HEADS:
                        act.wait_ge(d_norm, DIFF_HEADS * layer + h - 1)
                        nc.scalar.activation(o_hi[:, 4 + h - 2, :], dq[:, h - 2, :], ACT.Copy).then_inc(o_half, 1)
                    j = k - OUT_LAG
                    if j >= 0 and STEPS[j][0] == "f" and STEPS[j][2] == TB - 1 and STEPS[j][1] % 2:
                        pair = STEPS[j][1] // 2
                        act.wait_ge(mixed, NHEAD * layer + DIFF_HEADS + 2 * pair + 2)
                        nc.scalar.activation(o_hi[:, pair, :], bank[6 + pair % 2][:, :], ACT.Copy).then_inc(o_half, 1)
                for m in range(KT):
                    if m < 6:
                        act_cut(n0 + MIX_IN + m + 3)
                    act_h_tile(r, m)
                for n in range(6, 8):
                    act_cut(n0 + MIX_IN + n + 3)
                act_root(r)

            act.wait_ge(consts_in, 32)
            act.wait_ge(small_ready, 1)
            for n in range(3):
                act_cut(n)
            act.wait_ge(lam_sum, 1)
            nc.scalar.activation(lam[:, 0:4], bank[7][:, 0:4], ACT.Exp).then_inc(lam_exp, 1)
            for m in range(KT):
                act_h_tile(0, m)
            act_root(0)
            for layer in range(DEPTH):
                n0, r = layer * LAYER_UNITS, 3 * layer
                ffn(2 * layer, r + 1, n0)
                mixer(layer, r + 2, n0 + FFN_UNITS)
                ffn(2 * layer + 1, r + 3, n0 + FFN_UNITS + MIX_UNITS)

        @block.vector
        def _(dve):
            def residual(r, wait_tile, scale):
                for m in range(KT + 1):
                    if m < KT:
                        wait_tile(m)
                        if scale is None:
                            ins = nc.vector.tensor_copy(x[:, m, :], bank[m][:, :])
                        else:
                            ins = nc.vector.scalar_tensor_tensor(out=x[:, m, :], in0=bank[m][:, :], scalar=scale,
                                                                 in1=x[:, m, :], op0=ALU.mult, op1=ALU.add)
                        ins.then_inc(x_ready, 1)
                    if m >= 1:
                        dve_h_tile(r, m - 1)

            def ffn(f, r, n0):
                with dve.Fori(0, FT // 2) as it:
                    for c in range(4):
                        dve_cut(n0 + c + 3, it)
                        dve.wait_ge(unit_used, count(n0 + c + 1, it, SLOTS))
                        nc.vector.tensor_tensor(tmp[:, 2 * (c % 2), :], bank[c][:, :], rstd[:, :],
                                                ALU.mult).then_inc(up_evac, 1)
                        if c % 2:
                            j = 22 * f + c // 2 + 1
                            dve.drain()
                            dve.wait_ge(gate_silu, count(j, it, 2))
                            nc.vector.tensor_tensor(tmp[:, 3, :], tmp[:, 1, :], tmp[:, 2, :],
                                                    ALU.mult).then_inc(prod_ready, 1)
                            dve.wait_ge(hid_half, count(j, it, 2))
                            tile = bass.ds(it * 2 + c // 2, 1)
                            nc.vector.tensor_tensor(
                                hid_lo[:, tile, :].rearrange("p o n -> p (o n)"), tmp[:, 3, :],
                                hid_hi[:, tile, :].rearrange("p o n -> p (o n)").bitcast(F32),
                                ALU.subtract).then_inc(hid_ready, 1)
                n0 += UP_UNITS
                with dve.Fori(0, 4) as it:
                    for c in range(4):
                        dve_cut(n0 + c + 3, it)
                for j in range(16, 20):
                    dve_cut(n0 + j + 3)
                residual(r, lambda m: dve.wait_ge(down_done, 7 * f + m + 1) if m < 7
                         else dve.wait_ge(unit_used, n0 + DOWN_UNITS), 0.5)
                dve_cut(n0 + 23)
                dve_cut(n0 + 24)
                dve_norm(r)

            def rope(layer, b):
                dst = (dq if b < 4 else dk)[:, b % 4, :]
                dve.wait_ge(turned, 8 * layer + b + 1)
                nc.vector.tensor_tensor(dst, tmp[:, b % 2, :], cos_sin[:, 0, :], ALU.mult)
                nc.vector.tensor_tensor(tmp[:, 2 + b % 2, :], tmp[:, 2 + b % 2, :], cos_sin[:, 1, :], ALU.mult)
                dve.drain()
                nc.vector.tensor_tensor(dst, dst, tmp[:, 2 + b % 2, :], ALU.add).then_inc(qk_ready, 1)

            def mixer(layer, r, n0):
                for i, (kind, t) in enumerate(MIX_ORDER):
                    dve_cut(n0 + i + 3)
                    dve.wait_ge(unit_used, n0 + i + 1)
                    src = bank[i % 4]
                    if kind in ("dq", "dk"):
                        if i == 0:
                            dve.wait_ge(rope_in_sem, 16 * (layer + 1))
                        nc.vector.scalar_tensor_tensor(
                            out=tmp[:, i % 2, :], in0=src[:, :], scalar=HEAD ** -0.5 if kind == "dq" else 1.0,
                            in1=rstd[:, :], op0=ALU.mult, op1=ALU.mult).then_inc(in_evac, 1)
                    elif kind in ("fq", "fk"):
                        nc.vector.scalar_tensor_tensor(
                            out=(fq if kind == "fq" else fk)[:, t, :], in0=src[:, :],
                            scalar=HEAD ** -0.5 if kind == "fq" else 1.0, in1=rstd[:, :], op0=ALU.mult,
                            op1=ALU.mult).then_inc(in_evac, 1)
                    elif kind == "gates":
                        nc.vector.tensor_tensor(gate_rows[:, 0, :], src[0:8, :], rstd[0:8, :],
                                                ALU.mult).then_inc(in_evac, 1)
                        nc.vector.memset(tmp[0:8, 1, :], 1.0)
                        dve.drain()
                        nc.vector.tensor_scalar(gate_rows[:, 0, :], gate_rows[:, 0, :],
                                                col(f"forget_bias{layer}", 0, slice(0, 8)), None,
                                                ALU.add).then_inc(g_step, 1)
                        dve.wait_ge(g_step, 2 * layer + 2)
                        nc.vector.scalar_tensor_tensor(out=gate_rows[:, 0, :], in0=gate_rows[:, 0, :], scalar=0.0,
                                                       in1=gate_rows[:, 1, :], op0=ALU.min, op1=ALU.subtract)
                        dve.drain()
                        nc.vector.tensor_tensor_scan(negcum, tmp[0:8, 1, :], gate_rows[:, 0, :], 0.0, ALU.mult,
                                                     ALU.subtract).then_inc(cum_ready, 1)
                    else:
                        j = i - 17
                        if j == 0:
                            dve.wait_ge(cum_ready, layer + 1)
                        if j >= 2:
                            dve.wait_ge(v_turned, 8 * layer + j - 1)
                        nc.vector.tensor_tensor(tmp[:, j % 2, :], src[:, :], rstd[:, :],
                                                ALU.mult).then_inc(in_evac, 1)
                    if 1 <= i <= 8:
                        rope(layer, i - 1)
                for k in range(NSTEP + OUT_LAG):
                    if k < NSTEP:
                        width = P * (STEPS[k][2] + 1)
                        for e in range(FIRST_EXP[k], FIRST_EXP[k] + (2 if STEPS[k][0] == "d" else 1)):
                            dve.wait_ge(scored, NEXP * layer + e + 1)
                            nc.vector.tensor_reduce(softstat[:, e, 0:1], bank[e % 4][:, 0:width], AX_X, ALU.max,
                                                    negate=True).then_inc(maxed, 1)
                    if 1 <= k <= NSTEP:
                        weigh(layer, k - 1)
                    if k >= OUT_LAG and STEPS[k - OUT_LAG][2] == TB - 1:
                        head_out(layer, k - OUT_LAG)
                    h = k - D_NORM_STEP - 1
                    if 0 <= h < DIFF_HEADS:
                        dve.wait_ge(d_root, DIFF_HEADS * layer + h + 1)
                        nc.vector.reciprocal(tmp[:, h % 2, :], dk[:, h, :])
                        dve.drain()
                        nc.vector.scalar_tensor_tensor(
                            out=dq[:, h, :], in0=dq[:, h, :], scalar=lam[:, 6 + layer:7 + layer],
                            in1=tmp[:, h % 2, :], op0=ALU.mult, op1=ALU.mult).then_inc(d_norm, 1)
                    if 0 <= h - 1 < DIFF_HEADS:
                        dve.wait_ge(o_half, KT * layer + h)
                        nc.vector.tensor_tensor(o_lo[:, 4 + h - 1, :], dq[:, h - 1, :],
                                                o_hi[:, 4 + h - 1, :].bitcast(F32), ALU.subtract).then_inc(o_ready, 1)
                for m in range(KT + 1):
                    if m < KT:
                        if m < 6:
                            dve_cut(n0 + MIX_IN + m + 3)
                        dve.wait_ge(unit_used, n0 + MIX_IN + m + 1)
                        nc.vector.scalar_tensor_tensor(out=x[:, m, :], in0=bank[m % 4][:, :], scalar=1.0,
                                                       in1=x[:, m, :], op0=ALU.mult, op1=ALU.add).then_inc(x_ready, 1)
                    if m >= 1:
                        dve_h_tile(r, m - 1)
                for n in range(6, 8):
                    dve_cut(n0 + MIX_IN + n + 3)
                dve_norm(r)

            def weigh(layer, k):
                kind, h, b = STEPS[k]
                width, e = P * (b + 1), FIRST_EXP[k]
                dve.wait_ge(exped, NEXP * layer + e + (2 if kind == "d" else 1))
                if kind == "f":
                    nc.vector.reciprocal(softstat[:, e, 2:3], softstat[:, e, 1:2])
                    dve.drain()
                    nc.vector.tensor_scalar(probs[:, e % 4, 0:width], probs[:, e % 4, 0:width],
                                            softstat[:, e, 2:3], None, ALU.mult).then_inc(weighed, 1)
                else:
                    nc.vector.reciprocal(softstat[:, e:e + 2, 2], softstat[:, e:e + 2, 1])
                    dve.drain()
                    p0, p1 = probs[:, e % 4, 0:width], probs[:, (e + 1) % 4, 0:width]
                    nc.vector.tensor_scalar(p1, p1, softstat[:, e + 1, 2:3], lam[:, 4 + layer:5 + layer],
                                            ALU.mult, ALU.mult)
                    dve.drain()
                    nc.vector.scalar_tensor_tensor(out=p0, in0=p0, scalar=softstat[:, e, 2:3], in1=p1,
                                                   op0=ALU.mult, op1=ALU.subtract).then_inc(weighed, 1)

            def head_out(layer, k):
                kind, h, _ = STEPS[k]
                if kind == "d":
                    dve.wait_ge(mixed, NHEAD * layer + h + 1)
                    nc.vector.tensor_copy(dq[:, h, :], bank[6 + h % 2][:, :]).then_inc(d_out, 1)
                elif h % 2:
                    pair = h // 2
                    dve.wait_ge(o_half, KT * layer + DIFF_HEADS + pair + 1)
                    nc.vector.tensor_tensor(o_lo[:, pair, :], bank[6 + pair % 2][:, :],
                                            o_hi[:, pair, :].bitcast(F32), ALU.subtract).then_inc(o_ready, 1)

            dve.sem_inc(up_evac, 4)
            nc.vector.memset(small[:, 0:1], NORM_EPS)
            nc.vector.memset(small[:, 1:2], RMS_EPS)
            nc.vector.memset(small[:, 2:3], math.pi / 2).then_inc(small_ready, 1)
            dve.wait_ge(consts_in, 32)
            for layer in range(DEPTH):
                for i in range(2):
                    ins = nc.vector.tensor_tensor(tmp[0:HEAD, 3, 2 * layer + i:2 * layer + i + 1],
                                                  col(f"lq{i + 1}_{layer}", 0, slice(0, HEAD)),
                                                  col(f"lk{i + 1}_{layer}", 0, slice(0, HEAD)), ALU.mult)
            ins.then_inc(lam_prod, 1)
            for n in range(3):
                dve_cut(n)
            dve.wait_ge(lam_exp, 1)
            for layer in range(DEPTH):
                nc.vector.scalar_tensor_tensor(out=lam[:, 4 + layer:5 + layer], in0=lam[:, 2 * layer:2 * layer + 1],
                                               scalar=lambda_init(layer), in1=lam[:, 2 * layer + 1:2 * layer + 2],
                                               op0=ALU.add, op1=ALU.subtract)
                nc.vector.tensor_scalar(lam[:, 6 + layer:7 + layer], col(f"subln{layer}"),
                                        1.0 - lambda_init(layer), None, ALU.mult)
            dve.drain()
            residual(0, lambda m: dve.wait_ge(x_turned, m + 1), None)
            dve_norm(0)
            for layer in range(DEPTH):
                n0, r = layer * LAYER_UNITS, 3 * layer
                ffn(2 * layer, r + 1, n0)
                mixer(layer, r + 2, n0 + FFN_UNITS)
                ffn(2 * layer + 1, r + 3, n0 + FFN_UNITS + MIX_UNITS)

        @block.tensor
        def _(pe):
            def ffn(f, r, n0):
                def up(c, it, arrive=None):
                    pe.wait_ge(up_evac, count(UP_UNITS * f + c + 1, it, 4))
                    pe_unit(n0 + c, it, bank[c][:, :], h_hi, h_lo, arrive)

                up(0, None, pe_h_arrive(r - 1))
                pe_sum_squares(r - 1)
                for c in range(1, 4):
                    up(c, None)
                with pe.Fori(1, FT // 2) as it:
                    for c in range(4):
                        up(c, it)
                n0 += UP_UNITS

                def down(j, it, order, tile):
                    s = (n0 + j) % SLOTS
                    pe.wait_ge(lo_ready, count(n0 + j + 1, it, SLOTS))
                    pe.wait_ge(hid_ready, count(FT * f + j + 1, it, 4))
                    for m in order:
                        if j == 0 and m < 4:
                            pe.wait_ge(up_evac, UP_UNITS * (f + 1) + m + 1)
                        ins = pe_three(bank[m][:, :], w_hi[:, s, P * m:P * m + P], w_lo[:, s, P * m:P * m + P],
                                    hid_hi[:, tile, :], hid_lo[:, tile, :], j == 0 and it is None, False)
                    ins.then_inc(unit_used, 1)

                for j in range(4):
                    down(j, None, (4, 5, 6, 7, 0, 1, 2, 3), j)
                with pe.Fori(0, 3) as it:
                    for c in range(4):
                        s = (n0 + c) % SLOTS
                        pe.wait_ge(lo_ready, count(n0 + 4 + c + 1, it, SLOTS))
                        pe.wait_ge(hid_ready, count(FT * f + 4 + c + 1, it, 4))
                        tile = bass.ds(it * 4 + (4 + c), 1)
                        xhi = hid_hi[:, tile, :].rearrange("p o n -> p (o n)")
                        xlo = hid_lo[:, tile, :].rearrange("p o n -> p (o n)")
                        for m in range(8):
                            ins = pe_three(bank[m][:, :], w_hi[:, s, P * m:P * m + P], w_lo[:, s, P * m:P * m + P],
                                        xhi, xlo, False, False)
                        ins.then_inc(unit_used, 1)
                for j in range(16, 19):
                    down(j, None, range(8), j)
                pe.wait_ge(lo_ready, n0 + FT)
                pe.wait_ge(hid_ready, FT * (f + 1))
                for m in range(8):
                    for j in range(19, 22):
                        s = (n0 + j) % SLOTS
                        ins = pe_three(bank[m][:, :], w_hi[:, s, P * m:P * m + P], w_lo[:, s, P * m:P * m + P],
                                    hid_hi[:, j, :], hid_lo[:, j, :], False, j == 21)
                        if m == 7:
                            ins.then_inc(unit_used, 1)
                    if m < 7:
                        ins.then_inc(down_done, 1)

            def mixer(layer, r, n0):
                for i, (kind, t) in enumerate(MIX_ORDER):
                    if i >= 4:
                        pe.wait_ge(in_evac, MIX_IN * layer + i - 3)
                    pe_unit(n0 + i, None, bank[i % 4][:, :], h_hi, h_lo, pe_h_arrive(r - 1) if i == 0 else None)
                    if i == 0:
                        pe_sum_squares(r - 1)
                    if i >= 18:
                        turn_v(layer, i - 18)
                turn_v(layer, 7)
                for k in range(NSTEP + OUT_LAG):
                    if k < NSTEP:
                        scores(layer, k)
                    if 0 <= k - FLIP_LAG < NSTEP:
                        flip(layer, k - FLIP_LAG)
                    if 0 <= k - MIX_LAG < NSTEP and STEPS[k - MIX_LAG][2] == TB - 1:
                        mix(layer, k - MIX_LAG)
                    h = k - D_NORM_STEP
                    if 0 <= h < DIFF_HEADS:
                        pe.wait_ge(d_sq, DIFF_HEADS * layer + h + 1)
                        if h:
                            pe.wait_ge(d_root, DIFF_HEADS * layer + h)
                        nc.tensor.matmul(bank[7][:, :], ones, norm_sq[:, h % 2, :], start=True,
                                         stop=True).then_inc(d_ss, 1)
                for m in range(KT):
                    if m >= 4:
                        pe.wait_ge(x_ready, 8 * r + m - 3)
                    order = [4, 5, 6, 7, 0, 1, 2, 3]
                    s = (n0 + MIX_IN + m) % SLOTS
                    pe.wait_ge(lo_ready, n0 + MIX_IN + m + 1)
                    for i, kt in enumerate(order):
                        if m == 0:
                            pe.wait_ge(o_ready, KT * layer + i + 1)
                        ins = pe_three(bank[m % 4][:, :], w_hi[:, s, P * kt:P * kt + P], w_lo[:, s, P * kt:P * kt + P],
                                    o_hi[:, kt, :], o_lo[:, kt, :], i == 0, i == 7)
                    ins.then_inc(unit_used, 1)

            def turn_v(layer, j):
                pe.wait_ge(in_evac, MIX_IN * layer + 17 + j + 1)
                if j >= 2:
                    pe.wait_ge(v_ready, 8 * layer + j - 1)
                for b in range(TB):
                    ins = nc.tensor.transpose(bank[4 + j % 2][:, P * b:P * b + P], tmp[:, j % 2, P * b:P * b + P],
                                              identity)
                ins.then_inc(v_turned, 1)

            def scores(layer, k):
                kind, h, b = STEPS[k]
                width = P * (b + 1)
                if k == 0:
                    pe.wait_ge(qk_ready, 8 * (layer + 1))
                    pe.wait_ge(in_evac, MIX_IN * (layer + 1))
                    pe.wait_ge(cum_ready, layer + 1)
                    pe.wait_ge(v_ready, 8 * (layer + 1))
                for c in range(2 if kind == "d" else 1):
                    e = FIRST_EXP[k] + c
                    if e >= 4:
                        pe.wait_ge(exped, NEXP * layer + e - 3)
                    dst = bank[e % 4]
                    lo = HEAD * (c if kind == "d" else h % 2)
                    rows = slice(lo, lo + HEAD)
                    q, kk, t = (dq, dk, h) if kind == "d" else (fq, fk, h // 2)
                    nc.tensor.matmul(dst[:, 0:width], q[rows, t, P * b:P * b + P], kk[rows, t, 0:width],
                                     start=True, stop=False)
                    if kind == "f":
                        at = TAB["select"] + P * h
                        nc.tensor.matmul(dst[:, 0:width], tab[0:8, at:at + P], negcum[:, 0:width],
                                         start=False, stop=False)
                    nc.tensor.matmul(dst[:, P * b:width], identity, table("causal"), start=False,
                                     stop=True).then_inc(scored, 1)

            def flip(layer, k):
                kind, h, b = STEPS[k]
                pe.wait_ge(weighed, NSTEP * layer + k + 1)
                if k >= 2:
                    pe.wait_ge(flip_out, NSTEP * layer + k - 1)
                for kb in range(b + 1):
                    ins = nc.tensor.transpose(bank[4 + k % 2][:, P * kb:P * kb + P],
                                              probs[:, FIRST_EXP[k] % 4, P * kb:P * kb + P], identity)
                ins.then_inc(flipped, 1)

            def mix(layer, k):
                kind, h, _ = STEPS[k]
                pe.wait_ge(flip_out, NSTEP * layer + k + 1)
                if kind == "d":
                    if h >= 2:
                        pe.wait_ge(d_out, DIFF_HEADS * layer + h - 1)
                    dst, v, lo, n, at = bank[6 + h % 2], dv, P * h, P, 0
                else:
                    pair = h // 2
                    if h % 2 == 0:
                        if pair == 0:
                            pe.wait_ge(d_out, DIFF_HEADS * layer + 3)
                        elif pair == 1:
                            pe.wait_ge(d_root, DIFF_HEADS * (layer + 1))
                        else:
                            pe.wait_ge(o_ready, KT * layer + DIFF_HEADS + pair - 1)
                    dst, v, lo, n, at = bank[6 + pair % 2], fv, HEAD * h, HEAD, HEAD * (h % 2)
                for kb in range(TB):
                    ins = nc.tensor.matmul(dst[at:at + n, P * kb:S], v[:, kb, lo:lo + n],
                                           probs_t[:, head_of[k] % 2, kb, P * kb:S], start=kb == 0,
                                           stop=kb == TB - 1)
                ins.then_inc(mixed, 1)

            pe.wait_ge(consts_in, 32)
            pe.wait_ge(lam_prod, 1)
            nc.tensor.matmul(bank[7][:, 0:4], ones[0:HEAD, :], tmp[0:HEAD, 3, 0:4], start=True,
                             stop=True).then_inc(lam_sum, 1)
            pe.wait_ge(x_in_sem, 16)
            for m in range(KT):
                if m == 7:
                    pe.wait_ge(lam_exp, 1)
                for b in range(TB):
                    ins = nc.tensor.transpose(bank[m][:, P * b:P * b + P], x_tok[:, b, P * m:P * m + P], identity)
                ins.then_inc(x_turned, 1)
            for layer in range(DEPTH):
                n0, r = layer * LAYER_UNITS, 3 * layer
                ffn(2 * layer, r + 1, n0)
                mixer(layer, r + 2, n0 + FFN_UNITS)
                ffn(2 * layer + 1, r + 3, n0 + FFN_UNITS + MIX_UNITS)

        A_EVENTS = [("gates", 0), ("xm", 0), ("xm", 1), ("xm", 2), ("xm", 3), ("qk", 0), ("v", 0), ("xm", 4), ("xm", 5),
                    ("qk", 1), ("v", 1), ("xm", 6), ("xm", 7), ("qk", 2), ("v", 2), ("qk", 3), ("v", 3)]
        A_HEADS_END = len(A_EVENTS)
        A_EVENTS += [("om", t) for t in range(KT)] + [("zm", t) for t in range(KT)]
        A_POOL_AT = len(A_EVENTS)
        A_EVENTS += [("xp", 0), ("xp", 1)]
        for g in range(4):
            if g < 3:
                A_EVENTS += [("xp", 2 * g + 2), ("xp", 2 * g + 3)]
            A_EVENTS += [("pool", g), ("zp", 2 * g), ("zp", 2 * g + 1)]
        A_OUT = A_START + len(A_EVENTS)

        def a_banks(kind, t):
            return {"gates": [0], "xm": [1 + t % 2], "qk": [4, 5, 6, 7], "v": [0, 3], "om": [t % 4], "zm": [t % 4],
                    "xp": [t % 2], "pool": [4, 5], "zp": [2 + t % 2]}[kind]

        def last_user(events, banks_of, i):
            mine = set(banks_of(*events[i]))
            return max((j + 1 for j in range(i) if mine & set(banks_of(*events[j]))), default=0)

        def halves_after(i):
            return {2: 0, 6: 1, 10: 2, 14: 3}.get(i)

        def mix_after(i):
            kind, t = A_EVENTS[i]
            return 0 if (kind, t) == ("xp", 1) else t + 1 if kind == "pool" and t < 3 else None

        xc = place("xc", [P, KT, S], at=R_AT)
        mq = place("mq", [P, KT, S])
        mk = place("mk", [P, KT, S])
        mv = place("mv", [P, TB, D])
        M_AT = here[0]
        xm_hi = place("xm_hi", [P, 2, S], F32R)
        xm_lo = place("xm_lo", [P, 2, S], F32R)
        xc_hi = place("xc_hi", [P, 2, S], F32R)
        xc_lo = place("xc_lo", [P, 2, S], F32R)
        m_rows = place("m_rows", [36, 4, S])
        m_w = place("m_w", [P, 4, S], at=M_AT)
        m_decay = place("m_decay", [P, 2, S])
        m_negm = place("m_negm", [P, 2, S])
        hm = mq
        hsq = place("hsq", [P, 4, S], at=R_AT + 2 * 4 * KT * S)
        h_rstd = place("h_rstd", [P, 4, S])
        ya_hi = place("ya_hi", [P, KT, S], F32R, at=R_AT + 3 * 4 * KT * S)
        ya_lo = place("ya_lo", [P, KT, S], F32R)
        gate_p = place("gate_p", [P, 2, S])
        rot = place("rot", [P, 2, S])
        pos_i = place("pos_i", [P, S], I32, at=here[0] - 4 * S)
        yb_hi = place("yb_hi", [P, KT, S], F32R, at=R_AT)
        yb_lo = place("yb_lo", [P, KT, S], F32R)
        pm_hi = place("pm_hi", [P, 2, S], F32R, at=R_AT + 2 * 4 * KT * S)
        pm_lo = place("pm_lo", [P, 2, S], F32R)
        sums = place("sums", [P, 2, S])
        pooled = place("pooled", [P, 2, S])

        a_evac = sem("a_evac")
        a_act = sem("a_act")
        conv_ready = sem("conv_ready")
        silu_ready = sem("silu_ready")
        op_half, op_ready = sem("op_half"), sem("op_ready")
        m_gate = sem("m_gate")
        m_rows_ready, m_turned, m_cols_ready = sem("m_rows_ready"), sem("m_turned"), sem("m_cols_ready")
        m_bcast, m_negm_ready, m_evac = sem("m_bcast"), sem("m_negm_ready"), sem("m_evac")
        m_scored, m_masked, m_decayed, m_weighed = (sem(n) for n in ("m_scored", "m_masked", "m_decayed", "m_weighed"))
        m_used, m_scaled = sem("m_used"), sem("m_scaled")
        om_ready, hsq_half, hsq_ready = sem("om_ready"), sem("hsq_half"), sem("hsq_ready")
        hss_ready, hroot_ready = sem("hss_ready"), sem("hroot_ready")
        y_prod, y_half, y_ready = sem("y_prod"), sem("y_half"), sem("y_ready")
        pmix_ready, pm_half, pm_ready = sem("pmix_ready"), sem("pm_half"), sem("pm_ready")
        pos_in_sem, rot_step, rot_ready = sem("pos_in_sem"), sem("rot_step"), sem("rot_ready")
        M_STEPS = [(h, b) for h in range(M_HEADS) for b in range(TB)]

        @block.scalar
        def _(act):
            r = 7
            for m in range(KT):
                act_h_tile(r, m)
            act_root(r)
            for i, (kind, t) in enumerate(A_EVENTS[:A_HEADS_END]):
                act_cut(A_START + i + 3)
                if kind == "gates":
                    z, e = m_rows[32:36, 1, :], m_rows[32:36, 2, :]
                    act.wait_ge(m_gate, 1)
                    nc.scalar.activation(e, z, ACT.Abs)
                    act.drain()
                    nc.scalar.activation(e, e, ACT.Exp, scale=-1.0)
                    act.drain()
                    nc.scalar.activation(e, e, ACT.Ln, bias=1.0).then_inc(m_gate, 1)
                if kind == "xm":
                    act.wait_ge(conv_ready, t + 1)
                    nc.scalar.activation(xc[:, t, :], xc[:, t, :], ACT.Silu).then_inc(silu_ready, 1)
                h = halves_after(i)
                if h is not None:
                    act.drain()
                    if h:
                        act.wait_ge(unit_used, A_START + i + 1)
                    for j in range(2):
                        nc.scalar.activation(xm_hi[:, j, :], tmp[:, j, :], ACT.Copy).then_inc(op_half, 1)
                    for j in range(2):
                        nc.scalar.activation(xc_hi[:, j, :], xc[:, 2 * h + j, :], ACT.Copy).then_inc(op_half, 1)
            for k in range(len(M_STEPS) + 1):
                if k < len(M_STEPS):
                    h, b = M_STEPS[k]
                    if b == 0:
                        act.wait_ge(m_bcast, h + 1)
                        if h >= 2:
                            act.wait_ge(m_scaled, h - 1)
                        nc.scalar.activation(m_negm[:, h % 2, :], bank[0][:, :], ACT.Copy)
                        nc.scalar.activation(tmp[:, 2 + h % 2, :], bank[1][:, :], ACT.Exp).then_inc(m_negm_ready, 1)
                    act.wait_ge(m_masked, k + 1)
                    if b == 0:
                        act.drain()
                    if b < TB - 1:
                        nc.scalar.activation(m_decay[:, k % 2, P * (b + 1):S], m_negm[:, h % 2, P * (b + 1):S], ACT.Exp,
                                             bias=m_cols[:, 4 * b + h:4 * b + h + 1])
                    nc.scalar.activation(m_decay[:, k % 2, P * b:P * b + P], m_mask[:, k % 2, :],
                                         ACT.Exp).then_inc(m_decayed, 1)
                if k and k % TB == 0:
                    h = k // TB - 1
                    act.wait_ge(m_used, k)
                    for j in range(2):
                        nc.scalar.activation(hm[:, 2 * h + j, :], bank[4 + j][:, :], ACT.Copy)
                    if h >= 2:
                        act.wait_ge(m_scaled, h - 1)
                    nc.scalar.activation(tmp[:, h % 2, :], bank[6][:, :], ACT.Abs).then_inc(m_evac, 1)
            act.dma_start(pos_i[:, :], pos_in.to_broadcast([P, S])).then_inc(pos_in_sem, 16)
            for i in range(A_HEADS_END, len(A_EVENTS)):
                kind, t = A_EVENTS[i]
                act_cut(A_START + i + 3)
                if kind in ("om", "zm", "zp"):
                    buf = gate_p[:, t % 2, :] if kind == "zp" else tmp[:, t % 2, :]
                    act.wait_ge(a_evac, i + 1)
                    nc.scalar.activation(buf, buf, ACT.Sigmoid if kind == "om" else ACT.Silu).then_inc(a_act, 1)
                if kind == "om":
                    act.wait_ge(om_ready, t + 1)
                    if t % 2 and t > 2:
                        act.wait_ge(hsq_ready, t // 2)
                    nc.scalar.activation(tmp[:, 2, :] if t % 2 else hsq[:, t // 2, :], hm[:, t, :],
                                         ACT.Square).then_inc(hsq_half, 1)
                    if t == KT - 1:
                        for h in range(M_HEADS):
                            act.wait_ge(hss_ready, h + 1)
                            nc.scalar.activation(h_rstd[:, h, :], bank[4 + h][:, :], ACT.Sqrt, scale=1.0 / M_DIM,
                                                 bias=small[:, 1:2]).then_inc(hroot_ready, 1)
                if kind == "zm":
                    act.wait_ge(y_prod, t + 1)
                    nc.scalar.activation(ya_hi[:, t, :], hm[:, t, :], ACT.Copy).then_inc(y_half, 1)
                if kind == "zp":
                    act.wait_ge(y_prod, KT + t + 1)
                    nc.scalar.activation(yb_hi[:, t, :], gate_p[:, t % 2, :], ACT.Copy).then_inc(y_half, 1)
                g = mix_after(i)
                if g is not None:
                    act.wait_ge(pmix_ready, g + 1)
                    if g:
                        act.wait_ge(unit_used, A_START + i + 1)
                    for j in range(2):
                        nc.scalar.activation(pm_hi[:, j, :], tmp[:, 2 + j, :], ACT.Copy).then_inc(pm_half, 1)
            for j in range(2):
                act.wait_ge(rot_step, j + 1)
                nc.scalar.activation(rot[:, j, :], rot[:, j, :], ACT.Sin).then_inc(rot_ready, 1)
            for m in range(KT):
                if m < 7:
                    for j in range(2):
                        act_cut(A_OUT + 2 * m + j + 3)
                act_h_tile(8, m)
            act_cut(A_OUT + 17)
            act_cut(A_OUT + 18)
            act_root(8)

        @block.vector
        def _(dve):
            r = 7
            for m in range(KT + 1):
                if m < KT:
                    nc.vector.scalar_tensor_tensor(out=x[:, m, :], in0=x[:, m, :], scalar=col("final_norm", m),
                                                   in1=rstd[:, :], op0=ALU.mult, op1=ALU.mult).then_inc(x_ready, 1)
                if m >= 1:
                    dve_h_tile(r, m - 1)
            dve_norm(r)

            def halves(h):
                for j in range(4):
                    dve.wait_ge(op_half, 4 * h + j + 1)
                    src, hi, lo = [(tmp[:, j, :], xm_hi, xm_lo), (xc[:, 2 * h + j % 2, :], xc_hi, xc_lo)][j // 2]
                    nc.vector.tensor_tensor(lo[:, j % 2, :], src, hi[:, j % 2, :].bitcast(F32),
                                            ALU.subtract).then_inc(op_ready, 1)

            for i, (kind, t) in enumerate(A_EVENTS[:A_HEADS_END]):
                dve_cut(A_START + i + 3)
                dve.wait_ge(unit_used, A_START + i + 1)
                if kind == "gates":
                    src = bank[0]
                    nc.vector.tensor_tensor(m_rows[0:4, 0, :], src[0:4, :], rstd[0:4, :], ALU.mult)
                    nc.vector.tensor_tensor(m_rows[32:36, 1, :], src[32:36, :], rstd[32:36, :],
                                            ALU.mult).then_inc(a_evac, 1)
                    nc.vector.memset(m_rows[32:36, 3, :], 1.0)
                    dve.drain()
                    for rows, j in ((slice(0, 4), 0), (slice(32, 36), 1)):
                        ins = nc.vector.tensor_scalar(m_rows[rows, j, :], m_rows[rows, j, :], col("b_if", 0, rows),
                                                      None, ALU.add)
                    ins.then_inc(m_gate, 1)
                    dve.wait_ge(m_gate, 2)
                    z, e, f = (m_rows[32:36, j, :] for j in (1, 2, 3))
                    nc.vector.scalar_tensor_tensor(out=z, in0=z, scalar=0.0, in1=e, op0=ALU.min, op1=ALU.subtract)
                    dve.drain()
                    nc.vector.tensor_tensor_scan(e, f, z, 0.0, ALU.mult, ALU.add)
                    nc.vector.memset(m_rows[0:4, 1, :], 0.0)
                    dve.drain()
                    a, zero, big, f = (m_rows[0:4, j, :] for j in range(4))
                    nc.vector.tensor_copy(f, e)
                    dve.drain()
                    nc.vector.tensor_tensor(a, a, f, ALU.subtract)
                    dve.drain()
                    nc.vector.tensor_tensor_scan(big, zero, a, 0.0, ALU.add, ALU.max)
                    dve.drain()
                    nc.vector.tensor_scalar(big, big, -1.0, None, ALU.mult)
                    dve.drain()
                    nc.vector.tensor_tensor(f, big, f, ALU.subtract).then_inc(m_rows_ready, 1)
                elif kind == "xm":
                    if t >= 2:
                        dve.wait_ge(op_ready, 4 * (t // 2))
                    xm, acc = tmp[:, t % 2, :], xc[:, t, :]
                    nc.vector.tensor_tensor(xm, bank[1 + t % 2][:, :], rstd[:, :], ALU.mult).then_inc(a_evac, 1)
                    dve.drain()
                    nc.vector.tensor_scalar(acc, xm, col("conv_w", 8 * (CONV_K - 1) + t), col("conv_b", t), ALU.mult,
                                            ALU.add)
                    for s in range(1, CONV_K):
                        dve.drain()
                        ins = nc.vector.scalar_tensor_tensor(out=acc[:, s:S], in0=xm[:, 0:S - s],
                                                             scalar=col("conv_w", 8 * (CONV_K - 1 - s) + t),
                                                             in1=acc[:, s:S], op0=ALU.mult, op1=ALU.add)
                    ins.then_inc(conv_ready, 1)
                elif kind == "qk":
                    for j in range(2):
                        nc.vector.tensor_copy(mq[:, 2 * t + j, :], bank[4 + j][:, :])
                    for j in range(2):
                        ins = nc.vector.tensor_scalar(mk[:, 2 * t + j, :], bank[6 + j][:, :], M_DIM ** -0.5, None,
                                                      ALU.mult)
                    ins.then_inc(a_evac, 1)
                else:
                    for j in range(2):
                        ins = nc.vector.tensor_copy(mv[:, 2 * j:2 * j + 2, M_DIM * t:M_DIM * (t + 1)],
                                                    bank[3 * j][:, :].rearrange("p (b n) -> p b n", b=2))
                    ins.then_inc(a_evac, 1)
                h = halves_after(i)
                if h is not None:
                    dve.wait_ge(silu_ready, 2 * h + 2)
                    halves(h)
            def m_scale(h):
                dve.wait_ge(m_evac, h + 1)
                den = tmp[:, h % 2, :]
                nc.vector.tensor_tensor(den, den, tmp[:, 2 + h % 2, :], ALU.max)
                dve.drain()
                nc.vector.reciprocal(den, den)
                dve.drain()
                for j in range(2):
                    ins = nc.vector.tensor_tensor(hm[:, 2 * h + j, :], hm[:, 2 * h + j, :], den, ALU.mult)
                ins.then_inc(m_scaled, 1)
                dve.drain()

            dve.wait_ge(m_turned, 1)
            nc.vector.tensor_copy(m_cols[:, :], bank[7][:, 0:16]).then_inc(m_cols_ready, 1)
            dve.wait_ge(m_cols_ready, 1)
            for k, (h, b) in enumerate(M_STEPS):
                dve.wait_ge(m_negm_ready, h + 1)
                dve.drain()
                nc.vector.scalar_tensor_tensor(
                    out=m_mask[:, k % 2, :], in0=m_negm[:, h % 2, P * b:P * b + P],
                    scalar=m_cols[:, 4 * b + h:4 * b + h + 1], in1=table("causal_t"), op0=ALU.add,
                    op1=ALU.add).then_inc(m_masked, 1)
                dve.wait_ge(m_scored, k + 1)
                dve.wait_ge(m_decayed, k + 1)
                if k >= 4:
                    dve.wait_ge(m_used, k - 3)
                nc.vector.tensor_tensor(m_w[:, b, P * b:S], bank[2 + k % 2][:, P * b:S], m_decay[:, k % 2, P * b:S],
                                        ALU.mult).then_inc(m_weighed, 1)
                if b == 1 and h:
                    m_scale(h - 1)
            m_scale(M_HEADS - 1)

            def head_norm(h):
                dve.wait_ge(hroot_ready, h + 1)
                nc.vector.reciprocal(h_rstd[:, h, :], h_rstd[:, h, :])
                dve.drain()
                for t in (2 * h, 2 * h + 1):
                    nc.vector.scalar_tensor_tensor(out=hm[:, t, :], in0=hm[:, t, :], scalar=col("head_norm", t),
                                                   in1=h_rstd[:, h, :], op0=ALU.mult, op1=ALU.mult)
                dve.drain()
                for t in (2 * h, 2 * h + 1):
                    nc.vector.scalar_tensor_tensor(out=hm[:, t, :], in0=xc[:, t, :], scalar=col("skip", t),
                                                   in1=hm[:, t, :], op0=ALU.mult, op1=ALU.add)
                dve.drain()

            done = 0
            for i in range(A_HEADS_END, len(A_EVENTS)):
                kind, t = A_EVENTS[i]
                dve_cut(A_START + i + 3)
                if kind == "zm" and t % 2 == 0:
                    head_norm(t // 2)
                dve.wait_ge(unit_used, A_START + i + 1)
                if kind in ("om", "zm", "zp"):
                    done += 1
                    j = {"om": t % 4, "zm": t % 4, "zp": 2 + t % 2}[kind]
                    buf = gate_p[:, t % 2, :] if kind == "zp" else tmp[:, t % 2, :]
                    dve.drain()
                    nc.vector.tensor_tensor(buf, bank[j][:, :], rstd[:, :], ALU.mult).then_inc(a_evac, 1)
                    dve.wait_ge(a_act, done)
                if kind == "om":
                    nc.vector.tensor_tensor(hm[:, t, :], hm[:, t, :], buf, ALU.mult).then_inc(om_ready, 1)
                    if t % 2:
                        dve.wait_ge(hsq_half, t + 1)
                        nc.vector.tensor_tensor(hsq[:, t // 2, :], hsq[:, t // 2, :], tmp[:, 2, :],
                                                ALU.add).then_inc(hsq_ready, 1)
                if kind == "zm":
                    nc.vector.tensor_tensor(hm[:, t, :], hm[:, t, :], buf, ALU.mult).then_inc(y_prod, 1)
                    dve.wait_ge(y_half, t + 1)
                    nc.vector.tensor_tensor(ya_lo[:, t, :], hm[:, t, :], ya_hi[:, t, :].bitcast(F32),
                                            ALU.subtract).then_inc(y_ready, 1)
                if kind == "zp":
                    nc.vector.tensor_tensor(buf, buf, pooled[:, t % 2, :], ALU.mult).then_inc(y_prod, 1)
                    dve.wait_ge(y_half, KT + t + 1)
                    nc.vector.tensor_tensor(yb_lo[:, t, :], buf, yb_hi[:, t, :].bitcast(F32),
                                            ALU.subtract).then_inc(y_ready, 1)
                if kind == "xp":
                    g, w = t // 2, P_WINDOWS[t // 2]
                    if t % 2 == 0 and t >= 2:
                        dve.wait_ge(pm_ready, 2 * (t // 2))
                    xp = tmp[:, t % 2, :]
                    dve.drain()
                    nc.vector.tensor_tensor(xp, bank[t % 2][:, :], rstd[:, :], ALU.mult).then_inc(a_evac, 1)
                    src, s = xp, 1
                    while s < w:
                        dst = sums[:, (s.bit_length() - 1) % 2, :]
                        dve.drain()
                        nc.vector.tensor_copy(dst[:, 0:s], src[:, 0:s])
                        nc.vector.tensor_tensor(dst[:, s:S], src[:, s:S], src[:, 0:S - s], ALU.add)
                        src, s = dst, 2 * s
                    at = TAB["pool_head"] + 16 * g
                    dve.drain()
                    nc.vector.scalar_tensor_tensor(out=tmp[:, 2 + t % 2, 16:S], in0=src[:, 16:S], scalar=1.0 / w,
                                                   in1=xp[:, 16:S], op0=ALU.mult, op1=ALU.subtract)
                    nc.vector.tensor_tensor(src[:, 0:16], src[:, 0:16], tab[:, at:at + 16], ALU.mult)
                    dve.drain()
                    ins = nc.vector.tensor_tensor(tmp[:, 2 + t % 2, 0:16], src[:, 0:16], xp[:, 0:16], ALU.subtract)
                    if t % 2:
                        ins.then_inc(pmix_ready, 1)
                if kind == "pool":
                    dve.drain()
                    for j in range(2):
                        ins = nc.vector.tensor_scalar(pooled[:, j, :], bank[4 + j][:, :], col("pool_scale", 2 * t + j),
                                                      None, ALU.mult)
                    ins.then_inc(a_evac, 1)
                    dve.drain()
                g = mix_after(i)
                if g is not None:
                    for j in range(2):
                        dve.wait_ge(pm_half, 2 * g + j + 1)
                        nc.vector.tensor_tensor(pm_lo[:, j, :], tmp[:, 2 + j, :], pm_hi[:, j, :].bitcast(F32),
                                                ALU.subtract).then_inc(pm_ready, 1)
            ang, turns = tmp[:, 2, :], tmp[:, 1, :]
            TWO_PI = (6.28125, 0.0019350051879882812, 2 * math.pi - 6.28125 - 0.0019350051879882812)
            ROUND = 1.5 * 2.0 ** 23
            dve.wait_ge(pos_in_sem, 16)
            dve.drain()
            nc.vector.tensor_copy(ang, pos_i[:, :])
            dve.drain()
            nc.vector.tensor_scalar(ang, ang, col("inv_freq"), None, ALU.mult)
            for j in range(2):
                quarter = 0.25 * (1 - j)
                dve.drain()
                nc.vector.tensor_scalar(turns, ang, 0.5 / math.pi, quarter, ALU.mult, ALU.add)
                dve.drain()
                nc.vector.tensor_scalar(turns, turns, ROUND, None, ALU.add)
                dve.drain()
                nc.vector.tensor_scalar(turns, turns, -ROUND, None, ALU.add)
                src = ang
                for part in TWO_PI:
                    dve.drain()
                    nc.vector.scalar_tensor_tensor(out=rot[:, j, :], in0=turns, scalar=-part, in1=src, op0=ALU.mult,
                                                   op1=ALU.add)
                    src = rot[:, j, :]
                dve.drain()
                if j == 0:
                    nc.vector.tensor_scalar(src, src, math.pi / 2, None, ALU.add)
                    dve.drain()
                nc.vector.tensor_scalar(src, src, 3.1415925, -3.1415925, ALU.min, ALU.max).then_inc(rot_step, 1)
            dve.wait_ge(rot_ready, 2)
            nc.vector.tensor_scalar(rot[:, 1, :], rot[:, 1, :], col("rope_sign"), None, ALU.mult)
            for m in range(KT + 1):
                if m < KT:
                    if m < 7:
                        for j in range(2):
                            dve_cut(A_OUT + 2 * m + j + 3)
                    dve.wait_ge(unit_used, A_OUT + 2 * m + 2)
                    nc.vector.tensor_tensor(x[:, m, :], bank[m % 4][:, :], x[:, m, :], ALU.add).then_inc(x_ready, 1)
                if m >= 1:
                    dve_h_tile(8, m - 1)
            dve_cut(A_OUT + 17)
            dve_cut(A_OUT + 18)
            dve_norm(8)

        @block.tensor
        def _(pe):
            def spread(h):
                at = TAB["select"] + P * h
                if h:
                    pe.wait_ge(m_negm_ready, h)
                for j in range(2):
                    ins = nc.tensor.matmul(bank[j][:, :], tab[0:4, at:at + P], m_rows[0:4, 2 + j, :], start=True,
                                           stop=True)
                ins.then_inc(m_bcast, 1)

            def m_scores(k):
                h, b = M_STEPS[k]
                if k >= 2:
                    pe.wait_ge(m_weighed, k - 1)
                for i in range(2):
                    ins = nc.tensor.matmul(bank[2 + k % 2][:, P * b:S], mk[:, 2 * h + i, P * b:P * b + P],
                                           mq[:, 2 * h + i, P * b:S], start=i == 0, stop=i == 1)
                ins.then_inc(m_scored, 1)

            def m_mix(k):
                h, b = M_STEPS[k]
                pe.wait_ge(m_weighed, k + 1)
                if b == 0 and h:
                    pe.wait_ge(m_evac, h)
                w = m_w[:, b, P * b:S]
                for j in range(2):
                    at = M_DIM * h + P * j
                    nc.tensor.matmul(bank[4 + j][:, P * b:S], mv[:, b, at:at + P], w, start=b == 0, stop=b == TB - 1)
                nc.tensor.matmul(bank[6][:, P * b:S], ones, w, start=b == 0, stop=b == TB - 1).then_inc(m_used, 1)

            def attend():
                pe.wait_ge(m_rows_ready, 1)
                pe.wait_ge(a_evac, A_HEADS_END)
                for b in range(TB):
                    ins = nc.tensor.transpose(bank[7][:, 4 * b:4 * b + 4], m_rows[0:4, 0, P * b:P * b + P],
                                              identity[0:4, 0:4])
                ins.then_inc(m_turned, 1)
                spread(0)
                m_scores(0)
                for k, (h, b) in enumerate(M_STEPS):
                    if k + 1 < len(M_STEPS):
                        m_scores(k + 1)
                    if b == 2 and h + 1 < M_HEADS:
                        spread(h + 1)
                    m_mix(k)

            pe_sum_squares(FINAL)
            for i, (kind, t) in enumerate(A_EVENTS):
                n, s = A_START + i, (A_START + i) % SLOTS
                need = last_user(A_EVENTS, a_banks, i)
                if need:
                    pe.wait_ge(a_evac, need)
                banks = [bank[b] for b in a_banks(kind, t)]
                if kind in ("qk", "v"):
                    pe.wait_ge(lo_ready, n + 1)
                    pe.wait_ge(op_ready, 4 * t + 4)
                    if kind == "qk":
                        for j in range(4):
                            for kt in range(2):
                                at = 512 * (j // 2) + M_DIM * kt + P * (j % 2)
                                ins = pe_three(banks[j][:, :], w_hi[:, s, at:at + P], w_lo[:, s, at:at + P],
                                            xc_hi[:, kt, :], xc_lo[:, kt, :], kt == 0, kt == 1)
                    else:
                        for b in range(TB):
                            for kt in range(2):
                                at = M_DIM * kt
                                ins = pe_three(banks[b // 2][:, M_DIM * (b % 2):M_DIM * (b % 2) + M_DIM],
                                            xm_hi[:, kt, P * b:P * b + P], xm_lo[:, kt, P * b:P * b + P],
                                            w_hi[:, s, at:at + M_DIM], w_lo[:, s, at:at + M_DIM], kt == 0, kt == 1)
                    ins.then_inc(unit_used, 1)
                elif kind == "pool":
                    pe.wait_ge(lo_ready, n + 1)
                    pe.wait_ge(pm_ready, 2 * t + 2)
                    for j in range(2):
                        for kt in range(2):
                            at = M_DIM * kt + P * j
                            ins = pe_three(banks[j][:, :], w_hi[:, s, at:at + P], w_lo[:, s, at:at + P], pm_hi[:, kt, :],
                                        pm_lo[:, kt, :], kt == 0, kt == 1)
                    ins.then_inc(unit_used, 1)
                else:
                    pe_unit(n, None, banks[0][:, :], h_hi, h_lo, pe_h_arrive(7) if i == 0 else None)
                if i == 0:
                    pe_sum_squares(7)
                if i == A_HEADS_END - 1:
                    attend()
                if (kind, t) == ("om", KT - 1):
                    for h in range(M_HEADS):
                        pe.wait_ge(hsq_ready, h + 1)
                        nc.tensor.matmul(bank[4 + h][:, :], ones, hsq[:, h, :], start=True,
                                         stop=True).then_inc(hss_ready, 1)

            for m in range(KT):
                if m >= 4:
                    pe.wait_ge(x_ready, 8 * 8 + m - 3)
                for j in range(2):
                    n = A_OUT + 2 * m + j
                    s = n % SLOTS
                    pe.wait_ge(lo_ready, n + 1)
                    if m == 0:
                        pe.wait_ge(y_ready, KT * (j + 1))
                    for kt in range(8):
                        ins = pe_three(bank[m % 4][:, :], w_hi[:, s, P * kt:P * kt + P], w_lo[:, s, P * kt:P * kt + P],
                                    (yb_hi if j else ya_hi)[:, kt, :], (yb_lo if j else ya_lo)[:, kt, :],
                                    j == 0 and kt == 0, j == 1 and kt == 7)
                    ins.then_inc(unit_used, 1)

        C_EVENTS = [("cq", t) for t in range(QT)] + [("ckv", t) for t in range(KVT)] + [("kpe", 0)] + \
                   [("z", t) for t in range(KT)]
        C_Q = C_START + len(C_EVENTS)
        C_KV, C_OUT = C_Q + C_UQ, C_Q + C_UQ + C_UKV
        Q_EVENTS = [("nope", h) for h in range(C_HEADS)] + [("rope", p) for p in range(C_HEADS // 2)]
        C_STEPS = [(h, b) for h in range(C_HEADS) for b in range(TB)]

        zs = place("zs", [P, KT, S], at=R_AT)
        qn = place("qn", [P, C_HEADS, S])
        qr = place("qr", [P, C_HEADS // 2, S])
        kn = place("kn", [P, C_HEADS, S])
        kr = place("kr", [P, C_HEADS // 2, S])
        c_probs = place("c_probs", [P, 4, S])
        ckv_hi = place("ckv_hi", [P, KVT, S], F32R)
        ckv_lo = place("ckv_lo", [P, KVT, S], F32R)
        q_rstd = place("q_rstd", [P, S], at=R_AT + 80 * 1024)
        kv_rstd = place("kv_rstd", [P, S])
        cq_hi = place("cq_hi", [P, QT, S], F32R, at=R_AT + 4 * S * (2 * KT + 4))
        cq_lo = place("cq_lo", [P, QT, S], F32R)
        ckv = place("ckv", [P, KVT, S], at=R_AT + 4 * S * (3 * KT + 4))
        kpe_sq, kpe = c_probs[:, 0, :], c_probs[:, 1, :]
        cv = place("cv", [P, TB, C_HEADS * P], at=H_AT)
        c_probs_t = place("c_probs_t", [P, 2, TB, S])
        co_hi = place("co_hi", [P, C_HEADS, S], F32R, at=R_AT + 4 * S * KT)
        co_lo = place("co_lo", [P, C_HEADS, S], F32R, at=R_AT + 4 * S * (2 * KT + 4))
        out_tok = place("out_tok", [P, 2, TB, P], at=R_AT + 4 * S * (3 * KT + 8))

        c_evac, c_act = sem("c_evac"), sem("c_act")
        qsum_ready, kvsum_ready, lat_ss, lat_root = (sem(n) for n in ("qsum_ready", "kvsum_ready", "lat_ss", "lat_root"))
        ckv_norm, ckv_half, lat_ready, ckv_ready = (sem(n) for n in ("ckv_norm", "ckv_half", "lat_ready", "ckv_ready"))
        kpe_ready = sem("kpe_ready")
        q_evac, q_act, q_summed, q_root, q_ready = (sem(n) for n in ("q_evac", "q_act", "q_summed", "q_root", "q_ready"))
        k_evac, k_act, k_summed, k_root, k_ready = (sem(n) for n in ("k_evac", "k_act", "k_summed", "k_root", "k_ready"))
        q_total, k_evac_v = sem("q_total"), sem("k_evac_v")
        c_scored, c_maxed, c_exped = sem("c_scored"), sem("c_maxed"), sem("c_exped")
        c_weighed, c_flipped, c_flip_out = sem("c_weighed"), sem("c_flipped"), sem("c_flip_out")
        c_mixed, co_prod, co_half, co_ready = (sem(n) for n in ("c_mixed", "co_prod", "co_half", "co_ready"))
        out_turned, out_copied = sem("out_turned"), sem("out_copied")
        out_done = [sem("out_done0"), sem("out_done1")]

        def c_out(h):
            nc.scalar.wait_ge(co_prod, h + 1)
            nc.scalar.activation(co_hi[:, h, :], tmp[:, h % 2, :], ACT.Copy).then_inc(co_half, 1)

        def c_head(h):
            nc.vector.wait_ge(c_mixed, h + 1)
            nc.vector.drain()
            nc.vector.tensor_tensor(tmp[:, h % 2, :], bank[6 + h % 2][:, :], zs[:, h, :], ALU.mult).then_inc(co_prod, 1)
            nc.vector.wait_ge(co_half, h + 1)
            nc.vector.tensor_tensor(co_lo[:, h, :], tmp[:, h % 2, :], co_hi[:, h, :].bitcast(F32),
                                    ALU.subtract).then_inc(co_ready, 1)

        @block.scalar
        def _(act):
            def swap(dst, src):
                for q in range(4):
                    ins = nc.scalar.activation(dst[32 * q:32 * q + 32, :], src[32 * (q ^ 1):32 * (q ^ 1) + 32, :], ACT.Copy)
                return ins

            for e, (kind, t) in enumerate(C_EVENTS):
                act_cut(C_START + e + 3)
                buf = tmp[:, e % 2, :]
                act.wait_ge(c_evac, e + 1)
                if kind == "cq":
                    nc.scalar.activation(q_rstd[:, :] if t == 0 else tmp[:, 2 + e % 2, :], buf, ACT.Square)
                    nc.scalar.activation(cq_hi[:, t, :], buf, ACT.Copy, scale=col("q_norm", t)).then_inc(c_act, 1)
                elif kind == "ckv":
                    nc.scalar.activation(kv_rstd[:, :] if t == 0 else tmp[:, 2 + e % 2, :], ckv[:, t, :],
                                         ACT.Square).then_inc(c_act, 1)
                elif kind == "kpe":
                    nc.scalar.activation(kpe_sq, buf, ACT.Square)
                    swap(tmp[:, 2 + e % 2, :], kpe).then_inc(c_act, 1)
                else:
                    nc.scalar.activation(zs[:, t, :], buf, ACT.Silu).then_inc(c_act, 1)
                if (kind, t) in (("z", 1), ("z", 2)):
                    j, dst, n = (0, q_rstd, Q_LORA) if t == 1 else (1, kv_rstd, KV_LORA)
                    act.wait_ge(lat_ss, j + 1)
                    nc.scalar.activation(dst[:, :], bank[6 + j][:, :], ACT.Sqrt, scale=1.0 / n,
                                         bias=small[:, 1:2]).then_inc(lat_root, 1)
                if (kind, t) == ("z", 5):
                    for j in range(KVT):
                        act.wait_ge(ckv_norm, j + 1)
                        nc.scalar.activation(ckv_hi[:, j, :], ckv[:, j, :], ACT.Copy).then_inc(ckv_half, 1)
            for e, (kind, t) in enumerate(Q_EVENTS):
                if kind == "nope" and t % 2 == 0:
                    act_cut(C_Q + t // 2 + 3)
                if kind == "rope" and t % 2 == 0:
                    act_cut(C_Q + 4 + t // 2 + 3)
                act.wait_ge(q_evac, e + 1)
                if e >= 2:
                    act.wait_ge(q_summed, e - 1)
                if kind == "nope":
                    nc.scalar.activation(tmp[:, 2 + e % 2, :], qn[:, t, :], ACT.Square).then_inc(q_act, 1)
                else:
                    nc.scalar.activation(tmp[:, 2 + e % 2, :], tmp[:, e % 2, :], ACT.Square)
                    act.drain()
                    swap(tmp[:, e % 2, :], qr[:, t, :]).then_inc(q_act, 1)
            act.wait_ge(q_total, 1)
            nc.scalar.activation(q_scale[:, :], q_scale[:, :], ACT.Sqrt, scale=1.0 / QK_HEAD,
                                 bias=small[:, 1:2]).then_inc(q_root, 1)
            for h in range(C_HEADS):
                if h % 2 == 0:
                    act_cut(C_KV + h // 2 + 3)
                act.wait_ge(k_evac, h + 1)
                nc.scalar.activation(tmp[:, h % 2, :], kn[:, h, :], ACT.Square).then_inc(k_act, 1)
                act.wait_ge(k_summed, h + 1)
                if h >= 2:
                    act.wait_ge(k_ready, h - 1)
                nc.scalar.activation(tmp[:, 2 + h % 2, :], bank[6 + h % 2][:, :], ACT.Sqrt, scale=1.0 / QK_HEAD,
                                     bias=small[:, 1:2]).then_inc(k_root, 1)
            for k in range(len(C_STEPS) + OUT_LAG):
                if k < len(C_STEPS):
                    h, b = C_STEPS[k]
                    width = P * (b + 1)
                    act.wait_ge(c_maxed, k + 1)
                    if k >= 4:
                        act.wait_ge(c_flipped, k - 3)
                    nc.scalar.activation(c_probs[:, k % 4, 0:width], bank[k % 4][:, 0:width], ACT.Exp,
                                         scale=q_scale[:, 8 * b + h:8 * b + h + 1], bias=softstat[:, k, 0:1],
                                         accum_out=softstat[:, k, 1:2]).then_inc(c_exped, 1)
                if 0 <= k - FLIP_LAG < len(C_STEPS):
                    j = k - FLIP_LAG
                    h, b = C_STEPS[j]
                    act.wait_ge(c_flipped, j + 1)
                    if b == 0 and h >= 2:
                        act.wait_ge(c_mixed, h - 1)
                    nc.scalar.activation(c_probs_t[:, h % 2, 0:b + 1, P * b:P * b + P],
                                         bank[4 + j % 2][:, 0:P * (b + 1)].rearrange("p (b n) -> p b n", n=P),
                                         ACT.Copy).then_inc(c_flip_out, 1)
                if k >= OUT_LAG and (k - OUT_LAG) % TB == TB - 1:
                    c_out((k - OUT_LAG) // TB)
            for m in range(KT):
                act_cut(C_OUT + m + 3)
                act.wait_ge(out_turned, m + 1)
                if m >= 2:
                    act.wait_ge(out_done[m % 2], 16 * (m // 2))
                nc.scalar.activation(out_tok[:, m % 2, :, :], bank[4 + m % 2][:, :].rearrange("p (b n) -> p b n", b=TB),
                                     ACT.Copy).then_inc(out_copied, 1)

        @block.sync
        def _(sp):
            for m in range(KT):
                sp.wait_ge(out_copied, m + 1)
                sp.dma_start(out[:, P * m:P * m + P].rearrange("(b p) n -> p b n", p=P),
                             out_tok[:, m % 2, :, :]).then_inc(out_done[m % 2], 16)
            for j in range(2):
                sp.wait_ge(out_done[j], 16 * (KT // 2))

        @block.vector
        def _(dve):
            def rope(dst, src, turned):
                nc.vector.tensor_tensor(dst, src, rot[:, 0, :], ALU.mult)
                nc.vector.tensor_tensor(turned, turned, rot[:, 1, :], ALU.mult)
                dve.drain()
                return nc.vector.tensor_tensor(dst, dst, turned, ALU.add)

            def finish(e):
                kind, t = C_EVENTS[e]
                dve.wait_ge(c_act, e + 1)
                if kind == "cq":
                    nc.vector.scalar_tensor_tensor(out=cq_lo[:, t, :], in0=tmp[:, e % 2, :], scalar=col("q_norm", t),
                                                   in1=cq_hi[:, t, :].bitcast(F32), op0=ALU.mult,
                                                   op1=ALU.subtract).then_inc(lat_ready, 1)
                if kind in ("cq", "ckv") and t:
                    total = q_rstd if kind == "cq" else kv_rstd
                    dve.drain()
                    ins = nc.vector.tensor_tensor(total[:, :], total[:, :], tmp[:, 2 + e % 2, :], ALU.add)
                    if t == (QT if kind == "cq" else KVT) - 1:
                        ins.then_inc(qsum_ready if kind == "cq" else kvsum_ready, 1)
                if kind == "kpe":
                    rope(kpe, kpe, tmp[:, 2 + e % 2, :]).then_inc(kpe_ready, 1)

            for e, (kind, t) in enumerate(C_EVENTS):
                dve_cut(C_START + e + 3)
                dve.wait_ge(unit_used, C_START + e + 1)
                dve.drain()
                dst = ckv[:, t, :] if kind == "ckv" else tmp[:, e % 2, :]
                ins = nc.vector.tensor_tensor(dst, bank[e % 4][:, :], rstd[:, :], ALU.mult)
                if kind == "kpe":
                    dve.drain()
                    ins = nc.vector.tensor_scalar(kpe, tmp[:, e % 2, :], col("kn_rope"), None, ALU.mult)
                ins.then_inc(c_evac, 1)
                if e:
                    finish(e - 1)
                if (kind, t) in (("z", 2), ("z", 3)):
                    j, dst = (0, q_rstd) if t == 2 else (1, kv_rstd)
                    dve.wait_ge(lat_root, j + 1)
                    nc.vector.reciprocal(dst[:, :], dst[:, :])
                if (kind, t) == ("z", 4):
                    dve.drain()
                    for j in range(KVT):
                        nc.vector.scalar_tensor_tensor(out=ckv[:, j, :], in0=ckv[:, j, :], scalar=col("kv_norm", j),
                                                       in1=kv_rstd[:, :], op0=ALU.mult, op1=ALU.mult).then_inc(ckv_norm, 1)
            finish(len(C_EVENTS) - 1)
            for j in range(KVT):
                dve.wait_ge(ckv_half, j + 1)
                nc.vector.tensor_tensor(ckv_lo[:, j, :], ckv[:, j, :], ckv_hi[:, j, :].bitcast(F32),
                                        ALU.subtract).then_inc(ckv_ready, 1)

            def q_finish(e):
                kind, t = Q_EVENTS[e]
                dve.wait_ge(q_act, e + 1)
                dve.drain()
                if kind == "nope":
                    nc.vector.tensor_scalar(qn[:, t, :], qn[:, t, :], col("qn_nope"), None, ALU.mult).then_inc(q_ready, 1)
                else:
                    rope(qr[:, t, :], qr[:, t, :], tmp[:, e % 2, :]).then_inc(q_ready, 1)

            for e, (kind, t) in enumerate(Q_EVENTS):
                if kind == "nope" and t % 2 == 0:
                    dve_cut(C_Q + t // 2 + 3)
                if kind == "rope" and t % 2 == 0:
                    dve_cut(C_Q + 4 + t // 2 + 3)
                dve.wait_ge(unit_used, C_Q + (t // 2 if kind == "nope" else 4 + t // 2) + 1)
                dve.drain()
                dst = qn[:, t, :] if kind == "nope" else tmp[:, e % 2, :]
                ins = nc.vector.tensor_tensor(dst, bank[e % 4][:, :], q_rstd[:, :], ALU.mult)
                if kind == "rope":
                    dve.drain()
                    ins = nc.vector.tensor_scalar(qr[:, t, :], dst, col("qn_rope"), None, ALU.mult)
                ins.then_inc(q_evac, 1)
                if e:
                    q_finish(e - 1)
            q_finish(len(Q_EVENTS) - 1)
            dve.wait_ge(q_summed, len(Q_EVENTS))
            nc.vector.tensor_copy(q_scale[:, :], bank[7][:, 0:32])
            dve.drain()
            nc.vector.tensor_tensor(q_scale[:, :], q_scale[:, :], bank[7][:, 32:64], ALU.add).then_inc(q_total, 1)
            dve.wait_ge(q_root, 1)
            nc.vector.reciprocal(q_scale[:, :], q_scale[:, :])
            dve.drain()
            nc.vector.tensor_scalar(q_scale[:, :], q_scale[:, :], QK_HEAD ** -0.5, None, ALU.mult)

            def k_finish(h):
                dve.wait_ge(k_root, h + 1)
                r = tmp[:, 2 + h % 2, :]
                nc.vector.reciprocal(r, r)
                dve.drain()
                at = slice(QK_ROPE * (h % 2), QK_ROPE * (h % 2) + QK_ROPE)
                nc.vector.tensor_tensor(kr[at, h // 2, :], kpe[at, :], r[at, :], ALU.mult)
                nc.vector.scalar_tensor_tensor(out=kn[:, h, :], in0=kn[:, h, :], scalar=col("kn_nope"), in1=r,
                                               op0=ALU.mult, op1=ALU.mult).then_inc(k_ready, 1)

            for h in range(C_HEADS):
                if h % 2 == 0:
                    dve_cut(C_KV + h // 2 + 3)
                    dve.wait_ge(unit_used, C_KV + h // 2 + 1)
                dve.drain()
                nc.vector.tensor_copy(kn[:, h, :], bank[h % 2][:, :]).then_inc(k_evac, 1)
                j = h % 2
                nc.vector.tensor_copy(cv[:, 2 * j:2 * j + 2, P * (h - j):P * (h - j) + 2 * P],
                                      bank[2 + j][:, :].rearrange("p (b n) -> p b n", b=2)).then_inc(k_evac_v, 1)
                if h:
                    k_finish(h - 1)
            k_finish(C_HEADS - 1)
            dve.drain()
            for k in range(len(C_STEPS) + OUT_LAG):
                if k < len(C_STEPS):
                    h, b = C_STEPS[k]
                    width = P * (b + 1)
                    dve.wait_ge(c_scored, k + 1)
                    nc.vector.tensor_reduce(softstat[:, k, 0:1], bank[k % 4][:, 0:width], AX_X, ALU.max, negate=True)
                    dve.drain()
                    nc.vector.tensor_tensor(softstat[:, k, 0:1], softstat[:, k, 0:1], q_scale[:, 8 * b + h:8 * b + h + 1],
                                            ALU.mult).then_inc(c_maxed, 1)
                if 1 <= k <= len(C_STEPS):
                    width = P * (C_STEPS[k - 1][1] + 1)
                    p = c_probs[:, (k - 1) % 4, 0:width]
                    dve.wait_ge(c_exped, k)
                    nc.vector.reciprocal(softstat[:, k - 1, 2:3], softstat[:, k - 1, 1:2])
                    dve.drain()
                    nc.vector.tensor_scalar(p, p, softstat[:, k - 1, 2:3], None, ALU.mult).then_inc(c_weighed, 1)
                if k >= OUT_LAG and (k - OUT_LAG) % TB == TB - 1:
                    c_head((k - OUT_LAG) // TB)
            for m in range(KT):
                dve_cut(C_OUT + m + 3)
                dve.wait_ge(unit_used, C_OUT + m + 1)
                nc.vector.tensor_tensor(x[:, m, :], bank[m % 4][:, :], x[:, m, :], ALU.add).then_inc(x_ready, 1)

        @block.tensor
        def _(pe):
            three = pe_three
            for e, (kind, t) in enumerate(C_EVENTS):
                if e >= 4:
                    pe.wait_ge(c_evac, e - 3)
                pe_unit(C_START + e, None, bank[e % 4][:, :], h_hi, h_lo, pe_h_arrive(8) if e == 0 else None)
                if e == 0:
                    pe_sum_squares(8)
                if (kind, t) in (("z", 0), ("z", 1)):
                    j, total, ready = (0, q_rstd, qsum_ready) if t == 0 else (1, kv_rstd, kvsum_ready)
                    pe.wait_ge(ready, 1)
                    nc.tensor.matmul(bank[6 + j][:, :], ones, total[:, :], start=True, stop=True).then_inc(lat_ss, 1)

            def q_sums(e):
                kind, t = Q_EVENTS[e]
                pe.wait_ge(q_act, e + 1)
                at, sums_of = (t, ones[:, 0:1]) if kind == "nope" else (32 + 2 * t, table("halves", 2))
                for b in range(TB):
                    ins = nc.tensor.matmul(bank[7][:, at + 8 * b:at + 8 * b + sums_of.shape[1]],
                                           tmp[:, 2 + e % 2, P * b:P * b + P], sums_of, start=True, stop=True)
                ins.then_inc(q_summed, 1)

            pe.wait_ge(lat_ready, QT)
            for e, (kind, t) in enumerate(Q_EVENTS):
                n = C_Q + (t // 2 if kind == "nope" else 4 + t // 2)
                s = n % SLOTS
                if t % 2 == 0:
                    pe.wait_ge(lo_ready, n + 1)
                if e < 4:
                    pe.wait_ge(c_evac, len(C_EVENTS))
                else:
                    pe.wait_ge(q_evac, e - 3)
                for kt in range(QT):
                    at = P * (QT * (t % 2) + kt)
                    ins = three(bank[e % 4][:, :], w_hi[:, s, at:at + P], w_lo[:, s, at:at + P], cq_hi[:, kt, :],
                                cq_lo[:, kt, :], kt == 0, kt == QT - 1)
                if t % 2:
                    ins.then_inc(unit_used, 1)
                if e:
                    q_sums(e - 1)
            q_sums(len(Q_EVENTS) - 1)
            pe.wait_ge(ckv_ready, KVT)
            pe.wait_ge(q_root, 1)
            for u in range(C_UKV):
                n = C_KV + u
                s = n % SLOTS
                pe.wait_ge(lo_ready, n + 1)
                if u == 0:
                    pe.wait_ge(q_evac, len(Q_EVENTS))
                else:
                    pe.wait_ge(k_evac_v, 2 * u)
                for j in range(2):
                    for kt in range(KVT):
                        at = P * (KVT * j + kt)
                        three(bank[j][:, :], w_hi[:, s, at:at + P], w_lo[:, s, at:at + P], ckv_hi[:, kt, :],
                              ckv_lo[:, kt, :], kt == 0, kt == KVT - 1)
                for b in range(TB):
                    for kt in range(KVT):
                        at = 4 * P + 2 * P * kt
                        ins = three(bank[2 + b // 2][:, 2 * P * (b % 2):2 * P * (b % 2) + 2 * P],
                                    ckv_hi[:, kt, P * b:P * b + P], ckv_lo[:, kt, P * b:P * b + P],
                                    w_hi[:, s, at:at + 2 * P], w_lo[:, s, at:at + 2 * P], kt == 0, kt == KVT - 1)
                ins.then_inc(unit_used, 1)
                for h in (2 * u, 2 * u + 1):
                    pe.wait_ge(k_act, h + 1)
                    if h == 0:
                        pe.wait_ge(kpe_ready, 1)
                    if h >= 2:
                        pe.wait_ge(k_root, h - 1)
                    nc.tensor.matmul(bank[6 + h % 2][:, :], ones, tmp[:, h % 2, :], start=True, stop=False)
                    nc.tensor.matmul(bank[6 + h % 2][:, :], ones[0:64, :], kpe_sq[0:64, :], start=False,
                                     stop=True).then_inc(k_summed, 1)
            nstep = len(C_STEPS)
            for k in range(nstep + MIX_LAG):
                if k < nstep:
                    h, b = C_STEPS[k]
                    width = P * (b + 1)
                    dst = bank[k % 4]
                    if k == 0:
                        pe.wait_ge(q_ready, len(Q_EVENTS))
                        pe.wait_ge(k_evac_v, C_HEADS)
                    pe.wait_ge(k_ready, h + 1)
                    if k >= 4:
                        pe.wait_ge(c_exped, k - 3)
                    rows, t = slice(64 * (h % 2), 64 * (h % 2) + 64), h // 2
                    nc.tensor.matmul(dst[:, 0:width], qn[:, h, P * b:P * b + P], kn[:, h, 0:width], start=True, stop=False)
                    nc.tensor.matmul(dst[:, 0:width], qr[rows, t, P * b:P * b + P], kr[rows, t, 0:width], start=False,
                                     stop=False)
                    nc.tensor.matmul(dst[:, P * b:width], identity, table("chunked"), start=False,
                                     stop=True).then_inc(c_scored, 1)
                j = k - FLIP_LAG
                if 0 <= j < nstep:
                    pe.wait_ge(c_weighed, j + 1)
                    if j >= 2:
                        pe.wait_ge(c_flip_out, j - 1)
                    for kb in range(C_STEPS[j][1] + 1):
                        ins = nc.tensor.transpose(bank[4 + j % 2][:, P * kb:P * kb + P], c_probs[:, j % 4, P * kb:P * kb + P],
                                                  identity)
                    ins.then_inc(c_flipped, 1)
                if k >= MIX_LAG and (k - MIX_LAG) % TB == TB - 1:
                    h = (k - MIX_LAG) // TB
                    pe.wait_ge(c_flip_out, k - MIX_LAG + 1)
                    if h >= 2:
                        pe.wait_ge(co_ready, h - 1)
                    elif h == 0:
                        pe.wait_ge(k_root, C_HEADS)
                    for kb in range(TB):
                        ins = nc.tensor.matmul(bank[6 + h % 2][:, P * kb:S], cv[:, kb, P * h:P * h + P],
                                               c_probs_t[:, h % 2, kb, P * kb:S], start=kb == 0, stop=kb == TB - 1)
                    ins.then_inc(c_mixed, 1)

            def turn_out(m):
                pe.wait_ge(x_ready, 8 * 9 + m + 1)
                if m >= 2:
                    pe.wait_ge(out_copied, m - 1)
                for b in range(TB):
                    ins = nc.tensor.transpose(bank[4 + m % 2][:, P * b:P * b + P], x[:, m, P * b:P * b + P], identity)
                ins.then_inc(out_turned, 1)

            for m in range(KT):
                s = (C_OUT + m) % SLOTS
                pe.wait_ge(lo_ready, C_OUT + m + 1)
                if m >= 4:
                    pe.wait_ge(x_ready, 8 * 9 + m - 3)
                for kt in range(C_HEADS):
                    if m == 0:
                        pe.wait_ge(co_ready, kt + 1)
                    ins = three(bank[m % 4][:, :], w_hi[:, s, P * kt:P * kt + P], w_lo[:, s, P * kt:P * kt + P],
                                co_hi[:, kt, :], co_lo[:, kt, :], kt == 0, kt == C_HEADS - 1)
                ins.then_inc(unit_used, 1)
                if m:
                    turn_out(m - 1)
            turn_out(KT - 1)



def _by_column(np, w, start, width=P, pad=P):
    k = w.shape[0] // P
    u = np.zeros((P, k, pad), np.float32)
    u[:, :, :width] = w[:, start:start + width].reshape(k, P, width).transpose(1, 0, 2)
    return u


def _unit(np, *parts):
    u = np.concatenate([p.reshape(P, -1) for p in parts], axis=1)
    if u.shape[1] < UNIT:
        u = np.concatenate([u, np.zeros((P, UNIT - u.shape[1]), np.float32)], axis=1)
    return u


def _second(np, a, add):
    w = a["a_w_in_2"][0]
    cuts = {"xm": 0, "om": 1024, "zm": 2056, "xp": 3080, "zp": 4104}
    gates = np.zeros((D, P), np.float32)
    gates[:, :M_HEADS] = w[:, 2048:2048 + M_HEADS]
    gates[:, 32:32 + M_HEADS] = w[:, 2048 + M_HEADS:2056]

    def x_units(kind, tiles):
        for t in tiles:
            add(_by_column(np, w, cuts[kind] + P * t))

    def qk(h):
        add(*(_by_column(np, a[f"a_w_{k}_2"][0, h], 0, M_DIM, M_DIM) for k in "qk"))

    def v(h):
        add(_by_column(np, a["a_w_v_2"][0, h], 0, M_DIM, M_DIM))

    add(_by_column(np, gates, 0))
    x_units("xm", range(4))
    qk(0), v(0)
    x_units("xm", (4, 5))
    qk(1), v(1)
    x_units("xm", (6, 7))
    qk(2), v(2), qk(3), v(3)
    x_units("om", range(KT))
    x_units("zm", range(KT))
    x_units("xp", (0, 1))
    for g in range(4):
        if g < 3:
            x_units("xp", (2 * g + 2, 2 * g + 3))
        add(_by_column(np, a["a_pool_w_2"][0, g], 0, M_DIM, M_DIM))
        x_units("zp", (2 * g, 2 * g + 1))
    for m in range(KT):
        for j in range(2):
            add(_by_column(np, a["a_w_out_2"][0, D * j:D * j + D], P * m))

    w = a["c_w_in_2"][0]
    for t in range(QT + KVT):
        add(_by_column(np, w, P * t))
    pe = w[:, Q_LORA + KV_LORA:Q_LORA + KV_LORA + QK_ROPE]
    add(_by_column(np, np.concatenate([pe, pe], axis=1), 0))
    for t in range(KT):
        add(_by_column(np, w, Q_LORA + KV_LORA + QK_ROPE + P * t))
    w = a["c_w_uq_2"][0]
    for h in range(0, C_HEADS, 2):
        add(*(_by_column(np, w, QK_HEAD * i) for i in (h, h + 1)))
    for p in (0, 2):
        add(*(np.concatenate([_by_column(np, w, QK_HEAD * i + QK_NOPE, QK_ROPE, QK_ROPE) for i in (2 * j, 2 * j + 1)],
                             axis=2) for j in (p, p + 1)))
    w = a["c_w_ukv_2"][0]
    for h in range(0, C_HEADS, 2):
        vs = np.concatenate([_by_column(np, w, 2 * P * i + P) for i in (h, h + 1)], axis=2)
        add(*(_by_column(np, w, 2 * P * i) for i in (h, h + 1)), vs)
    for m in range(KT):
        add(_by_column(np, a["c_w_out_2"][0], P * m))


def _stream(np, a):
    s = np.zeros((UNITS, P, UNIT), np.float32)
    at = 0

    def add(*parts):
        nonlocal at
        s[at] = _unit(np, *parts)
        at += 1

    def ffn(up, down):
        for j in range(FT):
            add(_by_column(np, up, P * j))
            add(_by_column(np, up, D_FF + P * j))
        for j in range(FT):
            add(down[P * j:P * j + P])

    for l in range(DEPTH):
        ffn(a["ffn1_w_gate_up"][l], a["ffn1_w_down"][l])
        w = a["w_in"][l]
        for start in (1544, 2056, 0, 512):
            for t in range(4):
                add(_by_column(np, w, start + P * t))
        add(_by_column(np, w, 1536, FOX_HEADS))
        for start in (1024, 2568):
            for t in range(4):
                add(_by_column(np, w, start + P * t))
        for m in range(KT):
            add(_by_column(np, a["w_out"][l], P * m))
        ffn(a["ffn2_w_gate_up"][l], a["ffn2_w_down"][l])
    assert at == A_START
    _second(np, a, add)
    return s


def _pack_cols(np, a):
    c = np.zeros((P, NCOLS), np.float32)

    def put(name, v, row=0):
        v = np.asarray(v)
        if v.size >= P:
            n = v.size // P
            c[:, COLS[name]:COLS[name] + n] = v.reshape(n, P).T
        else:
            c[row:row + v.size, COLS[name]] = v

    for l in range(DEPTH):
        for k in ("ffn1_norm", "mix_norm", "ffn2_norm"):
            put(f"{k}{l}", a[k][l])
        put(f"subln{l}", a["diff_subln"][l])
        put(f"forget_bias{l}", a["forget_bias"][l])
        for k in ("q1", "k1", "q2", "k2"):
            put(f"l{k}_{l}", a[f"lambda_{k}"][l])
    put("final_norm", a["final_norm"])
    put("a_norm", a["a_norm_g_2"][0])
    put("conv_w", a["a_conv_w_2"][0])
    put("conv_b", a["a_conv_b_2"][0])
    put("head_norm", a["a_head_norm_g_2"][0])
    put("skip", a["a_skip_2"][0])
    put("pool_scale", a["a_pool_scale_2"][0])
    put("b_if", a["a_b_if_2"][0][:M_HEADS])
    put("b_if", a["a_b_if_2"][0][M_HEADS:], row=32)
    put("c_norm", a["c_norm_g_2"][0])
    put("q_norm", a["c_q_norm_g_2"][0])
    put("kv_norm", a["c_kv_norm_g_2"][0])
    for k in ("qn", "kn"):
        g = a[f"c_{k}_g_2"][0]
        put(f"{k}_nope", g[:QK_NOPE])
        put(f"{k}_rope", np.concatenate([g[QK_NOPE:], g[QK_NOPE:]]))
    f = np.float32(ROPE_THETA) ** (-np.arange(0, QK_ROPE, 2, dtype=np.float32) / np.float32(QK_ROPE))
    put("inv_freq", np.tile(f.astype(np.float32), 4))
    put("rope_sign", np.tile(np.repeat(np.float32([-1.0, 1.0]), 32), 2))
    return c


def _tables(np):
    t = np.zeros((P, NTAB), np.float32)
    i = np.arange(P)
    t[:, 0:P] = np.eye(P)
    t[:, P:2 * P] = 1.0
    for c in range(2):
        t[64 * c:64 * c + 64, TAB["halves"] + c] = 1.0
    t[:, TAB["causal"]:][:, :P] = np.where(i[None, :] <= i[:, None], 0.0, -BIG)
    t[:, TAB["causal_t"]:][:, :P] = np.where(i[None, :] >= i[:, None], 0.0, -BIG)
    t[:, TAB["chunked"]:][:, :P] = np.where(i[None, :] // 64 <= i[:, None] // 64, 0.0, -BIG)
    for h in range(FOX_HEADS):
        t[h, TAB["select"] + P * h:TAB["select"] + P * h + P] = 1.0
    for g, w in enumerate(P_WINDOWS):
        t[:, TAB["pool_head"] + 16 * g:TAB["pool_head"] + 16 * g + 16] = 1.0 / np.minimum(np.arange(16) + 1, w)
    return t


def _rope(np):
    inv = 1.0 / (ROPE_THETA ** (np.arange(0, HEAD, 2, dtype=np.float32) / HEAD))
    ang = np.arange(S, dtype=np.float32)[None, :] * np.tile(inv.astype(np.float32), 4)[:, None]
    sign = np.tile(np.repeat(np.float32([-1.0, 1.0]), 32), 2)[:, None]
    return np.stack([np.cos(ang), np.sin(ang) * sign], axis=1).astype(np.float32)


def kernel(**inputs):
    import numpy as np
    import concourse.bacc as bacc
    from concourse.bass_utils import run_bass_kernel_spmd as run

    a = {k: np.asarray(v) for k, v in inputs.items()}
    arrays = {
        "x": np.ascontiguousarray(a["x"][0]), "stream": _stream(np, a), "cols": _pack_cols(np, a),
        "tables": _tables(np), "rope": _rope(np), "positions": np.ascontiguousarray(a["positions_2"]),
    }
    nc = bacc.Bacc("TRN2", target_bir_lowering=False, num_devices=1)
    args = [nc.dram_tensor(n, v.shape, mybir.dt.from_np(v.dtype), kind="ExternalInput").ap()
            for n, v in arrays.items()]
    out = nc.dram_tensor("out", (S, D), F32, kind="ExternalOutput").ap()
    build(nc, *args, out)
    r = run(nc, [arrays], core_ids=[0])
    return r.results[0]["out"].reshape(1, S, D)
```

```python
import math
from contextlib import ExitStack

import concourse.bass as bass
from concourse import mybir

P = 128
D = 1024
S = 512
KT = D // P
TB = S // P
DEPTH = 2
D_FF = 2816
FT = D_FF // P
FOX_HEADS = 8
DIFF_HEADS = 4
HEAD = 64
M_HEADS = 4
M_DIM = D // M_HEADS
CONV_K = 4
P_WINDOWS = (2, 4, 8, 16)
C_HEADS = 8
QK_NOPE, QK_ROPE = 128, 64
QK_HEAD = QK_NOPE + QK_ROPE
Q_LORA, KV_LORA = 384, 256
QT, KVT = Q_LORA // P, KV_LORA // P
ROPE_THETA = 10000.0
NORM_EPS, RMS_EPS = 1e-5, 1e-6
SLOTS = 4
X_PARTS = 4
START_CUTS = (3, 5, 7)
UNIT = 8 * P
BIG = 1.0e30

F32 = mybir.dt.float32
F32R = mybir.dt.float32r
BF16 = mybir.dt.bfloat16
I32 = mybir.dt.int32
ALU = mybir.AluOpType
ACT = mybir.ActivationFunctionType
AX_X = mybir.AxisListType.X

UP_UNITS, DOWN_UNITS = 2 * FT, FT
FFN_UNITS = UP_UNITS + DOWN_UNITS
MIX_IN = 25
MIX_UNITS = MIX_IN + KT
LAYER_UNITS = 2 * FFN_UNITS + MIX_UNITS
A_START = DEPTH * LAYER_UNITS
A_EVENTS = [("gates", 0), ("xm", 0), ("xm", 1), ("xm", 2), ("xm", 3), ("qk", 0), ("xm", 4), ("v", 0), ("xm", 5),
            ("qk", 1), ("xm", 6), ("v", 1), ("xm", 7), ("qk", 2), ("v", 2), ("qk", 3), ("v", 3)]
A_HEADS_END = len(A_EVENTS)
A_EVENTS += [("om", t) for t in range(KT)]
A_EVENTS += [("zm", 0), ("zm", 1), ("zm", 2), ("xp", 0), ("zm", 3), ("zm", 4), ("xp", 1), ("zm", 5), ("xp", 2), ("zm", 6),
             ("xp", 3), ("pool", 0), ("zm", 7), ("zp", 0), ("zp", 1), ("xp", 4), ("xp", 5), ("pool", 1), ("zp", 2),
             ("xp", 6), ("zp", 3), ("xp", 7), ("pool", 2), ("zp", 4), ("zp", 5), ("pool", 3), ("zp", 6), ("zp", 7)]
A_OUT = A_START + len(A_EVENTS)
C_START = A_OUT + 2 * KT
C_LATENT = [("cq", t) for t in range(QT)] + [("ckv", t) for t in range(KVT)] + [("kpe", 0)]
C_EVENTS = C_LATENT + [("z", 0), ("z", 1), ("q", 0), ("z", 2), ("q", 1), ("z", 3), ("q", 2), ("z", 4), ("q", 3), ("z", 5),
                       ("r", 0), ("z", 6), ("r", 1), ("z", 7)] + [("kv", u) for u in range(C_HEADS // 2)]
C_OUT = C_START + len(C_EVENTS)
UNITS = C_OUT + KT
FINAL = 3 * DEPTH
NORMS = FINAL + 2

COLS = {}


def _columns():
    at = 0
    for name, n in (
        [(f"{k}{l}", 8) for l in range(DEPTH) for k in ("ffn1_norm", "mix_norm", "ffn2_norm")]
        + [(f"{k}{l}", 1) for l in range(DEPTH) for k in ("subln", "forget_bias", "lq1_", "lk1_", "lq2_", "lk2_")]
        + [("final_norm", 8), ("a_norm", 8), ("conv_w", 32), ("conv_b", 8), ("head_norm", 8), ("skip", 8),
           ("pool_scale", 8), ("b_if", 1), ("c_norm", 8), ("q_norm", QT), ("kv_norm", KVT),
           ("qn_nope", 1), ("qn_rope", 1), ("kn_nope", 1), ("kn_rope", 1), ("inv_freq", 1), ("rope_sign", 1)]
    ):
        COLS[name] = at
        at += n
    return at


NCOLS = _columns()
TAB = {"identity": 0, "ones": P, "causal_t": 2 * P, "select": 3 * P, "pool_head": (3 + M_HEADS) * P}
TAB["halves"] = TAB["pool_head"] + 16 * len(P_WINDOWS)
NTAB = TAB["halves"] + 2
TABB = {"identity": 0, "causal": P, "chunked": 2 * P, "select": 3 * P}
NTABB = (3 + FOX_HEADS) * P
CUM_ROWS = (0, 32, 64)


def lambda_init(layer):
    return 0.8 - 0.6 * math.exp(-0.3 * layer)


def count(start, it, step):
    return start if it is None else it * step + start


def build(nc, x_in, stream, cols_in, tab_in, rope_in, pos_in, out):
    with ExitStack() as ctx:
        def sem(name):
            return ctx.enter_context(nc.semaphore(name))

        here = [0]
        arena_bytes = 207 * 1024
        arena = ctx.enter_context(nc.sbuf_tensor("arena", [P, arena_bytes // 4], F32))
        origin = -(-(nc.sbuf_base - arena_bytes) // 32) * 32

        def place(name, shape, dt=F32, at=None):
            size = (2 if dt == BF16 else 4) * math.prod(shape[1:])
            at = -(-here[0] // 32) * 32 if at is None else at
            here[0] = at + size
            assert here[0] <= arena_bytes, (name, here[0])
            return nc.alloc_sbuf_tensor_at(name, shape, dt, offset=origin + at)

        x = place("x", [P, KT, S])
        w_raw = place("w_raw", [P, SLOTS, UNIT])
        w_hi = place("w_hi", [P, SLOTS, UNIT], F32R)
        w_lo = place("w_lo", [P, SLOTS, UNIT], F32R)
        rstd = place("rstd", [P, S])
        sqsum = place("sqsum", [P, S])
        tmp = place("tmp", [P, 4, S])
        cols = place("cols", [P, NCOLS])
        tab = place("tab", [P, NTAB])
        tabb = place("tabb", [P, NTABB], BF16)
        cum_parts = place("cum_parts", [CUM_ROWS[2] + 8, S], BF16)
        lam = place("lam", [P, 8])
        final_gain = place("final_gain", [P, KT])
        small = place("small", [P, 4])
        softstat = place("softstat", [P, 64, 3])
        d_stat = place("d_stat", [P, DIFF_HEADS * TB])
        m_cols = place("m_cols", [P, 4 * TB])
        m_mask = place("m_mask", [P, 2, P])
        q_scale = place("q_scale", [P, C_HEADS * TB])
        H_AT = -(-here[0] // 32) * 32
        h_hi = place("h_hi", [P, KT, S], F32R)
        h_lo = place("h_lo", [P, KT, S], F32R)
        R_AT = here[0]
        hid_hi = place("hid_hi", [P, FT, S], F32R, at=R_AT)
        hid_lo = place("hid_lo", [P, FT, S], F32R)
        x_tok = place("x_tok", [P, TB, D], at=R_AT)
        tab_in_f32 = place("tab_in_f32", [P, NTABB], at=R_AT + 64 * 1024)
        final_sq = place("final_sq", [P, KT, S], at=R_AT)
        dq = place("dq", [P, 4, S], at=R_AT)
        dk = place("dk", [P, 4, S])
        fq = place("fq", [P, 4, S])
        fk = place("fk", [P, 4, S])
        fv = place("fv", [P, TB, S])
        dv = place("dv", [P, TB, S])
        o_hi = place("o_hi", [P, KT, S], F32R)
        o_lo = place("o_lo", [P, KT, S], F32R)
        probs = place("probs", [P, 4, S])
        cos_sin = place("cos_sin", [P, 2, S], at=here[0] - 4 * 4 * S)
        cum_part = place("cum_part", [8, S], BF16, at=R_AT + 80 * 1024 + 4096)
        probs_t = place("probs_t", [P, 2, TB, S], at=H_AT)
        gate_rows = tmp[0:8, 2:4, :]
        negcum = sqsum[0:8, :]

        bank = [ctx.enter_context(nc.psum_tensor(f"bank{b}", [P, S], F32)) for b in range(8)]

        identity = tab[:, 0:P]
        ones = tab[:, P:2 * P]

        def table(name, n=P):
            return tab[:, TAB[name]:TAB[name] + n]

        def table_b(name, n=P, h=0, rows=slice(0, P)):
            return tabb[rows, TABB[name] + n * h:TABB[name] + n * h + n]

        def col(name, i=0, rows=slice(0, P)):
            return cols[rows, COLS[name] + i:COLS[name] + i + 1]

        cols_in_sem, tables_in = sem("cols_in_sem"), sem("tables_in")
        tables_b_in = sem("tables_b_in")
        identity_in = sem("identity_in")
        x_in_sem = [sem(f"x_in{i}") for i in range(X_PARTS)]
        landed = [sem(f"landed{b}") for b in range(SLOTS)]
        hi_ready = sem("hi_ready")
        lo_ready = sem("lo_ready")
        unit_used = sem("unit_used")
        x_ready = sem("x_ready")
        sq_ready = sem("sq_ready")
        sq_added = sem("sq_added")
        h_half = sem("h_half")
        h_ready = sem("h_ready")
        ss_ready = sem("ss_ready")
        sd_ready = sem("sd_ready")
        final_sq_ready, final_ss, final_sum, final_root = (
            sem(n) for n in ("final_sq_ready", "final_ss", "final_sum", "final_root"))
        small_ready = sem("small_ready")
        lam_prod, lam_sum, lam_exp = sem("lam_prod"), sem("lam_sum"), sem("lam_exp")
        x_turned = sem("x_turned")
        up_evac = sem("up_evac")
        gate_silu = sem("gate_silu")
        prod_ready, hid_half, hid_ready = sem("prod_ready"), sem("hid_half"), sem("hid_ready")
        down_done = sem("down_done")
        in_evac = sem("in_evac")
        rope_in_sem = sem("rope_in_sem")
        turned = sem("turned")
        v_turned, v_ready = sem("v_turned"), sem("v_ready")
        g_step = sem("g_step")
        cum_ready, qk_ready = sem("cum_ready"), sem("qk_ready")
        scored, maxed, exped = sem("scored"), sem("maxed"), sem("exped")
        weighed, flipped, flip_out = sem("weighed"), sem("flipped"), sem("flip_out")
        mixed = sem("mixed")
        d_out, d_sq, d_ss, d_root, d_norm = (sem(n) for n in ("d_out", "d_sq", "d_ss", "d_root", "d_norm"))
        d_inverse, d_spread = sem("d_inverse"), sem("d_spread")
        o_half, o_ready = sem("o_half"), sem("o_ready")

        block = ctx.enter_context(nc.Block())
        half_gain = {0: "ffn1_norm0", 1: "mix_norm0", 2: "ffn2_norm0", 3: "ffn1_norm1", 4: "mix_norm1",
                     5: "ffn2_norm1", FINAL + 1: "c_norm"}

        MIX_ORDER = [(k, i) for k in ("dq", "dk", "fq", "fk") for i in range(4)] + [("gates", 0)] + \
                    [(k, i) for k in ("fv", "dv") for i in range(4)]
        STEPS = [("d", h, b) for h in range(DIFF_HEADS) for b in range(TB)] + \
                [("f", h, b) for h in range(FOX_HEADS) for b in range(TB)]
        EXPS = []
        FIRST_EXP = []
        for k, (kind, _, _) in enumerate(STEPS):
            FIRST_EXP.append(len(EXPS))
            EXPS += [(k, c) for c in range(2 if kind == "d" else 1)]
        NSTEP, NEXP = len(STEPS), len(EXPS)
        NHEAD = DIFF_HEADS + FOX_HEADS
        head_of = [h if kind == "d" else DIFF_HEADS + h for kind, h, _ in STEPS]
        FLIP_LAG, MIX_LAG, OUT_LAG = 2, 4, 7
        D_FIRST = TB * DIFF_HEADS + MIX_LAG - 1
        D_SQUARE = {D_FIRST: 0, D_FIRST + 1: 1, D_FIRST + 2: 2, D_FIRST + 4: 3}
        D_ROOT = {D_FIRST + 3: slice(0, 3 * TB), D_FIRST + 5: slice(3 * TB, 4 * TB)}
        D_INVERSE = {k + 1: columns for k, columns in D_ROOT.items()}
        D_SPREAD, D_SCALE, D_HALVES = ({D_FIRST + d + h: h for h in range(DIFF_HEADS)} for d in (6, 7, 8))
        d_bank = (6, 6, 6, 7)

        def x_count(r):
            return KT * (r + (r > FINAL))

        def gain(r, m):
            return final_gain[:, m:m + 1] if r == FINAL else col(half_gain[r], m)

        def act_cut(n, it=None):
            if n >= UNITS:
                return
            s = n % SLOTS
            nc.scalar.wait_ge(landed[s], count(16 * (n // SLOTS + 1), it, 16))
            if n >= SLOTS:
                nc.scalar.wait_ge(unit_used, count(n - SLOTS + 1, it, SLOTS))
            nc.scalar.activation(w_hi[:, s, :], w_raw[:, s, :], ACT.Copy).then_inc(hi_ready, 1)

        def act_h_tile(r, m):
            nc.scalar.wait_ge(x_ready, x_count(r) + m + 1)
            if m >= 2:
                nc.scalar.wait_ge(sq_added, KT * r + m - 1)
            nc.scalar.activation(tmp[:, m % 2, :], x[:, m, :], ACT.Square).then_inc(sq_ready, 1)
            nc.scalar.activation(h_hi[:, m, :], x[:, m, :], ACT.Copy, scale=gain(r, m)).then_inc(h_half, 1)
            if r == FINAL:
                nc.scalar.activation(final_sq[:, m, :], x[:, m, :], ACT.Square,
                                     scale=col("final_norm", m)).then_inc(final_sq_ready, 1)

        def act_root(r):
            nc.scalar.wait_ge(ss_ready, r + 1)
            eps = small[:, 0:1] if r <= FINAL else small[:, 1:2]
            nc.scalar.activation(tmp[:, 2, :], bank[7][:, :], ACT.Sqrt, scale=1.0 / D, bias=eps).then_inc(sd_ready, 1)

        def pool_squares(r):
            for m in range(KT):
                nc.gpsimd.wait_ge(sq_ready, 8 * r + m + 1)
                if m == 0:
                    if r:
                        nc.gpsimd.wait_ge(ss_ready, r)
                    if r in (2, 5):
                        nc.gpsimd.wait_ge(cum_ready, r // 3 + 1)
                    nc.gpsimd.tensor_copy(sqsum[:, :], tmp[:, 0, :]).then_inc(sq_added, 1)
                else:
                    nc.gpsimd.wait_ge(sq_added, 8 * r + m)
                    nc.gpsimd.tensor_tensor(sqsum[:, :], sqsum[:, :], tmp[:, m % 2, :],
                                            ALU.add).then_inc(sq_added, 1)

        def dve_cut(n, it=None):
            if n >= UNITS:
                return
            s = n % SLOTS
            nc.vector.wait_ge(hi_ready, count(n + 1, it, SLOTS))
            nc.vector.tensor_tensor(w_lo[:, s, :], w_raw[:, s, :], w_hi[:, s, :].bitcast(F32),
                                    ALU.subtract).then_inc(lo_ready, 1)

        def dve_h_tile(r, m):
            nc.vector.wait_ge(h_half, KT * r + m + 1)
            nc.vector.scalar_tensor_tensor(out=h_lo[:, m, :], in0=x[:, m, :], scalar=gain(r, m),
                                           in1=h_hi[:, m, :].bitcast(F32), op0=ALU.mult,
                                           op1=ALU.subtract).then_inc(h_ready, 1)

        def dve_norm(r):
            nc.vector.wait_ge(sd_ready, r + 1)
            nc.vector.reciprocal(rstd[:, :], tmp[:, 2, :])
            nc.vector.drain()

        def pe_three(dst, whi, wlo, xhi, xlo, start, stop):
            nc.tensor.matmul(dst, whi, xhi, start=start, stop=False)
            nc.tensor.matmul(dst, whi, xlo, start=False, stop=False)
            return nc.tensor.matmul(dst, wlo, xhi, start=False, stop=stop)

        def pe_unit(n, it, dst, hi, lo, arrive=None):
            s = n % SLOTS
            nc.tensor.wait_ge(lo_ready, count(n + 1, it, SLOTS))
            for kt in range(8):
                if arrive:
                    arrive(kt)
                ins = pe_three(dst, w_hi[:, s, P * kt:P * kt + P], w_lo[:, s, P * kt:P * kt + P],
                            hi[:, kt, :], lo[:, kt, :], kt == 0, kt == 7)
            ins.then_inc(unit_used, 1)

        def pe_h_arrive(r):
            return lambda kt: nc.tensor.wait_ge(h_ready, KT * r + kt + 1)

        def pe_sum_squares(r):
            nc.tensor.wait_ge(sq_added, KT * r + KT)
            nc.tensor.matmul(bank[7][:, :], ones, sqsum[:, :], start=True, stop=True).then_inc(ss_ready, 1)

        @block.sync
        def _(sp):
            sp.dma_start(tab[:, 0:P], tab_in[:, 0:P]).then_inc(identity_in, 16)
            x_rows = x_in.rearrange("(b p) d -> p b d", p=P)
            for i in range(X_PARTS):
                part = slice(D // X_PARTS * i, D // X_PARTS * (i + 1))
                sp.dma_start(x_tok[:, :, part], x_rows[:, :, part]).then_inc(x_in_sem[i], 16)
                if i == 0:
                    sp.dma_start(cols[:, :], cols_in).then_inc(cols_in_sem, 16)
            sp.dma_start(w_raw[:, 0, :], stream[0, :, :]).then_inc(landed[0], 16)
            sp.dma_start(tab[:, P:NTAB], tab_in[:, P:NTAB]).then_inc(tables_in, 16)
            sp.dma_start(tab_in_f32[:, :], tab_in[:, NTAB:]).then_inc(tables_b_in, 16)
            for n in range(1, SLOTS):
                sp.dma_start(w_raw[:, n, :], stream[n, :, :]).then_inc(landed[n], 16)
            with sp.Fori(1, UNITS // SLOTS) as it:
                for s in range(SLOTS):
                    sp.wait_ge(lo_ready, it * SLOTS + (s - SLOTS + 1))
                    sp.dma_start(w_raw[:, s, :], stream[bass.ds(it * SLOTS + s, 1), :, :]
                                 .rearrange("o p n -> p (o n)")).then_inc(landed[s], 16)
            for n in range(UNITS // SLOTS * SLOTS, UNITS):
                sp.wait_ge(lo_ready, n - SLOTS + 1)
                sp.dma_start(w_raw[:, n % SLOTS, :], stream[n, :, :]).then_inc(landed[n % SLOTS], 16)

        @block.gpsimd
        def _(pool):
            for r in range(FINAL + 1):
                pool_squares(r)

        @block.scalar
        def _(act):
            def ffn(f, r, n0):
                def up(c, it):
                    act_cut(n0 + c + 3, it)
                    j = 22 * f + c // 2 + 1
                    if c % 2 == 0:
                        act.wait_ge(up_evac, count(4 + UP_UNITS * f + c + 1, it, 4))
                        nc.scalar.activation(tmp[:, 1, :], tmp[:, 0, :], ACT.Silu).then_inc(gate_silu, 1)
                    else:
                        act.wait_ge(prod_ready, count(j, it, 2))
                        dst = hid_hi[:, c // 2, :] if it is None else \
                            hid_hi[:, bass.ds(it * 2 + c // 2, 1), :].rearrange("p o n -> p (o n)")
                        nc.scalar.activation(dst, tmp[:, 3, :], ACT.Copy).then_inc(hid_half, 1)

                for c in range(4):
                    up(c, None)
                with act.Fori(1, FT // 2) as it:
                    for c in range(4):
                        up(c, it)
                n0 += UP_UNITS
                with act.Fori(0, 4) as it:
                    for c in range(4):
                        act_cut(n0 + c + 3, it)
                for j in range(16, 20):
                    act_cut(n0 + j + 3)
                for m in range(KT):
                    act_h_tile(r, m)
                act_cut(n0 + 23)
                act_cut(n0 + 24)
                if r != FINAL:
                    act_root(r)

            def mixer(layer, r, n0):
                act.dma_start(cos_sin[:, :, :], rope_in).then_inc(rope_in_sem, 16)
                for i, (kind, t) in enumerate(MIX_ORDER + [("", 0)]):
                    if i < MIX_IN:
                        act_cut(n0 + i + 3)
                    if 1 <= i <= 8:
                        b = i - 1
                        act.wait_ge(in_evac, MIX_IN * layer + b + 1)
                        for q in range(4):
                            ins = nc.scalar.activation(tmp[32 * q:32 * q + 32, 2 + b % 2, :],
                                                       tmp[32 * (q ^ 1):32 * (q ^ 1) + 32, b % 2, :], ACT.Copy)
                        ins.then_inc(turned, 1)
                    if kind == "gates":
                        act.wait_ge(g_step, 2 * layer + 1)
                        nc.scalar.activation(gate_rows[:, 1, :], gate_rows[:, 0, :], ACT.Abs)
                        act.drain()
                        nc.scalar.activation(gate_rows[:, 1, :], gate_rows[:, 1, :], ACT.Exp, scale=-1.0)
                        act.drain()
                        nc.scalar.activation(gate_rows[:, 1, :], gate_rows[:, 1, :], ACT.Ln,
                                             bias=1.0).then_inc(g_step, 1)
                    j = i - 18
                    if 0 <= j < 8:
                        act.wait_ge(v_turned, 8 * layer + j + 1)
                        v = (fv if j < 4 else dv)[:, :, P * (j % 4):P * (j % 4) + P]
                        nc.scalar.activation(v, bank[4 + j % 2][:, :].rearrange("p (b n) -> p b n", b=TB),
                                             ACT.Copy).then_inc(v_ready, 1)
                for k in range(NSTEP + OUT_LAG):
                    if k < NSTEP:
                        width = P * (STEPS[k][2] + 1)
                        for e in range(FIRST_EXP[k], FIRST_EXP[k] + (2 if STEPS[k][0] == "d" else 1)):
                            act.wait_ge(maxed, NEXP * layer + e + 1)
                            if e >= 4:
                                act.wait_ge(flipped, NSTEP * layer + EXPS[e - 4][0] + 1)
                            nc.scalar.activation(probs[:, e % 4, 0:width], bank[e % 4][:, 0:width], ACT.Exp,
                                                 bias=softstat[:, e, 0:1],
                                                 accum_out=softstat[:, e, 1:2]).then_inc(exped, 1)
                    if 0 <= k - FLIP_LAG < NSTEP:
                        j = k - FLIP_LAG
                        b, hh = STEPS[j][2], head_of[j]
                        act.wait_ge(flipped, NSTEP * layer + j + 1)
                        if b == 0 and hh >= 2:
                            act.wait_ge(mixed, NHEAD * layer + hh - 1)
                        nc.scalar.activation(probs_t[:, hh % 2, 0:b + 1, P * b:P * b + P],
                                             bank[4 + j % 2][:, 0:P * (b + 1)].rearrange("p (b n) -> p b n", n=P),
                                             ACT.Copy).then_inc(flip_out, 1)
                    if k in D_SQUARE:
                        h = D_SQUARE[k]
                        act.wait_ge(d_out, DIFF_HEADS * layer + h + 1)
                        nc.scalar.activation(dk[:, h, :], dq[:, h, :], ACT.Square).then_inc(d_sq, 1)
                    if k in D_ROOT:
                        c = D_ROOT[k]
                        act.wait_ge(d_ss, DIFF_HEADS * layer + c.stop // TB)
                        nc.scalar.activation(d_stat[:, c], bank[d_bank[c.stop // TB - 1]][:, c], ACT.Sqrt, scale=1.0 / P,
                                             bias=small[:, 0:1]).then_inc(d_root, 1)
                    if k in D_HALVES:
                        h = D_HALVES[k]
                        act.wait_ge(d_norm, DIFF_HEADS * layer + h + 1)
                        nc.scalar.activation(o_hi[:, 4 + h, :], dq[:, h, :], ACT.Copy).then_inc(o_half, 1)
                    j = k - OUT_LAG
                    if j >= 0 and STEPS[j][0] == "f" and STEPS[j][2] == TB - 1 and STEPS[j][1] % 2:
                        pair = STEPS[j][1] // 2
                        act.wait_ge(mixed, NHEAD * layer + DIFF_HEADS + 2 * pair + 2)
                        nc.scalar.activation(o_hi[:, pair, :], bank[6 + pair % 2][:, :], ACT.Copy).then_inc(o_half, 1)
                for m in range(KT):
                    if m < 6:
                        act_cut(n0 + MIX_IN + m + 3)
                    act_h_tile(r, m)
                for n in range(6, 8):
                    act_cut(n0 + MIX_IN + n + 3)
                act_root(r)

            act.wait_ge(cols_in_sem, 16)
            act.wait_ge(small_ready, 1)
            for m in range(KT):
                act_h_tile(0, m)
                if m in START_CUTS:
                    act_cut(START_CUTS.index(m))
            act_root(0)
            act.wait_ge(lam_sum, 1)
            nc.scalar.activation(lam[:, 0:4], bank[6][:, 0:4], ACT.Exp).then_inc(lam_exp, 1)
            for layer in range(DEPTH):
                n0, r = layer * LAYER_UNITS, 3 * layer
                ffn(2 * layer, r + 1, n0)
                mixer(layer, r + 2, n0 + FFN_UNITS)
                ffn(2 * layer + 1, r + 3, n0 + FFN_UNITS + MIX_UNITS)

        @block.vector
        def _(dve):
            def residual(r, wait_tile, scale):
                for m in range(KT + 1):
                    if m < KT:
                        wait_tile(m)
                        nc.vector.scalar_tensor_tensor(out=x[:, m, :], in0=bank[m][:, :], scalar=scale, in1=x[:, m, :],
                                                       op0=ALU.mult, op1=ALU.add).then_inc(x_ready, 1)
                    if m >= 1:
                        dve_h_tile(r, m - 1)

            def ffn(f, r, n0):
                with dve.Fori(0, FT // 2) as it:
                    for c in range(4):
                        dve_cut(n0 + c + 3, it)
                        dve.wait_ge(unit_used, count(n0 + c + 1, it, SLOTS))
                        nc.vector.tensor_tensor(tmp[:, 2 * (c % 2), :], bank[c][:, :], rstd[:, :],
                                                ALU.mult).then_inc(up_evac, 1)
                        if c % 2:
                            j = 22 * f + c // 2 + 1
                            dve.drain()
                            dve.wait_ge(gate_silu, count(j, it, 2))
                            nc.vector.tensor_tensor(tmp[:, 3, :], tmp[:, 1, :], tmp[:, 2, :],
                                                    ALU.mult).then_inc(prod_ready, 1)
                            dve.wait_ge(hid_half, count(j, it, 2))
                            tile = bass.ds(it * 2 + c // 2, 1)
                            nc.vector.tensor_tensor(
                                hid_lo[:, tile, :].rearrange("p o n -> p (o n)"), tmp[:, 3, :],
                                hid_hi[:, tile, :].rearrange("p o n -> p (o n)").bitcast(F32),
                                ALU.subtract).then_inc(hid_ready, 1)
                n0 += UP_UNITS
                with dve.Fori(0, 4) as it:
                    for c in range(4):
                        dve_cut(n0 + c + 3, it)
                for j in range(16, 20):
                    dve_cut(n0 + j + 3)
                residual(r, lambda m: dve.wait_ge(down_done, 7 * f + m + 1) if m < 7
                         else dve.wait_ge(unit_used, n0 + DOWN_UNITS), 0.5)
                dve_cut(n0 + 23)
                dve_cut(n0 + 24)
                if r != FINAL:
                    dve_norm(r)

            def rope(layer, b):
                dst = (dq if b < 4 else dk)[:, b % 4, :]
                dve.wait_ge(turned, 8 * layer + b + 1)
                nc.vector.tensor_tensor(dst, tmp[:, b % 2, :], cos_sin[:, 0, :], ALU.mult)
                nc.vector.tensor_tensor(tmp[:, 2 + b % 2, :], tmp[:, 2 + b % 2, :], cos_sin[:, 1, :], ALU.mult)
                dve.drain()
                nc.vector.tensor_tensor(dst, dst, tmp[:, 2 + b % 2, :], ALU.add).then_inc(qk_ready, 1)

            def mixer(layer, r, n0):
                for i, (kind, t) in enumerate(MIX_ORDER):
                    dve_cut(n0 + i + 3)
                    dve.wait_ge(unit_used, n0 + i + 1)
                    src = bank[i % 4]
                    if kind in ("dq", "dk"):
                        if i == 0:
                            dve.wait_ge(rope_in_sem, 16 * (layer + 1))
                        nc.vector.scalar_tensor_tensor(
                            out=tmp[:, i % 2, :], in0=src[:, :], scalar=HEAD ** -0.5 if kind == "dq" else 1.0,
                            in1=rstd[:, :], op0=ALU.mult, op1=ALU.mult).then_inc(in_evac, 1)
                    elif kind in ("fq", "fk"):
                        nc.vector.scalar_tensor_tensor(
                            out=(fq if kind == "fq" else fk)[:, t, :], in0=src[:, :],
                            scalar=HEAD ** -0.5 if kind == "fq" else 1.0, in1=rstd[:, :], op0=ALU.mult,
                            op1=ALU.mult).then_inc(in_evac, 1)
                    elif kind == "gates":
                        nc.vector.tensor_tensor(gate_rows[:, 0, :], src[0:8, :], rstd[0:8, :],
                                                ALU.mult).then_inc(in_evac, 1)
                        nc.vector.memset(tmp[0:8, 1, :], 1.0)
                        dve.drain()
                        nc.vector.tensor_scalar(gate_rows[:, 0, :], gate_rows[:, 0, :],
                                                col(f"forget_bias{layer}", 0, slice(0, 8)), None,
                                                ALU.add).then_inc(g_step, 1)
                        dve.wait_ge(g_step, 2 * layer + 2)
                        nc.vector.scalar_tensor_tensor(out=gate_rows[:, 0, :], in0=gate_rows[:, 0, :], scalar=0.0,
                                                       in1=gate_rows[:, 1, :], op0=ALU.min, op1=ALU.subtract)
                        dve.drain()
                        nc.vector.tensor_tensor_scan(negcum, tmp[0:8, 1, :], gate_rows[:, 0, :], 0.0, ALU.mult,
                                                     ALU.subtract)
                        for i_part, row in enumerate(CUM_ROWS):
                            dve.drain()
                            ins = nc.vector.tensor_copy(cum_parts[row:row + 8, :], negcum)
                            if i_part < 2:
                                nc.vector.tensor_copy(cum_part[:, :], negcum)
                                dve.drain()
                                nc.vector.tensor_tensor(negcum, negcum, cum_part[:, :], ALU.subtract)
                        ins.then_inc(cum_ready, 1)
                    else:
                        j = i - 17
                        if j == 0:
                            dve.wait_ge(cum_ready, layer + 1)
                        if j >= 2:
                            dve.wait_ge(v_turned, 8 * layer + j - 1)
                        nc.vector.tensor_tensor(tmp[:, j % 2, :], src[:, :], rstd[:, :],
                                                ALU.mult).then_inc(in_evac, 1)
                    if 1 <= i <= 8:
                        rope(layer, i - 1)
                for k in range(NSTEP + OUT_LAG):
                    if k < NSTEP:
                        width = P * (STEPS[k][2] + 1)
                        for e in range(FIRST_EXP[k], FIRST_EXP[k] + (2 if STEPS[k][0] == "d" else 1)):
                            dve.wait_ge(scored, NEXP * layer + e + 1)
                            nc.vector.tensor_reduce(softstat[:, e, 0:1], bank[e % 4][:, 0:width], AX_X, ALU.max,
                                                    negate=True).then_inc(maxed, 1)
                    if 1 <= k <= NSTEP:
                        weigh(layer, k - 1)
                    if k in D_INVERSE:
                        dve.wait_ge(d_root, 2 * layer + 1 + (D_INVERSE[k].start > 0))
                        nc.vector.reciprocal(d_stat[:, D_INVERSE[k]], d_stat[:, D_INVERSE[k]]).then_inc(d_inverse, 1)
                    if k in D_SCALE:
                        h = D_SCALE[k]
                        dve.wait_ge(d_spread, DIFF_HEADS * layer + h + 1)
                        nc.vector.scalar_tensor_tensor(
                            out=dq[:, h, :], in0=dq[:, h, :], scalar=lam[:, 6 + layer:7 + layer], in1=bank[7][:, :],
                            op0=ALU.mult, op1=ALU.mult).then_inc(d_norm, 1)
                    if k in D_HALVES:
                        h = D_HALVES[k]
                        dve.wait_ge(o_half, KT * layer + h + 1)
                        nc.vector.tensor_tensor(o_lo[:, 4 + h, :], dq[:, h, :], o_hi[:, 4 + h, :].bitcast(F32),
                                                ALU.subtract).then_inc(o_ready, 1)
                    if k >= OUT_LAG and STEPS[k - OUT_LAG][2] == TB - 1:
                        head_out(layer, k - OUT_LAG)
                for m in range(KT + 1):
                    if m < KT:
                        if m < 6:
                            dve_cut(n0 + MIX_IN + m + 3)
                        dve.wait_ge(unit_used, n0 + MIX_IN + m + 1)
                        nc.vector.scalar_tensor_tensor(out=x[:, m, :], in0=bank[m % 4][:, :], scalar=1.0,
                                                       in1=x[:, m, :], op0=ALU.mult, op1=ALU.add).then_inc(x_ready, 1)
                    if m >= 1:
                        dve_h_tile(r, m - 1)
                for n in range(6, 8):
                    dve_cut(n0 + MIX_IN + n + 3)
                dve_norm(r)

            def weigh(layer, k):
                kind, h, b = STEPS[k]
                width, e = P * (b + 1), FIRST_EXP[k]
                dve.wait_ge(exped, NEXP * layer + e + (2 if kind == "d" else 1))
                if kind == "f":
                    nc.vector.reciprocal(softstat[:, e, 2:3], softstat[:, e, 1:2])
                    dve.drain()
                    nc.vector.tensor_scalar(probs[:, e % 4, 0:width], probs[:, e % 4, 0:width],
                                            softstat[:, e, 2:3], None, ALU.mult).then_inc(weighed, 1)
                else:
                    nc.vector.reciprocal(softstat[:, e:e + 2, 2], softstat[:, e:e + 2, 1])
                    dve.drain()
                    p0, p1 = probs[:, e % 4, 0:width], probs[:, (e + 1) % 4, 0:width]
                    nc.vector.tensor_scalar(p1, p1, softstat[:, e + 1, 2:3], lam[:, 4 + layer:5 + layer],
                                            ALU.mult, ALU.mult)
                    dve.drain()
                    nc.vector.scalar_tensor_tensor(out=p0, in0=p0, scalar=softstat[:, e, 2:3], in1=p1,
                                                   op0=ALU.mult, op1=ALU.subtract).then_inc(weighed, 1)

            def head_out(layer, k):
                kind, h, _ = STEPS[k]
                if kind == "d":
                    dve.wait_ge(mixed, NHEAD * layer + h + 1)
                    nc.vector.tensor_copy(dq[:, h, :], bank[6 + h % 2][:, :]).then_inc(d_out, 1)
                elif h % 2:
                    pair = h // 2
                    dve.wait_ge(o_half, KT * layer + DIFF_HEADS + pair + 1)
                    nc.vector.tensor_tensor(o_lo[:, pair, :], bank[6 + pair % 2][:, :],
                                            o_hi[:, pair, :].bitcast(F32), ALU.subtract).then_inc(o_ready, 1)

            dve.sem_inc(up_evac, 4)
            nc.vector.memset(small[:, 0:1], NORM_EPS)
            nc.vector.memset(small[:, 1:2], RMS_EPS)
            nc.vector.memset(small[:, 2:3], NORM_EPS * RMS_EPS).then_inc(small_ready, 1)
            dve.wait_ge(cols_in_sem, 16)
            for m in range(KT + 1):
                if m < KT:
                    dve.wait_ge(x_turned, m + 1)
                    nc.vector.tensor_copy(x[:, m, :], bank[m][:, :]).then_inc(x_ready, 1)
                if m >= 1:
                    dve_h_tile(0, m - 1)
                    if m - 1 in START_CUTS:
                        dve_cut(START_CUTS.index(m - 1))
            dve.wait_ge(tables_b_in, 16)
            nc.vector.tensor_copy(tabb[:, :], tab_in_f32[:, :])
            nc.vector.memset(cum_parts[:, :], 0.0)
            at, a_at = COLS["final_norm"], COLS["a_norm"]
            nc.vector.tensor_tensor(final_gain[:, :], cols[:, at:at + KT], cols[:, a_at:a_at + KT], ALU.mult)
            for layer in range(DEPTH):
                for i in range(2):
                    ins = nc.vector.tensor_tensor(tmp[0:HEAD, 3, 2 * layer + i:2 * layer + i + 1],
                                                  col(f"lq{i + 1}_{layer}", 0, slice(0, HEAD)),
                                                  col(f"lk{i + 1}_{layer}", 0, slice(0, HEAD)), ALU.mult)
            ins.then_inc(lam_prod, 1)
            dve_norm(0)
            dve.wait_ge(lam_exp, 1)
            for layer in range(DEPTH):
                nc.vector.scalar_tensor_tensor(out=lam[:, 4 + layer:5 + layer], in0=lam[:, 2 * layer:2 * layer + 1],
                                               scalar=lambda_init(layer), in1=lam[:, 2 * layer + 1:2 * layer + 2],
                                               op0=ALU.add, op1=ALU.subtract)
                nc.vector.tensor_scalar(lam[:, 6 + layer:7 + layer], col(f"subln{layer}"),
                                        1.0 - lambda_init(layer), None, ALU.mult)
            dve.drain()
            for layer in range(DEPTH):
                n0, r = layer * LAYER_UNITS, 3 * layer
                ffn(2 * layer, r + 1, n0)
                mixer(layer, r + 2, n0 + FFN_UNITS)
                ffn(2 * layer + 1, r + 3, n0 + FFN_UNITS + MIX_UNITS)

        @block.tensor
        def _(pe):
            def ffn(f, r, n0):
                def up(c, it, arrive=None):
                    pe.wait_ge(up_evac, count(UP_UNITS * f + c + 1, it, 4))
                    pe_unit(n0 + c, it, bank[c][:, :], h_hi, h_lo, arrive)

                if r == 1:
                    pe.wait_ge(tables_in, 16)
                up(0, None, pe_h_arrive(r - 1))
                if r == 1:
                    pe.wait_ge(lam_prod, 1)
                    nc.tensor.matmul(bank[6][:, 0:4], ones[0:HEAD, :], tmp[0:HEAD, 3, 0:4], start=True,
                                     stop=True).then_inc(lam_sum, 1)
                pe_sum_squares(r - 1)
                for c in range(1, 4):
                    up(c, None)
                with pe.Fori(1, FT // 2) as it:
                    for c in range(4):
                        up(c, it)
                n0 += UP_UNITS

                def down(j, it, order, tile):
                    s = (n0 + j) % SLOTS
                    pe.wait_ge(lo_ready, count(n0 + j + 1, it, SLOTS))
                    pe.wait_ge(hid_ready, count(FT * f + j + 1, it, 4))
                    for m in order:
                        if j == 0 and m < 4:
                            pe.wait_ge(up_evac, UP_UNITS * (f + 1) + m + 1)
                        ins = pe_three(bank[m][:, :], w_hi[:, s, P * m:P * m + P], w_lo[:, s, P * m:P * m + P],
                                    hid_hi[:, tile, :], hid_lo[:, tile, :], j == 0 and it is None, False)
                    ins.then_inc(unit_used, 1)

                for j in range(4):
                    down(j, None, (4, 5, 6, 7, 0, 1, 2, 3), j)
                with pe.Fori(0, 3) as it:
                    for c in range(4):
                        s = (n0 + c) % SLOTS
                        pe.wait_ge(lo_ready, count(n0 + 4 + c + 1, it, SLOTS))
                        pe.wait_ge(hid_ready, count(FT * f + 4 + c + 1, it, 4))
                        tile = bass.ds(it * 4 + (4 + c), 1)
                        xhi = hid_hi[:, tile, :].rearrange("p o n -> p (o n)")
                        xlo = hid_lo[:, tile, :].rearrange("p o n -> p (o n)")
                        for m in range(8):
                            ins = pe_three(bank[m][:, :], w_hi[:, s, P * m:P * m + P], w_lo[:, s, P * m:P * m + P],
                                        xhi, xlo, False, False)
                        ins.then_inc(unit_used, 1)
                for j in range(16, 19):
                    down(j, None, range(8), j)
                pe.wait_ge(lo_ready, n0 + FT)
                pe.wait_ge(hid_ready, FT * (f + 1))
                for m in range(8):
                    for j in range(19, 22):
                        s = (n0 + j) % SLOTS
                        ins = pe_three(bank[m][:, :], w_hi[:, s, P * m:P * m + P], w_lo[:, s, P * m:P * m + P],
                                    hid_hi[:, j, :], hid_lo[:, j, :], False, j == 21)
                        if m == 7:
                            ins.then_inc(unit_used, 1)
                    if m < 7:
                        ins.then_inc(down_done, 1)

            def mixer(layer, r, n0):
                for i, (kind, t) in enumerate(MIX_ORDER):
                    if i >= 4:
                        pe.wait_ge(in_evac, MIX_IN * layer + i - 3)
                    pe_unit(n0 + i, None, bank[i % 4][:, :], h_hi, h_lo, pe_h_arrive(r - 1) if i == 0 else None)
                    if i == 0:
                        pe_sum_squares(r - 1)
                    if i >= 18:
                        turn_v(layer, i - 18)
                turn_v(layer, 7)
                for k in range(NSTEP + OUT_LAG):
                    if k < NSTEP:
                        scores(layer, k)
                    if 0 <= k - FLIP_LAG < NSTEP:
                        flip(layer, k - FLIP_LAG)
                    if 0 <= k - MIX_LAG < NSTEP and STEPS[k - MIX_LAG][2] == TB - 1:
                        mix(layer, k - MIX_LAG)
                    if k in D_SQUARE:
                        h = D_SQUARE[k]
                        pe.wait_ge(d_sq, DIFF_HEADS * layer + h + 1)
                        pe.wait_ge(d_out, DIFF_HEADS * layer + max(3, h + 1))
                        for b in range(TB):
                            ins = nc.tensor.matmul(bank[d_bank[h]][:, TB * h + b:TB * h + b + 1],
                                                   dk[:, h, P * b:P * b + P], ones[:, 0:1], start=True, stop=True)
                        ins.then_inc(d_ss, 1)
                    if k in D_SPREAD:
                        h = D_SPREAD[k]
                        if h == 0:
                            pe.wait_ge(d_inverse, 2 * layer + 2)
                        else:
                            pe.wait_ge(d_norm, DIFF_HEADS * layer + h)
                        for b in range(TB):
                            c = TB * h + b
                            ins = nc.tensor.matmul(bank[7][:, P * b:P * b + P], d_stat[:, c:c + 1].to_broadcast([P, P]),
                                                   identity, start=True, stop=True)
                        ins.then_inc(d_spread, 1)
                for m in range(KT):
                    if m >= 4:
                        pe.wait_ge(x_ready, 8 * r + m - 3)
                    order = [4, 5, 6, 7, 0, 1, 2, 3]
                    s = (n0 + MIX_IN + m) % SLOTS
                    pe.wait_ge(lo_ready, n0 + MIX_IN + m + 1)
                    for i, kt in enumerate(order):
                        if m == 0:
                            pe.wait_ge(o_ready, KT * layer + i + 1)
                        ins = pe_three(bank[m % 4][:, :], w_hi[:, s, P * kt:P * kt + P], w_lo[:, s, P * kt:P * kt + P],
                                    o_hi[:, kt, :], o_lo[:, kt, :], i == 0, i == 7)
                    ins.then_inc(unit_used, 1)

            def turn_v(layer, j):
                pe.wait_ge(in_evac, MIX_IN * layer + 17 + j + 1)
                if j >= 2:
                    pe.wait_ge(v_ready, 8 * layer + j - 1)
                for b in range(TB):
                    ins = nc.tensor.transpose(bank[4 + j % 2][:, P * b:P * b + P], tmp[:, j % 2, P * b:P * b + P],
                                              identity)
                ins.then_inc(v_turned, 1)

            def scores(layer, k):
                kind, h, b = STEPS[k]
                width = P * (b + 1)
                if k == 0:
                    pe.wait_ge(qk_ready, 8 * (layer + 1))
                    pe.wait_ge(in_evac, MIX_IN * (layer + 1))
                    pe.wait_ge(cum_ready, layer + 1)
                    pe.wait_ge(v_ready, 8 * (layer + 1))
                for c in range(2 if kind == "d" else 1):
                    e = FIRST_EXP[k] + c
                    if e >= 4:
                        pe.wait_ge(exped, NEXP * layer + e - 3)
                    dst = bank[e % 4]
                    lo = HEAD * (c if kind == "d" else h % 2)
                    rows = slice(lo, lo + HEAD)
                    q, kk, t = (dq, dk, h) if kind == "d" else (fq, fk, h // 2)
                    nc.tensor.matmul(dst[:, 0:width], q[rows, t, P * b:P * b + P], kk[rows, t, 0:width],
                                     start=True, stop=False)
                    if kind == "f":
                        rows = slice(0, CUM_ROWS[2] + 8)
                        nc.tensor.matmul(dst[:, 0:width], table_b("select", P, h, rows), cum_parts[:, 0:width],
                                         start=False, stop=False)
                    nc.tensor.matmul(dst[:, P * b:width], table_b("identity"), table_b("causal"), start=False,
                                     stop=True).then_inc(scored, 1)

            def flip(layer, k):
                kind, h, b = STEPS[k]
                pe.wait_ge(weighed, NSTEP * layer + k + 1)
                if k >= 2:
                    pe.wait_ge(flip_out, NSTEP * layer + k - 1)
                for kb in range(b + 1):
                    ins = nc.tensor.transpose(bank[4 + k % 2][:, P * kb:P * kb + P],
                                              probs[:, FIRST_EXP[k] % 4, P * kb:P * kb + P], identity)
                ins.then_inc(flipped, 1)

            def mix(layer, k):
                kind, h, _ = STEPS[k]
                pe.wait_ge(flip_out, NSTEP * layer + k + 1)
                if kind == "d":
                    if h >= 2:
                        pe.wait_ge(d_out, DIFF_HEADS * layer + h - 1)
                    dst, v, lo, n, at = bank[6 + h % 2], dv, P * h, P, 0
                else:
                    pair = h // 2
                    if h % 2 == 0:
                        if pair == 0:
                            pe.wait_ge(d_root, 2 * layer + 1)
                        elif pair == 1:
                            pe.wait_ge(d_norm, DIFF_HEADS * (layer + 1))
                        else:
                            pe.wait_ge(o_ready, KT * layer + DIFF_HEADS + pair - 1)
                    dst, v, lo, n, at = bank[6 + pair % 2], fv, HEAD * h, HEAD, HEAD * (h % 2)
                for kb in range(TB):
                    ins = nc.tensor.matmul(dst[at:at + n, P * kb:S], v[:, kb, lo:lo + n],
                                           probs_t[:, head_of[k] % 2, kb, P * kb:S], start=kb == 0,
                                           stop=kb == TB - 1)
                ins.then_inc(mixed, 1)

            pe.wait_ge(identity_in, 16)
            for m in range(KT):
                if m % (KT // X_PARTS) == 0:
                    pe.wait_ge(x_in_sem[m // (KT // X_PARTS)], 16)
                for b in range(TB):
                    ins = nc.tensor.transpose(bank[m][:, P * b:P * b + P], x_tok[:, b, P * m:P * m + P], identity)
                ins.then_inc(x_turned, 1)
            for layer in range(DEPTH):
                n0, r = layer * LAYER_UNITS, 3 * layer
                ffn(2 * layer, r + 1, n0)
                mixer(layer, r + 2, n0 + FFN_UNITS)
                ffn(2 * layer + 1, r + 3, n0 + FFN_UNITS + MIX_UNITS)

        def a_banks(kind, t):
            return {"gates": [0], "xm": [(1, 2, 3, 0, 1, 2, 1, 2)[t]], "qk": [4, 5, 6, 7], "v": [0, 3], "om": [t % 4], "zm": [t % 4],
                    "xp": [6 + t % 2], "pool": [4, 5], "zp": [t % 4]}[kind]

        def evacs(i):
            return sum(kind != "qk" for kind, _ in A_EVENTS[:i + 1])

        def wait_banks(i):
            mine = set(a_banks(*A_EVENTS[i]))
            users = [j for j in range(i) if mine & set(a_banks(*A_EVENTS[j]))]
            heads = [A_EVENTS[j][1] + 1 for j in users if A_EVENTS[j][0] == "qk"]
            others = [evacs(j) for j in users if A_EVENTS[j][0] != "qk"]
            if heads:
                nc.tensor.wait_ge(qk_evac, heads[-1])
            if others:
                nc.tensor.wait_ge(a_evac, others[-1])

        def halves_after(i):
            kind, t = A_EVENTS[i]
            if i == 2:
                return [("xc", 0), ("xm", 0)]
            return [("xc" if kind == "qk" else "xm", t + 1)] if kind in ("qk", "v") and t + 1 < M_HEADS else []

        def mix_after(i):
            kind, t = A_EVENTS[i]
            return 0 if (kind, t) == ("xp", 1) else t + 1 if kind == "pool" and t < 3 else None

        xc = place("xc", [P, KT, S], at=R_AT)
        mq = place("mq", [P, KT, S])
        mk = place("mk", [P, KT, S])
        mv = place("mv", [P, TB, D])
        M_AT = here[0]
        xm_hi = place("xm_hi", [P, 2, S], F32R)
        xm_lo = place("xm_lo", [P, 2, S], F32R)
        xc_hi = place("xc_hi", [P, 2, S], F32R)
        xc_lo = place("xc_lo", [P, 2, S], F32R)
        m_rows = place("m_rows", [36, 4, S])
        m_w = place("m_w", [P, 4, S], at=M_AT)
        m_decay = place("m_decay", [P, 2, S])
        m_negm = place("m_negm", [P, 2, S])
        hm = mq
        hsq = place("hsq", [P, 4, S], at=R_AT + 2 * 4 * KT * S)
        h_rstd = place("h_rstd", [P, 4, S])
        ya_hi = place("ya_hi", [P, KT, S], F32R, at=R_AT + 3 * 4 * KT * S)
        ya_lo = place("ya_lo", [P, KT, S], F32R)
        gate_p = place("gate_p", [P, 2, S])
        rot = place("rot", [P, 2, S])
        pos_i = place("pos_i", [P, S], I32, at=here[0] - 4 * S)
        yb_hi = place("yb_hi", [P, KT, S], F32R, at=R_AT)
        yb_lo = place("yb_lo", [P, KT, S], F32R)
        pm_hi = place("pm_hi", [P, 2, S], F32R, at=R_AT + 2 * 4 * KT * S)
        pm_lo = place("pm_lo", [P, 2, S], F32R)
        sums = place("sums", [P, 2, S])
        pooled = place("pooled", [P, 2, S])

        a_evac = sem("a_evac")
        a_act = sem("a_act")
        conv_ready = sem("conv_ready")
        silu_ready = sem("silu_ready")
        xc_half, xc_ready = sem("xc_half"), sem("xc_ready")
        xm_half, xm_ready = sem("xm_half"), sem("xm_ready")
        qk_evac = sem("qk_evac")
        m_gate = sem("m_gate")
        m_rows_ready, m_turned, m_cols_ready = sem("m_rows_ready"), sem("m_turned"), sem("m_cols_ready")
        m_bcast, m_negm_ready, m_evac = sem("m_bcast"), sem("m_negm_ready"), sem("m_evac")
        m_scored, m_masked, m_decayed, m_weighed = (sem(n) for n in ("m_scored", "m_masked", "m_decayed", "m_weighed"))
        m_used, m_scaled = sem("m_used"), sem("m_scaled")
        om_ready, hsq_half, hsq_ready = sem("om_ready"), sem("hsq_half"), sem("hsq_ready")
        hss_ready, hroot_ready = sem("hss_ready"), sem("hroot_ready")
        y_prod, y_half, y_ready = sem("y_prod"), sem("y_half"), sem("y_ready")
        pmix_ready, pm_half, pm_ready = sem("pmix_ready"), sem("pm_half"), sem("pm_ready")
        pos_in_sem, rot_step, rot_ready = sem("pos_in_sem"), sem("rot_step"), sem("rot_ready")
        M_STEPS = [(h, b) for h in range(M_HEADS) for b in range(TB)]

        @block.gpsimd
        def _(pool):
            for h in range(M_HEADS):
                for j in range(2):
                    pool.wait_ge(xm_half, 2 * h + j + 1)
                    nc.gpsimd.tensor_tensor(xm_lo[:, j, :], tmp[:, (2 * h + j) % 4, :], xm_hi[:, j, :].bitcast(F32),
                                            ALU.subtract).then_inc(xm_ready, 1)
            pool_squares(FINAL + 1)

        @block.scalar
        def _(act):
            act_cut(A_START + 3)
            act.wait_ge(final_sum, 1)
            nc.scalar.activation(tmp[:, 3, :], tmp[:, 3, :], ACT.Sqrt, scale=1.0 / D,
                                 bias=small[:, 2:3]).then_inc(final_root, 1)
            act_root(FINAL)
            act_cut(A_START + 4)
            for i, (kind, t) in enumerate(A_EVENTS[:A_HEADS_END]):
                if i >= 2:
                    act_cut(A_START + i + 3)
                if kind == "xm":
                    act.wait_ge(conv_ready, t + 1)
                    nc.scalar.activation(xc[:, t, :], xc[:, t, :], ACT.Silu).then_inc(silu_ready, 1)
                if kind == "qk":
                    act.wait_ge(unit_used, A_START + i + 1)
                    for j in range(2):
                        nc.scalar.activation(mq[:, 2 * t + j, :], bank[4 + j][:, :], ACT.Copy)
                    for j in range(2):
                        ins = nc.scalar.activation(mk[:, 2 * t + j, :], bank[6 + j][:, :], ACT.Copy, scale=M_DIM ** -0.5)
                    ins.then_inc(qk_evac, 1)
                for operand, h in halves_after(i):
                    act.drain()
                    if operand == "xm" and h:
                        act.wait_ge(unit_used, A_START + i + 1)
                    for j in range(2):
                        if operand == "xm":
                            nc.scalar.activation(xm_hi[:, j, :], tmp[:, (2 * h + j) % 4, :], ACT.Copy).then_inc(xm_half, 1)
                        else:
                            nc.scalar.activation(xc_hi[:, j, :], xc[:, 2 * h + j, :], ACT.Copy).then_inc(xc_half, 1)
                if (kind, t) == ("qk", 1):
                    z, e = m_rows[32:36, 1, :], m_rows[32:36, 2, :]
                    act.wait_ge(m_gate, 1)
                    nc.scalar.activation(e, z, ACT.Abs)
                    act.drain()
                    nc.scalar.activation(e, e, ACT.Exp, scale=-1.0)
                    act.drain()
                    nc.scalar.activation(e, e, ACT.Ln, bias=1.0).then_inc(m_gate, 1)
            for k in range(len(M_STEPS) + 1):
                if k < len(M_STEPS):
                    h, b = M_STEPS[k]
                    if b == 0:
                        act.wait_ge(m_bcast, h + 1)
                        if h >= 2:
                            act.wait_ge(m_scaled, h - 1)
                        nc.scalar.activation(m_negm[:, h % 2, :], bank[0][:, :], ACT.Copy)
                        nc.scalar.activation(tmp[:, 2 + h % 2, :], bank[1][:, :], ACT.Exp).then_inc(m_negm_ready, 1)
                    act.wait_ge(m_masked, k + 1)
                    if b == 0:
                        act.drain()
                    if b < TB - 1:
                        nc.scalar.activation(m_decay[:, k % 2, P * (b + 1):S], m_negm[:, h % 2, P * (b + 1):S], ACT.Exp,
                                             bias=m_cols[:, 4 * b + h:4 * b + h + 1])
                    nc.scalar.activation(m_decay[:, k % 2, P * b:P * b + P], m_mask[:, k % 2, :],
                                         ACT.Exp).then_inc(m_decayed, 1)
                if k and k % TB == 0:
                    h = k // TB - 1
                    act.wait_ge(m_used, k)
                    for j in range(2):
                        nc.scalar.activation(hm[:, 2 * h + j, :], bank[4 + j][:, :], ACT.Copy)
                    if h >= 2:
                        act.wait_ge(m_scaled, h - 1)
                    nc.scalar.activation(tmp[:, h % 2, :], bank[6][:, :], ACT.Abs).then_inc(m_evac, 1)
            act.dma_start(pos_i[:, :], pos_in.to_broadcast([P, S])).then_inc(pos_in_sem, 16)
            for i in range(A_HEADS_END, len(A_EVENTS)):
                kind, t = A_EVENTS[i]
                act_cut(A_START + i + 3)
                if kind in ("om", "zm", "zp"):
                    buf = gate_p[:, t % 2, :] if kind == "zp" else tmp[:, t % 2, :]
                    act.wait_ge(a_evac, evacs(i))
                    nc.scalar.activation(buf, buf, ACT.Sigmoid if kind == "om" else ACT.Silu).then_inc(a_act, 1)
                if kind == "om":
                    act.wait_ge(om_ready, t + 1)
                    if t % 2 and t > 2:
                        act.wait_ge(hsq_ready, t // 2)
                    nc.scalar.activation(tmp[:, 2, :] if t % 2 else hsq[:, t // 2, :], hm[:, t, :],
                                         ACT.Square).then_inc(hsq_half, 1)
                    if t == KT - 1:
                        for h in range(M_HEADS):
                            act.wait_ge(hss_ready, h + 1)
                            nc.scalar.activation(h_rstd[:, h, :], bank[4 + h][:, :], ACT.Sqrt, scale=1.0 / M_DIM,
                                                 bias=small[:, 1:2]).then_inc(hroot_ready, 1)
                if kind == "zm":
                    act.wait_ge(y_prod, t + 1)
                    nc.scalar.activation(ya_hi[:, t, :], hm[:, t, :], ACT.Copy).then_inc(y_half, 1)
                if kind == "zp":
                    act.wait_ge(y_prod, KT + t + 1)
                    nc.scalar.activation(yb_hi[:, t, :], gate_p[:, t % 2, :], ACT.Copy).then_inc(y_half, 1)
                g = mix_after(i)
                if g is not None:
                    act.wait_ge(pmix_ready, g + 1)
                    if g:
                        act.wait_ge(unit_used, A_START + i + 1)
                    for j in range(2):
                        nc.scalar.activation(pm_hi[:, j, :], tmp[:, 2 + j, :], ACT.Copy).then_inc(pm_half, 1)
            for j in range(2):
                act.wait_ge(rot_step, j + 1)
                nc.scalar.activation(rot[:, j, :], rot[:, j, :], ACT.Sin).then_inc(rot_ready, 1)
            for m in range(KT):
                if m < 7:
                    for j in range(2):
                        act_cut(A_OUT + 2 * m + j + 3)
                act_h_tile(FINAL + 1, m)
            act_cut(A_OUT + 17)
            act_cut(A_OUT + 18)
            act_root(FINAL + 1)

        @block.vector
        def _(dve):
            dve.wait_ge(ss_ready, FINAL + 1)
            dve.wait_ge(final_ss, 1)
            nc.vector.tensor_copy(tmp[:, 3, :], bank[3][:, :])
            dve.drain()
            nc.vector.scalar_tensor_tensor(out=tmp[:, 3, :], in0=bank[7][:, :], scalar=RMS_EPS, in1=tmp[:, 3, :],
                                           op0=ALU.mult, op1=ALU.add).then_inc(final_sum, 1)
            dve_cut(A_START + 3)
            dve.wait_ge(final_root, 1)
            nc.vector.reciprocal(rstd[:, :], tmp[:, 3, :])
            dve_cut(A_START + 4)
            dve.drain()

            def halves(h):
                for j in range(2):
                    dve.wait_ge(xc_half, 2 * h + j + 1)
                    nc.vector.tensor_tensor(xc_lo[:, j, :], xc[:, 2 * h + j, :], xc_hi[:, j, :].bitcast(F32),
                                            ALU.subtract).then_inc(xc_ready, 1)

            def gates_bias():
                nc.vector.memset(m_rows[32:36, 3, :], 1.0)
                dve.drain()
                for rows, j in ((slice(0, 4), 0), (slice(32, 36), 1)):
                    ins = nc.vector.tensor_scalar(m_rows[rows, j, :], m_rows[rows, j, :], col("b_if", 0, rows),
                                                  None, ALU.add)
                ins.then_inc(m_gate, 1)

            def gates_sums():
                dve.wait_ge(m_gate, 2)
                z, e, f = (m_rows[32:36, j, :] for j in (1, 2, 3))
                nc.vector.scalar_tensor_tensor(out=z, in0=z, scalar=0.0, in1=e, op0=ALU.min, op1=ALU.subtract)
                dve.drain()
                nc.vector.tensor_tensor_scan(e, f, z, 0.0, ALU.mult, ALU.add)
                nc.vector.memset(m_rows[0:4, 1, :], 0.0)
                dve.drain()
                a, zero, big, f = (m_rows[0:4, j, :] for j in range(4))
                nc.vector.tensor_copy(f, e)
                dve.drain()
                nc.vector.tensor_tensor(a, a, f, ALU.subtract)
                dve.drain()
                nc.vector.tensor_tensor_scan(big, zero, a, 0.0, ALU.add, ALU.max)
                dve.drain()
                nc.vector.tensor_scalar(big, big, -1.0, None, ALU.mult)
                dve.drain()
                nc.vector.tensor_tensor(f, big, f, ALU.subtract).then_inc(m_rows_ready, 1)

            for i, (kind, t) in enumerate(A_EVENTS[:A_HEADS_END]):
                if i >= 2:
                    dve_cut(A_START + i + 3)
                dve.wait_ge(unit_used, A_START + i + 1)
                if kind == "gates":
                    src = bank[0]
                    nc.vector.tensor_tensor(m_rows[0:4, 0, :], src[0:4, :], rstd[0:4, :], ALU.mult)
                    nc.vector.tensor_tensor(m_rows[32:36, 1, :], src[32:36, :], rstd[32:36, :],
                                            ALU.mult).then_inc(a_evac, 1)
                elif kind == "xm":
                    dve.drain()
                    if t >= 4:
                        dve.wait_ge(xm_ready, 2 * (t // 2 - 1))
                    xm, acc = tmp[:, t % 4, :], xc[:, t, :]
                    nc.vector.tensor_tensor(xm, bank[a_banks(kind, t)[0]][:, :], rstd[:, :], ALU.mult).then_inc(a_evac, 1)
                    dve.drain()
                    nc.vector.tensor_scalar(acc, xm, col("conv_w", 8 * (CONV_K - 1) + t), col("conv_b", t), ALU.mult,
                                            ALU.add)
                    for s in range(1, CONV_K):
                        dve.drain()
                        ins = nc.vector.scalar_tensor_tensor(out=acc[:, s:S], in0=xm[:, 0:S - s],
                                                             scalar=col("conv_w", 8 * (CONV_K - 1 - s) + t),
                                                             in1=acc[:, s:S], op0=ALU.mult, op1=ALU.add)
                    ins.then_inc(conv_ready, 1)
                elif kind == "v":
                    for j in range(2):
                        ins = nc.vector.tensor_copy(mv[:, 2 * j:2 * j + 2, M_DIM * t:M_DIM * (t + 1)],
                                                    bank[3 * j][:, :].rearrange("p (b n) -> p b n", b=2))
                    ins.then_inc(a_evac, 1)
                if (kind, t) == ("v", 0):
                    gates_bias()
                for operand, h in halves_after(i):
                    if operand == "xc":
                        dve.wait_ge(silu_ready, 2 * h + 2)
                        halves(h)
                if (kind, t) == ("qk", 2):
                    gates_sums()
                if i == 2:
                    dve.wait_ge(sd_ready, FINAL + 1)
                    nc.vector.reciprocal(sqsum[:, :], tmp[:, 2, :])
            def m_scale(h):
                dve.wait_ge(m_evac, h + 1)
                den = tmp[:, h % 2, :]
                nc.vector.tensor_tensor(den, den, tmp[:, 2 + h % 2, :], ALU.max)
                dve.drain()
                nc.vector.reciprocal(den, den)
                dve.drain()
                for j in range(2):
                    ins = nc.vector.tensor_tensor(hm[:, 2 * h + j, :], hm[:, 2 * h + j, :], den, ALU.mult)
                ins.then_inc(m_scaled, 1)
                dve.drain()

            dve.wait_ge(m_turned, 1)
            nc.vector.tensor_copy(m_cols[:, :], bank[7][:, 0:16]).then_inc(m_cols_ready, 1)
            dve.wait_ge(m_cols_ready, 1)
            for k, (h, b) in enumerate(M_STEPS):
                dve.wait_ge(m_negm_ready, h + 1)
                dve.drain()
                nc.vector.scalar_tensor_tensor(
                    out=m_mask[:, k % 2, :], in0=m_negm[:, h % 2, P * b:P * b + P],
                    scalar=m_cols[:, 4 * b + h:4 * b + h + 1], in1=table("causal_t"), op0=ALU.add,
                    op1=ALU.add).then_inc(m_masked, 1)
                dve.wait_ge(m_scored, k + 1)
                dve.wait_ge(m_decayed, k + 1)
                if k >= 4:
                    dve.wait_ge(m_used, k - 3)
                nc.vector.tensor_tensor(m_w[:, b, P * b:S], bank[2 + k % 2][:, P * b:S], m_decay[:, k % 2, P * b:S],
                                        ALU.mult).then_inc(m_weighed, 1)
                if b == 1 and h:
                    m_scale(h - 1)
            m_scale(M_HEADS - 1)

            def head_norm(h):
                dve.wait_ge(hroot_ready, h + 1)
                nc.vector.reciprocal(h_rstd[:, h, :], h_rstd[:, h, :])
                dve.drain()
                for t in (2 * h, 2 * h + 1):
                    nc.vector.scalar_tensor_tensor(out=hm[:, t, :], in0=hm[:, t, :], scalar=col("head_norm", t),
                                                   in1=h_rstd[:, h, :], op0=ALU.mult, op1=ALU.mult)
                dve.drain()
                for t in (2 * h, 2 * h + 1):
                    nc.vector.scalar_tensor_tensor(out=hm[:, t, :], in0=xc[:, t, :], scalar=col("skip", t),
                                                   in1=hm[:, t, :], op0=ALU.mult, op1=ALU.add)
                dve.drain()

            done = 0
            for i in range(A_HEADS_END, len(A_EVENTS)):
                kind, t = A_EVENTS[i]
                dve_cut(A_START + i + 3)
                if kind == "zm" and t % 2 == 0:
                    head_norm(t // 2)
                dve.wait_ge(unit_used, A_START + i + 1)
                if kind in ("om", "zm", "zp"):
                    done += 1
                    buf = gate_p[:, t % 2, :] if kind == "zp" else tmp[:, t % 2, :]
                    dve.drain()
                    nc.vector.tensor_tensor(buf, bank[t % 4][:, :], rstd[:, :], ALU.mult).then_inc(a_evac, 1)
                    dve.wait_ge(a_act, done)
                if kind == "om":
                    nc.vector.tensor_tensor(hm[:, t, :], hm[:, t, :], buf, ALU.mult).then_inc(om_ready, 1)
                    nc.vector.scalar_tensor_tensor(out=x[:, t, :], in0=x[:, t, :], scalar=col("final_norm", t),
                                                   in1=sqsum[:, :], op0=ALU.mult, op1=ALU.mult).then_inc(x_ready, 1)
                    if t % 2:
                        dve.wait_ge(hsq_half, t + 1)
                        nc.vector.tensor_tensor(hsq[:, t // 2, :], hsq[:, t // 2, :], tmp[:, 2, :],
                                                ALU.add).then_inc(hsq_ready, 1)
                if kind == "zm":
                    nc.vector.tensor_tensor(hm[:, t, :], hm[:, t, :], buf, ALU.mult).then_inc(y_prod, 1)
                    dve.wait_ge(y_half, t + 1)
                    nc.vector.tensor_tensor(ya_lo[:, t, :], hm[:, t, :], ya_hi[:, t, :].bitcast(F32),
                                            ALU.subtract).then_inc(y_ready, 1)
                if kind == "zp":
                    nc.vector.tensor_tensor(buf, buf, pooled[:, t % 2, :], ALU.mult).then_inc(y_prod, 1)
                    dve.wait_ge(y_half, KT + t + 1)
                    nc.vector.tensor_tensor(yb_lo[:, t, :], buf, yb_hi[:, t, :].bitcast(F32),
                                            ALU.subtract).then_inc(y_ready, 1)
                if kind == "xp":
                    g, w = t // 2, P_WINDOWS[t // 2]
                    if t % 2 == 0 and t >= 2:
                        dve.wait_ge(pm_ready, 2 * (t // 2))
                    xp = tmp[:, t % 2, :]
                    dve.drain()
                    nc.vector.tensor_tensor(xp, bank[6 + t % 2][:, :], rstd[:, :], ALU.mult).then_inc(a_evac, 1)
                    src, s = xp, 1
                    while s < w:
                        dst = sums[:, (s.bit_length() - 1) % 2, :]
                        dve.drain()
                        nc.vector.tensor_copy(dst[:, 0:s], src[:, 0:s])
                        nc.vector.tensor_tensor(dst[:, s:S], src[:, s:S], src[:, 0:S - s], ALU.add)
                        src, s = dst, 2 * s
                    at = TAB["pool_head"] + 16 * g
                    dve.drain()
                    nc.vector.scalar_tensor_tensor(out=tmp[:, 2 + t % 2, 16:S], in0=src[:, 16:S], scalar=1.0 / w,
                                                   in1=xp[:, 16:S], op0=ALU.mult, op1=ALU.subtract)
                    nc.vector.tensor_tensor(src[:, 0:16], src[:, 0:16], tab[:, at:at + 16], ALU.mult)
                    dve.drain()
                    ins = nc.vector.tensor_tensor(tmp[:, 2 + t % 2, 0:16], src[:, 0:16], xp[:, 0:16], ALU.subtract)
                    if t % 2:
                        ins.then_inc(pmix_ready, 1)
                if kind == "pool":
                    dve.drain()
                    for j in range(2):
                        ins = nc.vector.tensor_scalar(pooled[:, j, :], bank[4 + j][:, :], col("pool_scale", 2 * t + j),
                                                      None, ALU.mult)
                    ins.then_inc(a_evac, 1)
                    dve.drain()
                g = mix_after(i)
                if g is not None:
                    for j in range(2):
                        dve.wait_ge(pm_half, 2 * g + j + 1)
                        nc.vector.tensor_tensor(pm_lo[:, j, :], tmp[:, 2 + j, :], pm_hi[:, j, :].bitcast(F32),
                                                ALU.subtract).then_inc(pm_ready, 1)
            ang, turns = tmp[:, 2, :], tmp[:, 1, :]
            TWO_PI = (6.28125, 0.0019350051879882812, 2 * math.pi - 6.28125 - 0.0019350051879882812)
            ROUND = 1.5 * 2.0 ** 23
            dve.wait_ge(pos_in_sem, 16)
            dve.drain()
            nc.vector.tensor_copy(ang, pos_i[:, :])
            dve.drain()
            nc.vector.tensor_scalar(ang, ang, col("inv_freq"), None, ALU.mult)
            for j in range(2):
                quarter = 0.25 * (1 - j)
                dve.drain()
                nc.vector.tensor_scalar(turns, ang, 0.5 / math.pi, quarter, ALU.mult, ALU.add)
                dve.drain()
                nc.vector.tensor_scalar(turns, turns, ROUND, None, ALU.add)
                dve.drain()
                nc.vector.tensor_scalar(turns, turns, -ROUND, None, ALU.add)
                src = ang
                for part in TWO_PI:
                    dve.drain()
                    nc.vector.scalar_tensor_tensor(out=rot[:, j, :], in0=turns, scalar=-part, in1=src, op0=ALU.mult,
                                                   op1=ALU.add)
                    src = rot[:, j, :]
                dve.drain()
                if j == 0:
                    nc.vector.tensor_scalar(src, src, math.pi / 2, None, ALU.add)
                    dve.drain()
                nc.vector.tensor_scalar(src, src, 3.1415925, -3.1415925, ALU.min, ALU.max).then_inc(rot_step, 1)
            dve.wait_ge(rot_ready, 2)
            nc.vector.tensor_scalar(rot[:, 1, :], rot[:, 1, :], col("rope_sign"), None, ALU.mult)
            for m in range(KT + 1):
                if m < KT:
                    if m < 7:
                        for j in range(2):
                            dve_cut(A_OUT + 2 * m + j + 3)
                    dve.wait_ge(unit_used, A_OUT + 2 * m + 2)
                    nc.vector.tensor_tensor(x[:, m, :], bank[m % 4][:, :], x[:, m, :], ALU.add).then_inc(x_ready, 1)
                if m >= 1:
                    dve_h_tile(FINAL + 1, m - 1)
            dve_cut(A_OUT + 17)
            dve_cut(A_OUT + 18)
            dve_norm(FINAL + 1)

        @block.tensor
        def _(pe):
            def spread(h):
                at = TAB["select"] + P * h
                if h:
                    pe.wait_ge(m_negm_ready, h)
                for j in range(2):
                    ins = nc.tensor.matmul(bank[j][:, :], tab[0:4, at:at + P], m_rows[0:4, 2 + j, :], start=True,
                                           stop=True)
                ins.then_inc(m_bcast, 1)

            def m_scores(k):
                h, b = M_STEPS[k]
                if k >= 2:
                    pe.wait_ge(m_weighed, k - 1)
                for i in range(2):
                    ins = nc.tensor.matmul(bank[2 + k % 2][:, P * b:S], mk[:, 2 * h + i, P * b:P * b + P],
                                           mq[:, 2 * h + i, P * b:S], start=i == 0, stop=i == 1)
                ins.then_inc(m_scored, 1)

            def m_mix(k):
                h, b = M_STEPS[k]
                pe.wait_ge(m_weighed, k + 1)
                if b == 0 and h:
                    pe.wait_ge(m_evac, h)
                w = m_w[:, b, P * b:S]
                for j in range(2):
                    at = M_DIM * h + P * j
                    nc.tensor.matmul(bank[4 + j][:, P * b:S], mv[:, b, at:at + P], w, start=b == 0, stop=b == TB - 1)
                nc.tensor.matmul(bank[6][:, P * b:S], ones, w, start=b == 0, stop=b == TB - 1).then_inc(m_used, 1)

            def head_sums():
                for h in range(M_HEADS):
                    pe.wait_ge(hsq_ready, h + 1)
                    nc.tensor.matmul(bank[4 + h][:, :], ones, hsq[:, h, :], start=True, stop=True).then_inc(hss_ready, 1)

            def attend():
                pe.wait_ge(m_rows_ready, 1)
                pe.wait_ge(a_evac, evacs(A_HEADS_END - 1))
                pe.wait_ge(qk_evac, M_HEADS)
                for b in range(TB):
                    ins = nc.tensor.transpose(bank[7][:, 4 * b:4 * b + 4], m_rows[0:4, 0, P * b:P * b + P],
                                              identity[0:4, 0:4])
                ins.then_inc(m_turned, 1)
                spread(0)
                m_scores(0)
                for k, (h, b) in enumerate(M_STEPS):
                    if k + 1 < len(M_STEPS):
                        m_scores(k + 1)
                    if b == 2 and h + 1 < M_HEADS:
                        spread(h + 1)
                    m_mix(k)

            for i, (kind, t) in enumerate(A_EVENTS):
                n, s = A_START + i, (A_START + i) % SLOTS
                wait_banks(i)
                if (kind, t) == ("xp", 0):
                    pe.wait_ge(hroot_ready, M_HEADS)
                banks = [bank[b] for b in a_banks(kind, t)]
                if kind in ("qk", "v"):
                    pe.wait_ge(lo_ready, n + 1)
                    pe.wait_ge(xc_ready if kind == "qk" else xm_ready, 2 * t + 2)
                    if kind == "qk":
                        for j in range(4):
                            for kt in range(2):
                                at = 512 * (j // 2) + M_DIM * kt + P * (j % 2)
                                ins = pe_three(banks[j][:, :], w_hi[:, s, at:at + P], w_lo[:, s, at:at + P],
                                            xc_hi[:, kt, :], xc_lo[:, kt, :], kt == 0, kt == 1)
                    else:
                        for b in range(TB):
                            for kt in range(2):
                                at = M_DIM * kt
                                ins = pe_three(banks[b // 2][:, M_DIM * (b % 2):M_DIM * (b % 2) + M_DIM],
                                            xm_hi[:, kt, P * b:P * b + P], xm_lo[:, kt, P * b:P * b + P],
                                            w_hi[:, s, at:at + M_DIM], w_lo[:, s, at:at + M_DIM], kt == 0, kt == 1)
                    ins.then_inc(unit_used, 1)
                elif kind == "pool":
                    pe.wait_ge(lo_ready, n + 1)
                    pe.wait_ge(pm_ready, 2 * t + 2)
                    for j in range(2):
                        for kt in range(2):
                            at = M_DIM * kt + P * j
                            ins = pe_three(banks[j][:, :], w_hi[:, s, at:at + P], w_lo[:, s, at:at + P], pm_hi[:, kt, :],
                                        pm_lo[:, kt, :], kt == 0, kt == 1)
                    ins.then_inc(unit_used, 1)
                else:
                    pe_unit(n, None, banks[0][:, :], h_hi, h_lo, pe_h_arrive(FINAL) if i == 0 else None)
                if (kind, t) == ("om", KT - 1):
                    head_sums()
                if i == 0:
                    for m in range(KT):
                        pe.wait_ge(final_sq_ready, m + 1)
                        ins = nc.tensor.matmul(bank[3][:, :], ones, final_sq[:, m, :], start=m == 0, stop=m == KT - 1)
                    ins.then_inc(final_ss, 1)
                    pe_sum_squares(FINAL)
                if i == A_HEADS_END - 1:
                    attend()

            for m in range(KT):
                if m >= 4:
                    pe.wait_ge(x_ready, 8 * 8 + m - 3)
                else:
                    pe.wait_ge(a_evac, evacs(A_EVENTS.index(("zp", 4 + m))))
                for j in range(2):
                    n = A_OUT + 2 * m + j
                    s = n % SLOTS
                    pe.wait_ge(lo_ready, n + 1)
                    if m == 0:
                        pe.wait_ge(y_ready, KT * (j + 1))
                    for kt in range(8):
                        ins = pe_three(bank[m % 4][:, :], w_hi[:, s, P * kt:P * kt + P], w_lo[:, s, P * kt:P * kt + P],
                                    (yb_hi if j else ya_hi)[:, kt, :], (yb_lo if j else ya_lo)[:, kt, :],
                                    j == 0 and kt == 0, j == 1 and kt == 7)
                    ins.then_inc(unit_used, 1)

        Q_EVENTS = [("nope", h) for h in range(C_HEADS)] + [("rope", p) for p in range(C_HEADS // 2)]
        C_FLIP_LAG, C_MIX_LAG, C_OUT_LAG = 3, 5, 7
        C_STEPS = [(h, b) for h in range(C_HEADS) for b in range(TB)]

        def q_events(kind, u):
            return (2 * u, 2 * u + 1) if kind == "q" else (C_HEADS + 2 * u, C_HEADS + 2 * u + 1)


        zs = place("zs", [P, KT, S], at=R_AT)
        qn = place("qn", [P, C_HEADS, S])
        qr = place("qr", [P, C_HEADS // 2, S])
        kn = place("kn", [P, C_HEADS, S])
        kr = place("kr", [P, C_HEADS // 2, S])
        c_probs = place("c_probs", [P, 4, S])
        ckv_hi = place("ckv_hi", [P, KVT, S], F32R)
        ckv_lo = place("ckv_lo", [P, KVT, S], F32R)
        q_rstd = place("q_rstd", [P, S], at=R_AT + 80 * 1024)
        kv_rstd = place("kv_rstd", [P, S])
        cq_hi = place("cq_hi", [P, QT, S], F32R, at=R_AT + 4 * S * (2 * KT + 4))
        cq_lo = place("cq_lo", [P, QT, S], F32R)
        ckv = place("ckv", [P, KVT, S], at=R_AT + 4 * S * (3 * KT + 4))
        kpe_sq, kpe = c_probs[:, 0, :], sqsum[:, :]
        cv = place("cv", [P, TB, C_HEADS * P], at=H_AT)
        c_probs_t = place("c_probs_t", [P, 2, TB, S])
        co_hi = place("co_hi", [P, C_HEADS, S], F32R, at=R_AT + 4 * S * KT)
        co_lo = place("co_lo", [P, C_HEADS, S], F32R, at=R_AT + 4 * S * (2 * KT + 4))
        out_tok = place("out_tok", [P, 2, TB, P], at=R_AT + 4 * S * (3 * KT + 8))

        c_evac, c_act = sem("c_evac"), sem("c_act")
        z_evac, z_act = sem("z_evac"), sem("z_act")
        qsum_ready, kvsum_ready, lat_ss, lat_root = (sem(n) for n in ("qsum_ready", "kvsum_ready", "lat_ss", "lat_root"))
        ckv_norm, ckv_half, lat_ready, ckv_ready = (sem(n) for n in ("ckv_norm", "ckv_half", "lat_ready", "ckv_ready"))
        kpe_ready = sem("kpe_ready")
        q_evac, q_act, q_summed, q_root, q_ready = (sem(n) for n in ("q_evac", "q_act", "q_summed", "q_root", "q_ready"))
        k_evac, k_act, k_summed, k_root, k_ready = (sem(n) for n in ("k_evac", "k_act", "k_summed", "k_root", "k_ready"))
        q_total, k_evac_v = sem("q_total"), sem("k_evac_v")
        c_scored, c_maxed, c_exped = sem("c_scored"), sem("c_maxed"), sem("c_exped")
        c_weighed, c_flipped, c_flip_out = sem("c_weighed"), sem("c_flipped"), sem("c_flip_out")
        c_mixed, co_prod, co_half, co_ready = (sem(n) for n in ("c_mixed", "co_prod", "co_half", "co_ready"))
        out_turned, out_copied = sem("out_turned"), sem("out_copied")
        out_done = [sem("out_done0"), sem("out_done1")]

        def c_out(h):
            nc.scalar.wait_ge(co_prod, h + 1)
            nc.scalar.activation(co_hi[:, h, :], tmp[:, h % 2, :], ACT.Copy).then_inc(co_half, 1)

        def c_head(h):
            nc.vector.wait_ge(c_mixed, h + 1)
            if h == 0:
                nc.vector.wait_ge(z_act, KT)
            nc.vector.drain()
            nc.vector.tensor_tensor(tmp[:, h % 2, :], bank[6 + h % 2][:, :], zs[:, h, :], ALU.mult).then_inc(co_prod, 1)
            nc.vector.wait_ge(co_half, h + 1)
            nc.vector.tensor_tensor(co_lo[:, h, :], tmp[:, h % 2, :], co_hi[:, h, :].bitcast(F32),
                                    ALU.subtract).then_inc(co_ready, 1)

        @block.scalar
        def _(act):
            def swap(dst, src):
                for q in range(4):
                    ins = nc.scalar.activation(dst[32 * q:32 * q + 32, :], src[32 * (q ^ 1):32 * (q ^ 1) + 32, :], ACT.Copy)
                return ins

            def squares(e):
                kind, t = Q_EVENTS[e]
                act.wait_ge(q_evac, e + 1)
                if e >= 2:
                    act.wait_ge(q_summed, e - 1)
                if kind == "nope":
                    nc.scalar.activation(tmp[:, 2 + e % 2, :], qn[:, t, :], ACT.Square).then_inc(q_act, 1)
                else:
                    nc.scalar.activation(tmp[:, 2 + e % 2, :], tmp[:, e % 2, :], ACT.Square)
                    act.drain()
                    swap(tmp[:, e % 2, :], qr[:, t, :]).then_inc(q_act, 1)

            def act_key_roots(u):
                for h in (2 * u, 2 * u + 1):
                    act.wait_ge(k_summed, h + 1)
                    if h >= 2:
                        act.wait_ge(k_ready, h - 1)
                    nc.scalar.activation(tmp[:, 2 + h % 2, :], bank[6 + h % 2][:, :], ACT.Sqrt, scale=1.0 / QK_HEAD,
                                         bias=small[:, 1:2]).then_inc(k_root, 1)

            def act_keys_values(u):
                act.wait_ge(unit_used, C_START + C_EVENTS.index(("kv", u)) + 1)
                for j in range(2):
                    nc.scalar.activation(cv[:, 2 * j:2 * j + 2, 2 * P * u:2 * P * u + 2 * P],
                                         bank[2 + j][:, :].rearrange("p (b n) -> p b n", b=2),
                                         ACT.Copy).then_inc(k_evac_v, 1)
                for j in range(2):
                    nc.scalar.activation(kn[:, 2 * u + j, :], bank[4 * (u % 2) + j][:, :], ACT.Copy).then_inc(k_evac, 1)
                if u:
                    act_key_roots(u - 1)
                else:
                    act.wait_ge(q_ready, len(Q_EVENTS))
                    act.wait_ge(q_total, 1)
                    nc.scalar.activation(q_scale[:, :], q_scale[:, :], ACT.Sqrt, scale=1.0 / QK_HEAD,
                                         bias=small[:, 1:2]).then_inc(q_root, 1)
                act.drain()
                for j in range(2):
                    nc.scalar.activation(tmp[:, j, :], kn[:, 2 * u + j, :], ACT.Square).then_inc(k_act, 1)

            for i, (kind, t) in enumerate(C_EVENTS):
                act_cut(C_START + i + 3)
                if (kind, t) in C_LATENT:
                    buf = tmp[:, i % 2, :]
                    act.wait_ge(c_evac, i + 1)
                if kind == "cq":
                    nc.scalar.activation(q_rstd[:, :] if t == 0 else tmp[:, 2 + i % 2, :], buf, ACT.Square)
                    nc.scalar.activation(cq_hi[:, t, :], buf, ACT.Copy, scale=col("q_norm", t)).then_inc(c_act, 1)
                if kind == "ckv":
                    nc.scalar.activation(kv_rstd[:, :] if t == 0 else tmp[:, 2 + i % 2, :], ckv[:, t, :],
                                         ACT.Square).then_inc(c_act, 1)
                if kind == "kpe":
                    nc.scalar.activation(kpe_sq, buf, ACT.Square)
                    swap(tmp[:, 2 + i % 2, :], kpe).then_inc(c_act, 1)
                if kind == "z":
                    act.wait_ge(z_evac, t + 1)
                    nc.scalar.activation(zs[:, t, :], zs[:, t, :], ACT.Silu).then_inc(z_act, 1)
                if (kind, t) == ("z", 0):
                    for j, dst, n in ((0, q_rstd, Q_LORA), (1, kv_rstd, KV_LORA)):
                        act.wait_ge(lat_ss, j + 1)
                        nc.scalar.activation(dst[:, :], bank[6 + j][:, :], ACT.Sqrt, scale=1.0 / n,
                                             bias=small[:, 1:2]).then_inc(lat_root, 1)
                if (kind, t) == ("q", 0):
                    for j in range(KVT):
                        act.wait_ge(ckv_norm, j + 1)
                        nc.scalar.activation(ckv_hi[:, j, :], ckv[:, j, :], ACT.Copy).then_inc(ckv_half, 1)
                if kind in ("q", "r"):
                    for e in q_events(kind, t):
                        squares(e)
                if kind == "kv":
                    act_keys_values(t)
            act_key_roots(C_HEADS // 2 - 1)
            for k in range(len(C_STEPS) + C_OUT_LAG):
                if k < len(C_STEPS):
                    h, b = C_STEPS[k]
                    width = P * (b + 1)
                    act.wait_ge(c_maxed, k + 1)
                    if k >= 4:
                        act.wait_ge(c_flipped, k - 3)
                    nc.scalar.activation(c_probs[:, k % 4, 0:width], bank[k % 4][:, 0:width], ACT.Exp,
                                         scale=q_scale[:, 8 * b + h:8 * b + h + 1], bias=softstat[:, k, 0:1],
                                         accum_out=softstat[:, k, 1:2]).then_inc(c_exped, 1)
                if 0 <= k - C_FLIP_LAG < len(C_STEPS):
                    j = k - C_FLIP_LAG
                    h, b = C_STEPS[j]
                    act.wait_ge(c_flipped, j + 1)
                    if b == 0 and h >= 2:
                        act.wait_ge(c_mixed, h - 1)
                    nc.scalar.activation(c_probs_t[:, h % 2, 0:b + 1, P * b:P * b + P],
                                         bank[4 + j % 2][:, 0:P * (b + 1)].rearrange("p (b n) -> p b n", n=P),
                                         ACT.Copy).then_inc(c_flip_out, 1)
                if k >= C_OUT_LAG and (k - C_OUT_LAG) % TB == TB - 1:
                    c_out((k - C_OUT_LAG) // TB)
            for m in range(KT):
                act_cut(C_OUT + m + 3)
                act.wait_ge(out_turned, m + 1)
                if m >= 2:
                    act.wait_ge(out_done[m % 2], 16 * (m // 2))
                nc.scalar.activation(out_tok[:, m % 2, :, :], bank[4 + m % 2][:, :].rearrange("p (b n) -> p b n", b=TB),
                                     ACT.Copy).then_inc(out_copied, 1)

        @block.sync
        def _(sp):
            for m in range(KT):
                sp.wait_ge(out_copied, m + 1)
                sp.dma_start(out[:, P * m:P * m + P].rearrange("(b p) n -> p b n", p=P),
                             out_tok[:, m % 2, :, :]).then_inc(out_done[m % 2], 16)
            for j in range(2):
                sp.wait_ge(out_done[j], 16 * (KT // 2))

        @block.vector
        def _(dve):
            def rope(dst, src, turned):
                nc.vector.tensor_tensor(dst, src, rot[:, 0, :], ALU.mult)
                nc.vector.tensor_tensor(turned, turned, rot[:, 1, :], ALU.mult)
                dve.drain()
                return nc.vector.tensor_tensor(dst, dst, turned, ALU.add)

            def finish(e):
                kind, t = C_LATENT[e]
                dve.wait_ge(c_act, e + 1)
                if kind == "cq":
                    nc.vector.scalar_tensor_tensor(out=cq_lo[:, t, :], in0=tmp[:, e % 2, :], scalar=col("q_norm", t),
                                                   in1=cq_hi[:, t, :].bitcast(F32), op0=ALU.mult,
                                                   op1=ALU.subtract).then_inc(lat_ready, 1)
                if kind in ("cq", "ckv") and t:
                    total = q_rstd if kind == "cq" else kv_rstd
                    dve.drain()
                    ins = nc.vector.tensor_tensor(total[:, :], total[:, :], tmp[:, 2 + e % 2, :], ALU.add)
                    if t == (QT if kind == "cq" else KVT) - 1:
                        ins.then_inc(qsum_ready if kind == "cq" else kvsum_ready, 1)
                if kind == "kpe":
                    rope(kpe, kpe, tmp[:, 2 + e % 2, :]).then_inc(kpe_ready, 1)

            def q_finish(e):
                kind, t = Q_EVENTS[e]
                dve.wait_ge(q_act, e + 1)
                dve.drain()
                if kind == "nope":
                    nc.vector.tensor_scalar(qn[:, t, :], qn[:, t, :], col("qn_nope"), None, ALU.mult).then_inc(q_ready, 1)
                else:
                    rope(qr[:, t, :], qr[:, t, :], tmp[:, e % 2, :]).then_inc(q_ready, 1)

            def k_finish(h):
                dve.wait_ge(k_root, h + 1)
                r = tmp[:, 2 + h % 2, :]
                nc.vector.reciprocal(r, r)
                dve.drain()
                at = slice(QK_ROPE * (h % 2), QK_ROPE * (h % 2) + QK_ROPE)
                nc.vector.tensor_tensor(kr[at, h // 2, :], kpe[at, :], r[at, :], ALU.mult)
                nc.vector.scalar_tensor_tensor(out=kn[:, h, :], in0=kn[:, h, :], scalar=col("kn_nope"), in1=r,
                                               op0=ALU.mult, op1=ALU.mult).then_inc(k_ready, 1)

            for i, (kind, t) in enumerate(C_EVENTS):
                dve_cut(C_START + i + 3)
                dve.wait_ge(unit_used, C_START + i + 1)
                dve.drain()
                if (kind, t) in C_LATENT:
                    dst = ckv[:, t, :] if kind == "ckv" else tmp[:, i % 2, :]
                    ins = nc.vector.tensor_tensor(dst, bank[i % 4][:, :], rstd[:, :], ALU.mult)
                    if kind == "kpe":
                        dve.drain()
                        ins = nc.vector.tensor_scalar(kpe, tmp[:, i % 2, :], col("kn_rope"), None, ALU.mult)
                    ins.then_inc(c_evac, 1)
                    if i:
                        finish(i - 1)
                if kind == "z":
                    nc.vector.tensor_tensor(zs[:, t, :], bank[4 + t % 2][:, :], rstd[:, :], ALU.mult).then_inc(z_evac, 1)
                if (kind, t) == ("z", 0):
                    finish(len(C_LATENT) - 1)
                if (kind, t) == ("z", 1):
                    for j, dst in ((1, kv_rstd), (0, q_rstd)):
                        dve.wait_ge(lat_root, j + 1)
                        nc.vector.reciprocal(dst[:, :], dst[:, :])
                    dve.drain()
                    for j in range(KVT):
                        nc.vector.scalar_tensor_tensor(out=ckv[:, j, :], in0=ckv[:, j, :], scalar=col("kv_norm", j),
                                                       in1=kv_rstd[:, :], op0=ALU.mult, op1=ALU.mult).then_inc(ckv_norm, 1)
                if (kind, t) == ("z", 2):
                    for j in range(KVT):
                        dve.wait_ge(ckv_half, j + 1)
                        nc.vector.tensor_tensor(ckv_lo[:, j, :], ckv[:, j, :], ckv_hi[:, j, :].bitcast(F32),
                                                ALU.subtract).then_inc(ckv_ready, 1)
                if kind in ("q", "r"):
                    for e in q_events(kind, t):
                        dst = qn[:, Q_EVENTS[e][1], :] if kind == "q" else tmp[:, e % 2, :]
                        dve.drain()
                        ins = nc.vector.tensor_tensor(dst, bank[e % 4][:, :], q_rstd[:, :], ALU.mult)
                        if kind == "r":
                            dve.drain()
                            ins = nc.vector.tensor_scalar(qr[:, Q_EVENTS[e][1], :], dst, col("qn_rope"), None, ALU.mult)
                        ins.then_inc(q_evac, 1)
                        if e:
                            q_finish(e - 1)
                if (kind, t) == ("kv", 0):
                    q_finish(len(Q_EVENTS) - 1)
                    dve.wait_ge(q_summed, len(Q_EVENTS))
                    nc.vector.tensor_copy(q_scale[:, :], bank[7][:, 0:32])
                    dve.drain()
                    nc.vector.tensor_tensor(q_scale[:, :], q_scale[:, :], bank[7][:, 32:64], ALU.add).then_inc(q_total, 1)
                if (kind, t) == ("kv", 1):
                    dve.wait_ge(q_root, 1)
                    nc.vector.reciprocal(q_scale[:, :], q_scale[:, :])
                    dve.drain()
                    nc.vector.tensor_scalar(q_scale[:, :], q_scale[:, :], QK_HEAD ** -0.5, None, ALU.mult)
                if kind == "kv" and t:
                    k_finish(2 * t - 2)
                    k_finish(2 * t - 1)
            dve.drain()
            for k in range(len(C_STEPS) + C_OUT_LAG):
                if k < len(C_STEPS):
                    h, b = C_STEPS[k]
                    width = P * (b + 1)
                    if k in (TB, 2 * TB):
                        k_finish(C_HEADS - 3 + k // TB)
                    dve.wait_ge(c_scored, k + 1)
                    nc.vector.tensor_reduce(softstat[:, k, 0:1], bank[k % 4][:, 0:width], AX_X, ALU.max, negate=True)
                    dve.drain()
                    nc.vector.tensor_tensor(softstat[:, k, 0:1], softstat[:, k, 0:1], q_scale[:, 8 * b + h:8 * b + h + 1],
                                            ALU.mult).then_inc(c_maxed, 1)
                if 1 <= k <= len(C_STEPS):
                    width = P * (C_STEPS[k - 1][1] + 1)
                    p = c_probs[:, (k - 1) % 4, 0:width]
                    dve.wait_ge(c_exped, k)
                    nc.vector.reciprocal(softstat[:, k - 1, 2:3], softstat[:, k - 1, 1:2])
                    dve.drain()
                    nc.vector.tensor_scalar(p, p, softstat[:, k - 1, 2:3], None, ALU.mult).then_inc(c_weighed, 1)
                if k >= C_OUT_LAG and (k - C_OUT_LAG) % TB == TB - 1:
                    c_head((k - C_OUT_LAG) // TB)
            for m in range(KT):
                dve_cut(C_OUT + m + 3)
                dve.wait_ge(unit_used, C_OUT + m + 1)
                nc.vector.tensor_tensor(x[:, m, :], bank[m % 4][:, :], x[:, m, :], ALU.add).then_inc(x_ready, 1)

        @block.tensor
        def _(pe):
            three = pe_three
            def q_sums(e):
                kind, t = Q_EVENTS[e]
                pe.wait_ge(q_act, e + 1)
                at, sums_of = (t, ones[:, 0:1]) if kind == "nope" else (32 + 2 * t, table("halves", 2))
                for b in range(TB):
                    ins = nc.tensor.matmul(bank[7][:, at + 8 * b:at + 8 * b + sums_of.shape[1]],
                                           tmp[:, 2 + e % 2, P * b:P * b + P], sums_of, start=True, stop=True)
                ins.then_inc(q_summed, 1)

            def queries(kind, u, n):
                s = n % SLOTS
                pe.wait_ge(lo_ready, n + 1)
                for i, e in enumerate(q_events(kind, u)):
                    if e == 0:
                        pe.wait_ge(lat_ready, QT)
                        pe.wait_ge(c_evac, len(C_LATENT))
                    if e >= 4:
                        pe.wait_ge(q_evac, e - 3)
                    for kt in range(QT):
                        at = P * (QT * i + kt)
                        ins = pe_three(bank[e % 4][:, :], w_hi[:, s, at:at + P], w_lo[:, s, at:at + P], cq_hi[:, kt, :],
                                       cq_lo[:, kt, :], kt == 0, kt == QT - 1)
                    if i:
                        ins.then_inc(unit_used, 1)
                for e in q_events(kind, u):
                    if e >= 2:
                        q_sums(e - 2)

            def keys_values(u, n):
                s = n % SLOTS
                pe.wait_ge(lo_ready, n + 1)
                if u == 0:
                    pe.wait_ge(ckv_ready, KVT)
                    pe.wait_ge(q_evac, len(Q_EVENTS))
                elif u == 1:
                    pe.wait_ge(z_evac, KT)
                else:
                    pe.wait_ge(k_evac, 2 * u - 2)
                for j in range(2):
                    for kt in range(KVT):
                        at = P * (KVT * j + kt)
                        pe_three(bank[4 * (u % 2) + j][:, :], w_hi[:, s, at:at + P], w_lo[:, s, at:at + P], ckv_hi[:, kt, :],
                                 ckv_lo[:, kt, :], kt == 0, kt == KVT - 1)
                if u:
                    pe.wait_ge(k_evac_v, 2 * u)
                for b in range(TB):
                    for kt in range(KVT):
                        at = 4 * P + 2 * P * kt
                        ins = pe_three(bank[2 + b // 2][:, 2 * P * (b % 2):2 * P * (b % 2) + 2 * P],
                                       ckv_hi[:, kt, P * b:P * b + P], ckv_lo[:, kt, P * b:P * b + P],
                                       w_hi[:, s, at:at + 2 * P], w_lo[:, s, at:at + 2 * P], kt == 0, kt == KVT - 1)
                ins.then_inc(unit_used, 1)

            def key_sums(h):
                pe.wait_ge(k_act, h + 1)
                if h == 0:
                    pe.wait_ge(kpe_ready, 1)
                elif h == 1:
                    pe.wait_ge(q_total, 1)
                else:
                    pe.wait_ge(k_root, h - 1)
                nc.tensor.matmul(bank[6 + h % 2][:, :], ones, tmp[:, h % 2, :], start=True, stop=False)
                nc.tensor.matmul(bank[6 + h % 2][:, :], ones[0:64, :], kpe_sq[0:64, :], start=False,
                                 stop=True).then_inc(k_summed, 1)

            for i, (kind, t) in enumerate(C_EVENTS):
                n = C_START + i
                if (kind, t) in C_LATENT:
                    if i >= 4:
                        pe.wait_ge(c_evac, i - 3)
                    pe_unit(n, None, bank[i % 4][:, :], h_hi, h_lo, pe_h_arrive(NORMS - 1) if i == 0 else None)
                    if i == 0:
                        pe_sum_squares(NORMS - 1)
                if kind == "z":
                    if t >= 2:
                        pe.wait_ge(z_evac, t - 1)
                    pe_unit(n, None, bank[4 + t % 2][:, :], h_hi, h_lo)
                if (kind, t) == ("z", 0):
                    for j, total, ready in ((0, q_rstd, qsum_ready), (1, kv_rstd, kvsum_ready)):
                        pe.wait_ge(ready, 1)
                        nc.tensor.matmul(bank[6 + j][:, :], ones, total[:, :], start=True, stop=True).then_inc(lat_ss, 1)
                if kind in ("q", "r"):
                    queries(kind, t, n)
                if kind == "kv":
                    keys_values(t, n)
                if (kind, t) == ("kv", 0):
                    q_sums(len(Q_EVENTS) - 2)
                    q_sums(len(Q_EVENTS) - 1)
                if kind == "kv" and t:
                    key_sums(2 * t - 2)
                    key_sums(2 * t - 1)
            key_sums(C_HEADS - 2)
            key_sums(C_HEADS - 1)
            nstep = len(C_STEPS)
            for k in range(nstep + C_MIX_LAG):
                if k < nstep:
                    h, b = C_STEPS[k]
                    width = P * (b + 1)
                    dst = bank[k % 4]
                    if k == 0:
                        pe.wait_ge(q_ready, len(Q_EVENTS))
                        pe.wait_ge(k_evac, C_HEADS)
                    pe.wait_ge(k_ready, h + 1)
                    if k >= 4:
                        pe.wait_ge(c_exped, k - 3)
                    rows, t = slice(64 * (h % 2), 64 * (h % 2) + 64), h // 2
                    nc.tensor.matmul(dst[:, 0:width], qn[:, h, P * b:P * b + P], kn[:, h, 0:width], start=True, stop=False)
                    nc.tensor.matmul(dst[:, 0:width], qr[rows, t, P * b:P * b + P], kr[rows, t, 0:width], start=False,
                                     stop=False)
                    nc.tensor.matmul(dst[:, P * b:width], table_b("identity"), table_b("chunked"), start=False,
                                     stop=True).then_inc(c_scored, 1)
                j = k - C_FLIP_LAG
                if 0 <= j < nstep:
                    pe.wait_ge(c_weighed, j + 1)
                    if j >= 2:
                        pe.wait_ge(c_flip_out, j - 1)
                    for kb in range(C_STEPS[j][1] + 1):
                        ins = nc.tensor.transpose(bank[4 + j % 2][:, P * kb:P * kb + P], c_probs[:, j % 4, P * kb:P * kb + P],
                                                  identity)
                    ins.then_inc(c_flipped, 1)
                if k >= C_MIX_LAG and (k - C_MIX_LAG) % TB == TB - 1:
                    h = (k - C_MIX_LAG) // TB
                    pe.wait_ge(c_flip_out, k - C_MIX_LAG + 1)
                    if h >= 2:
                        pe.wait_ge(co_ready, h - 1)
                    elif h == 0:
                        pe.wait_ge(k_root, C_HEADS)
                    for kb in range(TB):
                        ins = nc.tensor.matmul(bank[6 + h % 2][:, P * kb:S], cv[:, kb, P * h:P * h + P],
                                               c_probs_t[:, h % 2, kb, P * kb:S], start=kb == 0, stop=kb == TB - 1)
                    ins.then_inc(c_mixed, 1)

            def turn_out(m):
                pe.wait_ge(x_ready, 8 * 9 + m + 1)
                if m >= 2:
                    pe.wait_ge(out_copied, m - 1)
                for b in range(TB):
                    ins = nc.tensor.transpose(bank[4 + m % 2][:, P * b:P * b + P], x[:, m, P * b:P * b + P], identity)
                ins.then_inc(out_turned, 1)

            for m in range(KT):
                s = (C_OUT + m) % SLOTS
                pe.wait_ge(lo_ready, C_OUT + m + 1)
                if m >= 4:
                    pe.wait_ge(x_ready, 8 * 9 + m - 3)
                for kt in range(C_HEADS):
                    if m == 0:
                        pe.wait_ge(co_ready, kt + 1)
                    ins = three(bank[m % 4][:, :], w_hi[:, s, P * kt:P * kt + P], w_lo[:, s, P * kt:P * kt + P],
                                co_hi[:, kt, :], co_lo[:, kt, :], kt == 0, kt == C_HEADS - 1)
                ins.then_inc(unit_used, 1)
                if m:
                    turn_out(m - 1)
            turn_out(KT - 1)



def _by_column(np, w, start, width=P, pad=P):
    k = w.shape[0] // P
    u = np.zeros((P, k, pad), np.float32)
    u[:, :, :width] = w[:, start:start + width].reshape(k, P, width).transpose(1, 0, 2)
    return u


def _unit(np, *parts):
    u = np.concatenate([p.reshape(P, -1) for p in parts], axis=1)
    if u.shape[1] < UNIT:
        u = np.concatenate([u, np.zeros((P, UNIT - u.shape[1]), np.float32)], axis=1)
    return u


def _second(np, a, add):
    w = a["a_w_in_2"][0]
    cuts = {"xm": 0, "om": 1024, "zm": 2056, "xp": 3080, "zp": 4104}
    gates = np.zeros((D, P), np.float32)
    gates[:, :M_HEADS] = w[:, 2048:2048 + M_HEADS]
    gates[:, 32:32 + M_HEADS] = w[:, 2048 + M_HEADS:2056]

    for kind, t in A_EVENTS:
        if kind == "gates":
            add(_by_column(np, gates, 0))
        elif kind == "qk":
            add(*(_by_column(np, a[f"a_w_{k}_2"][0, t], 0, M_DIM, M_DIM) for k in "qk"))
        elif kind == "v":
            add(_by_column(np, a["a_w_v_2"][0, t], 0, M_DIM, M_DIM))
        elif kind == "pool":
            add(_by_column(np, a["a_pool_w_2"][0, t], 0, M_DIM, M_DIM))
        else:
            add(_by_column(np, w, cuts[kind] + P * t))
    for m in range(KT):
        for j in range(2):
            add(_by_column(np, a["a_w_out_2"][0, D * j:D * j + D], P * m))

    w, uq, ukv = a["c_w_in_2"][0], a["c_w_uq_2"][0], a["c_w_ukv_2"][0]
    cuts = {"cq": 0, "ckv": Q_LORA, "z": Q_LORA + KV_LORA + QK_ROPE}
    pe = w[:, Q_LORA + KV_LORA:Q_LORA + KV_LORA + QK_ROPE]
    for kind, t in C_EVENTS:
        two = (2 * t, 2 * t + 1)
        if kind == "kpe":
            add(_by_column(np, np.concatenate([pe, pe], axis=1), 0))
        elif kind == "q":
            add(*(_by_column(np, uq, QK_HEAD * h) for h in two))
        elif kind == "r":
            add(*(np.concatenate([_by_column(np, uq, QK_HEAD * h + QK_NOPE, QK_ROPE, QK_ROPE) for h in (2 * j, 2 * j + 1)],
                                 axis=2) for j in two))
        elif kind == "kv":
            add(*(_by_column(np, ukv, 2 * P * h) for h in two),
                np.concatenate([_by_column(np, ukv, 2 * P * h + P) for h in two], axis=2))
        else:
            add(_by_column(np, w, cuts[kind] + P * t))
    for m in range(KT):
        add(_by_column(np, a["c_w_out_2"][0], P * m))


def _stream(np, a):
    s = np.zeros((UNITS, P, UNIT), np.float32)
    at = 0

    def add(*parts):
        nonlocal at
        s[at] = _unit(np, *parts)
        at += 1

    def ffn(up, down):
        for j in range(FT):
            add(_by_column(np, up, P * j))
            add(_by_column(np, up, D_FF + P * j))
        for j in range(FT):
            add(down[P * j:P * j + P])

    for l in range(DEPTH):
        ffn(a["ffn1_w_gate_up"][l], a["ffn1_w_down"][l])
        w = a["w_in"][l]
        for start in (1544, 2056, 0, 512):
            for t in range(4):
                add(_by_column(np, w, start + P * t))
        add(_by_column(np, w, 1536, FOX_HEADS))
        for start in (1024, 2568):
            for t in range(4):
                add(_by_column(np, w, start + P * t))
        for m in range(KT):
            add(_by_column(np, a["w_out"][l], P * m))
        ffn(a["ffn2_w_gate_up"][l], a["ffn2_w_down"][l])
    assert at == A_START
    _second(np, a, add)
    return s


def _pack_cols(np, a):
    c = np.zeros((P, NCOLS), np.float32)

    def put(name, v, row=0):
        v = np.asarray(v)
        if v.size >= P:
            n = v.size // P
            c[:, COLS[name]:COLS[name] + n] = v.reshape(n, P).T
        else:
            c[row:row + v.size, COLS[name]] = v

    for l in range(DEPTH):
        for k in ("ffn1_norm", "mix_norm", "ffn2_norm"):
            put(f"{k}{l}", a[k][l])
        put(f"subln{l}", a["diff_subln"][l])
        put(f"forget_bias{l}", a["forget_bias"][l])
        for k in ("q1", "k1", "q2", "k2"):
            put(f"l{k}_{l}", a[f"lambda_{k}"][l])
    put("final_norm", a["final_norm"])
    put("a_norm", a["a_norm_g_2"][0])
    put("conv_w", a["a_conv_w_2"][0])
    put("conv_b", a["a_conv_b_2"][0])
    put("head_norm", a["a_head_norm_g_2"][0])
    put("skip", a["a_skip_2"][0])
    put("pool_scale", a["a_pool_scale_2"][0])
    put("b_if", a["a_b_if_2"][0][:M_HEADS])
    put("b_if", a["a_b_if_2"][0][M_HEADS:], row=32)
    put("c_norm", a["c_norm_g_2"][0])
    put("q_norm", a["c_q_norm_g_2"][0])
    put("kv_norm", a["c_kv_norm_g_2"][0])
    for k in ("qn", "kn"):
        g = a[f"c_{k}_g_2"][0]
        put(f"{k}_nope", g[:QK_NOPE])
        put(f"{k}_rope", np.concatenate([g[QK_NOPE:], g[QK_NOPE:]]))
    f = np.float32(ROPE_THETA) ** (-np.arange(0, QK_ROPE, 2, dtype=np.float32) / np.float32(QK_ROPE))
    put("inv_freq", np.tile(f.astype(np.float32), 4))
    put("rope_sign", np.tile(np.repeat(np.float32([-1.0, 1.0]), 32), 2))
    return c


def _tables(np):
    t = np.zeros((P, NTAB + NTABB), np.float32)
    i = np.arange(P)
    t[:, 0:P] = np.eye(P)
    t[:, P:2 * P] = 1.0
    for c in range(2):
        t[64 * c:64 * c + 64, TAB["halves"] + c] = 1.0
    t[:, TAB["causal_t"]:][:, :P] = np.where(i[None, :] >= i[:, None], 0.0, -BIG)
    for h in range(M_HEADS):
        t[h, TAB["select"] + P * h:TAB["select"] + P * h + P] = 1.0
    for g, w in enumerate(P_WINDOWS):
        t[:, TAB["pool_head"] + 16 * g:TAB["pool_head"] + 16 * g + 16] = 1.0 / np.minimum(np.arange(16) + 1, w)
    b = t[:, NTAB:]
    b[:, 0:P] = np.eye(P)
    b[:, TABB["causal"]:][:, :P] = np.where(i[None, :] <= i[:, None], 0.0, -BIG)
    b[:, TABB["chunked"]:][:, :P] = np.where(i[None, :] // 64 <= i[:, None] // 64, 0.0, -BIG)
    for h in range(FOX_HEADS):
        for row in CUM_ROWS:
            b[row + h, TABB["select"] + P * h:TABB["select"] + P * h + P] = 1.0
    return t


def _rope(np):
    inv = 1.0 / (ROPE_THETA ** (np.arange(0, HEAD, 2, dtype=np.float32) / HEAD))
    ang = np.arange(S, dtype=np.float32)[None, :] * np.tile(inv.astype(np.float32), 4)[:, None]
    sign = np.tile(np.repeat(np.float32([-1.0, 1.0]), 32), 2)[:, None]
    return np.stack([np.cos(ang), np.sin(ang) * sign], axis=1).astype(np.float32)


def kernel(**inputs):
    import numpy as np
    import concourse.bacc as bacc
    from concourse.bass_utils import run_bass_kernel_spmd as run

    a = {k: np.asarray(v) for k, v in inputs.items()}
    arrays = {
        "x": np.ascontiguousarray(a["x"][0]), "stream": _stream(np, a), "cols": _pack_cols(np, a),
        "tables": _tables(np), "rope": _rope(np), "positions": np.ascontiguousarray(a["positions_2"]),
    }
    nc = bacc.Bacc("TRN2", target_bir_lowering=False, num_devices=1)
    args = [nc.dram_tensor(n, v.shape, mybir.dt.from_np(v.dtype), kind="ExternalInput").ap()
            for n, v in arrays.items()]
    out = nc.dram_tensor("out", (S, D), F32, kind="ExternalOutput").ap()
    build(nc, *args, out)
    r = run(nc, [arrays], core_ids=[0])
    return r.results[0]["out"].reshape(1, S, D)
```
